# Optimizing a Trainium2 kernel written in Bass

```python
import math
import jax, jax.numpy as jnp
from jax import lax
import numpy as np

D_MODEL = 2048
BATCH = 1
SEQ = 512
DEPTH = 1
DEC_BATCH = 8
DEC_SEQ = 1
PAST_LEN = 2048
PAGE_SIZE = 128

HEAD_DIM = 64
HEADS_PER_GROUP = 4
ATTN_GROUPS = ((128, 1), (512, 4), (2048, 16))
N_ATTN_GROUPS = len(ATTN_GROUPS)
N_HEADS = N_ATTN_GROUPS * HEADS_PER_GROUP
ATTN_WIDTH = N_HEADS * HEAD_DIM
ATTN_OUT = HEADS_PER_GROUP * HEAD_DIM
N_DIL_KEYS = 128
N_BUCKETS = 32
MAX_DISTANCE = 2048
ATTN_SCALE = HEAD_DIM ** -0.5
POOL_WINDOWS = (2, 4, 8, 16)
POOL_GROUP = D_MODEL // 16
POOL_WIDTH = len(POOL_WINDOWS) * POOL_GROUP
POOL_STATE = max(POOL_WINDOWS) - 1
CONV_CH = D_MODEL // 4
CONV_K = 3
D_FF = 5632
FFN_CONV_K = 3
N_BRANCH = 3
N_IN = 3 * ATTN_WIDTH + POOL_WIDTH + 3 * CONV_CH + N_BRANCH * D_MODEL
SPLITS = (ATTN_WIDTH, 2 * ATTN_WIDTH, 3 * ATTN_WIDTH,
          3 * ATTN_WIDTH + POOL_WIDTH,
          3 * ATTN_WIDTH + POOL_WIDTH + CONV_CH,
          3 * ATTN_WIDTH + POOL_WIDTH + 2 * CONV_CH,
          3 * ATTN_WIDTH + POOL_WIDTH + 3 * CONV_CH)
N_MOD = 6
EPS = 1e-6
NEG_INF = -1e30

kernel_name = 'gated_hybrid_pool_conv_dilated_attn_step'

def rms_norm(x, g):
    xf = x.astype(jnp.float32)
    y = xf * lax.rsqrt(jnp.mean(xf * xf, axis=-1, keepdims=True) + EPS)
    return (y * g.astype(jnp.float32)).astype(x.dtype)

def causal_dwconv(u_ext, w):
    k = w.shape[0]
    n = u_ext.shape[1] - (k - 1)
    return sum(u_ext[:, i:i + n] * w[i] for i in range(k))

def group_rel_bias(rel_bias):
    n = np.arange(N_DIL_KEYS + 1)
    max_exact = N_BUCKETS // 2
    out = []
    for g, (_, d) in enumerate(ATTN_GROUPS):
        dist = n * d
        large = max_exact + (np.log(np.maximum(dist, 1) / max_exact) / math.log(MAX_DISTANCE / max_exact)
                             * (N_BUCKETS - max_exact)).astype(np.int32)
        bucket = np.where(dist < max_exact, dist, np.minimum(large, N_BUCKETS - 1))
        out.append(rel_bias[bucket, g * HEADS_PER_GROUP:(g + 1) * HEADS_PER_GROUP].T)
    return jnp.stack(out)

def dilated_band_attention(q, k, v, bias, dilation):
    b, s, h, dh = q.shape
    n = N_DIL_KEYS
    L = s // dilation
    nb = -(-L // n)
    lp = nb * n

    def split(t):
        t = t.reshape(b, L, dilation, h, dh).transpose(0, 2, 1, 3, 4)
        return jnp.pad(t, ((0, 0), (0, 0), (0, lp - L), (0, 0), (0, 0)))

    def kblocks(t):
        t = jnp.pad(split(t), ((0, 0), (0, 0), (n, 0), (0, 0), (0, 0))).reshape(b, dilation, nb + 1, n, h, dh)
        return jnp.concatenate([t[:, :, :-1], t[:, :, 1:]], axis=3)

    qs = split(q).reshape(b, dilation, nb, n, h, dh)
    kb, vb = kblocks(k), kblocks(v)
    a_idx = np.arange(n)[:, None]
    c_idx = np.arange(2 * n)[None, :]
    dist = a_idx + n - c_idx
    band = (dist >= 0) & (dist <= n)
    key_idx = np.arange(nb)[:, None] * n - n + np.arange(2 * n)[None, :]
    valid = band[None] & (key_idx >= 0)[:, None, :]
    bias_qk = bias[:, np.clip(dist, 0, n)].astype(jnp.float32)
    s_ = jnp.einsum('brnqhd,brnkhd->brnhqk', qs, kb, preferred_element_type=jnp.float32) * ATTN_SCALE
    s_ = jnp.where(valid[None, None, :, None], s_ + bias_qk, NEG_INF)
    m = jnp.max(s_, axis=-1, keepdims=True)
    p = jnp.exp(s_ - m)
    l = jnp.sum(p, axis=-1, keepdims=True)
    o = jnp.einsum('brnhqk,brnkhd->brnqhd', (p / l).astype(v.dtype), vb)
    lse = (m + jnp.log(l))[..., 0]
    o = o.reshape(b, dilation, lp, h, dh)[:, :, :L].transpose(0, 2, 1, 3, 4).reshape(b, s, h, dh)
    lse = lse.transpose(0, 1, 2, 4, 3).reshape(b, dilation, lp, h)[:, :, :L].transpose(0, 2, 1, 3).reshape(b, s, h)
    return o, lse

def dilated_cache_attention(q, k_ext, v_ext, bias, dilation, n_past):
    t = q.shape[1]
    idx = n_past + np.arange(t)[:, None] - dilation * np.arange(N_DIL_KEYS + 1)[None, :]
    valid = idx >= 0
    idx = np.maximum(idx, 0)
    kg, vg = k_ext[:, idx], v_ext[:, idx]
    s_ = jnp.einsum('bthd,btnhd->bhtn', q, kg, preferred_element_type=jnp.float32) * ATTN_SCALE
    s_ = jnp.where(valid[None, None], s_ + bias[:, None, :].astype(jnp.float32), NEG_INF)
    m = jnp.max(s_, axis=-1, keepdims=True)
    p = jnp.exp(s_ - m)
    l = jnp.sum(p, axis=-1, keepdims=True)
    o = jnp.einsum('bhtn,btnhd->bthd', (p / l).astype(v_ext.dtype), vg)
    lse = (m + jnp.log(l))[..., 0].transpose(0, 2, 1)
    return o, lse

def combine_groups(outs, lses):
    o = jnp.stack(outs, axis=2)
    wgt = jax.nn.softmax(jnp.stack(lses, axis=2), axis=2)
    return jnp.einsum('btgh,btghd->bthd', wgt.astype(o.dtype), o)

def pool_prompt(p):
    _, s, _ = p.shape
    cs = jnp.pad(jnp.cumsum(p.astype(jnp.float32), axis=1), ((0, 0), (1, 0), (0, 0)))
    t = np.arange(s)
    means = []
    for gi, w in enumerate(POOL_WINDOWS):
        lo = np.maximum(t + 1 - w, 0)
        cg = cs[..., gi * POOL_GROUP:(gi + 1) * POOL_GROUP]
        cnt = (t + 1 - lo).astype(np.float32)
        means.append((cg[:, t + 1] - cg[:, lo]) / cnt[None, :, None])
    return jnp.concatenate(means, axis=-1) - p.astype(jnp.float32)

def pool_step(state, p):
    ext = jnp.concatenate([state, p], axis=1)
    cs = jnp.pad(jnp.cumsum(ext.astype(jnp.float32), axis=1), ((0, 0), (1, 0), (0, 0)))
    m = POOL_STATE + np.arange(p.shape[1])
    means = []
    for gi, w in enumerate(POOL_WINDOWS):
        cg = cs[..., gi * POOL_GROUP:(gi + 1) * POOL_GROUP]
        means.append((cg[:, m + 1] - cg[:, m + 1 - w]) / w)
    return jnp.concatenate(means, axis=-1) - p.astype(jnp.float32), ext[:, -POOL_STATE:]

def run_layer(x, c, lw, bias_g, hist):
    (norm_g, w_ada, b_ada, w_in, w_attn_br, w_pool_grp, pool_scale, w_pool_br,
     conv_w, w_conv_br, w_o, w_up, ffn_conv_w, w_down) = lw
    nb, t, _ = x.shape
    mod = (jax.nn.silu(c) @ w_ada + b_ada).reshape(nb, N_MOD, 1, D_MODEL)
    h = rms_norm(x, norm_g[0]) * (1 + mod[:, 1]) + mod[:, 0]
    q, k, v, p, gb, gc, hc, gl = jnp.split(h @ w_in, SPLITS, axis=-1)
    hs = (nb, t, N_ATTN_GROUPS, HEADS_PER_GROUP, HEAD_DIM)
    q, k, v = q.reshape(hs), k.reshape(hs), v.reshape(hs)
    u = gc * hc
    outs, lses = [], []
    if hist is None:
        for g, (_, d) in enumerate(ATTN_GROUPS):
            o, lse = dilated_band_attention(q[:, :, g], k[:, :, g], v[:, :, g], bias_g[g], d)
            outs.append(o)
            lses.append(lse)
        new_kv = [jnp.stack([k[:, -min(w, t):, g], v[:, -min(w, t):, g]], axis=2)
                  for g, (w, _) in enumerate(ATTN_GROUPS)]
        pm = pool_prompt(p)
        new_pool = p[:, -POOL_STATE:]
        u_ext = jnp.pad(u, ((0, 0), (CONV_K - 1, 0), (0, 0)))
    else:
        kv_caches, pool_state, conv_state, ffn_state = hist
        for g, (_, d) in enumerate(ATTN_GROUPS):
            cache = kv_caches[g]
            k_ext = jnp.concatenate([cache[:, :, 0], k[:, :, g]], axis=1)
            v_ext = jnp.concatenate([cache[:, :, 1], v[:, :, g]], axis=1)
            o, lse = dilated_cache_attention(q[:, :, g], k_ext, v_ext, bias_g[g], d, cache.shape[1])
            outs.append(o)
            lses.append(lse)
        new_kv = [jnp.stack([k[:, :, g], v[:, :, g]], axis=2) for g in range(N_ATTN_GROUPS)]
        pm, new_pool = pool_step(pool_state, p)
        u_ext = jnp.concatenate([conv_state, u], axis=1)
    br_c = combine_groups(outs, lses).reshape(nb, t, ATTN_OUT) @ w_attn_br
    pg = pm.astype(x.dtype).reshape(nb, t, len(POOL_WINDOWS), POOL_GROUP)
    pz = jnp.einsum('btgc,gce->btge', pg, w_pool_grp).reshape(nb, t, POOL_WIDTH)
    br_a = (pz * pool_scale) @ w_pool_br
    br_b = (gb * causal_dwconv(u_ext, conv_w)) @ w_conv_br
    new_conv = u_ext[:, -(CONV_K - 1):]
    gates = jax.nn.sigmoid(gl.reshape(nb, t, N_BRANCH, D_MODEL))
    merged = gates[:, :, 0] * br_a + gates[:, :, 1] * br_b + gates[:, :, 2] * br_c
    x = x + mod[:, 2] * rms_norm(merged @ w_o, norm_g[1])
    h2 = rms_norm(x, norm_g[2]) * (1 + mod[:, 4]) + mod[:, 3]
    up = h2 @ w_up
    if hist is None:
        up_ext = jnp.pad(up, ((0, 0), (FFN_CONV_K - 1, 0), (0, 0)))
    else:
        up_ext = jnp.concatenate([hist[3], up], axis=1)
    uc = causal_dwconv(up_ext, ffn_conv_w)
    f = (jax.nn.gelu(uc[..., :D_FF], approximate=True) * uc[..., D_FF:]) @ w_down
    new_ffn = up_ext[:, -(FFN_CONV_K - 1):]
    x = x + mod[:, 5] * rms_norm(f, norm_g[3])
    return x, (new_kv[0], new_kv[1], new_kv[2], new_pool, new_conv, new_ffn)

def setup_inputs(seed: int = 0) -> dict:
    key = jax.random.key(seed)
    ks = jax.random.split(key, 24)
    f32 = jnp.float32
    nrm = lambda k, shape, scale: jax.random.normal(k, shape, f32) * scale
    lc = [min(w, PAST_LEN) for w, _ in ATTN_GROUPS]
    return {
        'x_prompt': nrm(ks[0], (BATCH, SEQ, D_MODEL), 1.0),
        'x_sample': nrm(ks[1], (DEC_BATCH, DEC_SEQ, D_MODEL), 1.0),
        'c_prompt': nrm(ks[2], (BATCH, D_MODEL), 1.0),
        'c_sample': nrm(ks[3], (DEC_BATCH, D_MODEL), 1.0),
        'cache_kv_w128': nrm(ks[4], (DEPTH, DEC_BATCH, lc[0], 2, HEADS_PER_GROUP, HEAD_DIM), 1.0),
        'cache_kv_w512': nrm(ks[5], (DEPTH, DEC_BATCH, lc[1], 2, HEADS_PER_GROUP, HEAD_DIM), 1.0),
        'cache_kv_w2048': nrm(ks[6], (DEPTH, DEC_BATCH, lc[2], 2, HEADS_PER_GROUP, HEAD_DIM), 1.0),
        'state_pool': nrm(ks[7], (DEPTH, DEC_BATCH, POOL_STATE, POOL_WIDTH), 1.0),
        'state_conv': nrm(ks[8], (DEPTH, DEC_BATCH, CONV_K - 1, CONV_CH), 1.0),
        'state_ffn_conv': nrm(ks[9], (DEPTH, DEC_BATCH, FFN_CONV_K - 1, 2 * D_FF), 1.0),
        'rel_bias': nrm(ks[10], (N_BUCKETS, N_HEADS), 0.5),
        'norm_g': 1.0 + nrm(ks[11], (DEPTH, 4, D_MODEL), 0.02),
        'w_ada': nrm(ks[12], (DEPTH, D_MODEL, N_MOD * D_MODEL), 0.5 * D_MODEL ** -0.5),
        'b_ada': nrm(ks[13], (DEPTH, N_MOD * D_MODEL), 0.01),
        'w_in': nrm(ks[14], (DEPTH, D_MODEL, N_IN), D_MODEL ** -0.5),
        'w_attn_br': nrm(ks[15], (DEPTH, ATTN_OUT, D_MODEL), ATTN_OUT ** -0.5),
        'w_pool_grp': nrm(ks[16], (DEPTH, len(POOL_WINDOWS), POOL_GROUP, POOL_GROUP), POOL_GROUP ** -0.5),
        'pool_scale': 1.0 + nrm(ks[17], (DEPTH, POOL_WIDTH), 0.1),
        'w_pool_br': nrm(ks[18], (DEPTH, POOL_WIDTH, D_MODEL), POOL_WIDTH ** -0.5),
        'conv_w': nrm(ks[19], (DEPTH, CONV_K, CONV_CH), CONV_K ** -0.5),
        'w_conv_br': nrm(ks[20], (DEPTH, CONV_CH, D_MODEL), CONV_CH ** -0.5),
        'w_o': nrm(ks[21], (DEPTH, D_MODEL, D_MODEL), D_MODEL ** -0.5),
        'w_up': nrm(ks[22], (DEPTH, D_MODEL, 2 * D_FF), D_MODEL ** -0.5),
        'ffn_conv_w': nrm(jax.random.fold_in(ks[23], 1), (DEPTH, FFN_CONV_K, 2 * D_FF), FFN_CONV_K ** -0.5),
        'w_down': nrm(jax.random.fold_in(ks[23], 2), (DEPTH, D_FF, D_MODEL), D_FF ** -0.5),
    }

def reference(x_prompt, x_sample, c_prompt, c_sample, cache_kv_w128, cache_kv_w512, cache_kv_w2048,
              state_pool, state_conv, state_ffn_conv, rel_bias, norm_g, w_ada, b_ada, w_in, w_attn_br,
              w_pool_grp, pool_scale, w_pool_br, conv_w, w_conv_br, w_o, w_up, ffn_conv_w, w_down):
    bias_g = group_rel_bias(rel_bias)
    yp, ys = x_prompt, x_sample
    st_p, st_s = [], []
    for l in range(DEPTH):
        lw = (norm_g[l], w_ada[l], b_ada[l], w_in[l], w_attn_br[l], w_pool_grp[l], pool_scale[l],
              w_pool_br[l], conv_w[l], w_conv_br[l], w_o[l], w_up[l], ffn_conv_w[l], w_down[l])
        yp, sp = run_layer(yp, c_prompt, lw, bias_g, None)
        hist = ((cache_kv_w128[l], cache_kv_w512[l], cache_kv_w2048[l]), state_pool[l], state_conv[l], state_ffn_conv[l])
        ys, ss = run_layer(ys, c_sample, lw, bias_g, hist)
        st_p.append(sp)
        st_s.append(ss)
    kv128_p, kv512_p, kv2048_p, pool_p, conv_p, ffn_p = [jnp.stack([s[i] for s in st_p]) for i in range(6)]
    kv128_s, kv512_s, kv2048_s, pool_s, conv_s, ffn_s = [jnp.stack([s[i] for s in st_s]) for i in range(6)]
    return (yp, ys, kv128_p, kv512_p, kv2048_p, pool_p, conv_p, ffn_p,
            kv128_s, kv512_s, kv2048_s, pool_s, conv_s, ffn_s)


_drawn_inputs = setup_inputs


def setup_inputs(seed=0):
    import zlib

    import numpy as np

    out = dict(_drawn_inputs(seed))
    spreads = {}
    factors = {'cache_kv_w128': 5.476,
     'cache_kv_w512': 5.076,
     'cache_kv_w2048': 5.146,
     'rel_bias': 3.578,
     'b_ada': 2.98,
     'pool_scale': 3.338}
    for name, (base, spread) in spreads.items():
        noise = np.random.default_rng([zlib.crc32(name.encode()), seed]).standard_normal(out[name].shape)
        drawn = base * np.exp(spread * noise) if base else spread * noise
        out[name] = __import__('jax').numpy.asarray(drawn.astype(out[name].dtype))
    for name, factor in factors.items():
        out[name] = (out[name] * factor).astype(out[name].dtype)
    return out
```

```python
import math
import numpy as np
import concourse.bass as bass
from concourse import mybir

F32 = mybir.dt.float32
F32R = mybir.dt.float32r
ALU = mybir.AluOpType
ACT = mybir.ActivationFunctionType
AX = mybir.AxisListType
P = 128

D = 2048
KD = D // P
TP, NS = 512, 8
T = TP + NS
HALF = T // 2
NB = TP // P
G, HG, DH = 3, 4, 64
DIL = (1, 4, 16)
NK = 128
AW = G * HG * DH
QCH = AW // P
PW, CC = 512, 512
WIN = (2, 4, 8, 16)
DFF = 5632
FCH = DFF // P
ROUNDS, FPR = FCH // 4, 4
SCALE = DH ** -0.5
EPS = 1e-6
NEG = -1e30
RW = 5 * P
BW = RW + NK + 1
COL_P, COL_B, COL_C, COL_H, COL_G = 3 * AW, 3 * AW + PW, 3 * AW + PW + CC, 3 * AW + PW + 2 * CC, 3 * AW + PW + 3 * CC
PR, SA = slice(0, TP), slice(TP, T)
RAW, SPL = 4, 2
UNIT = 8 * P

U_ADA, N_ADA = 0, 8
U_QKV = U_ADA + 8 * N_ADA
U_PC = U_QKV + 9 * 4
U_M = U_PC + 2 * 16
U_O = U_M + 16 * 16
U_F0 = U_O + 8 * 4
U_F = U_F0 + 16
U_END = U_F + 10 * 24
UNITS = U_END + 8
C_QKV, C_PC, C_M, C_O, C_F0, C_F = 0, 9, 17, 65, 73, 77


def constants():
    n = np.arange(NK + 1)
    onehot = np.zeros((33, G, BW), np.float32)
    for g, d in enumerate(DIL):
        dist = n * d
        large = 16 + (np.log(np.maximum(dist, 1) / 16) / math.log(2048 / 16) * 16).astype(np.int32)
        bucket = np.where(dist < 16, dist, np.minimum(large, 31))
        for y in range(RW):
            delta = TP - 1 - y
            if delta >= 0 and delta % d == 0 and delta // d <= NK:
                onehot[bucket[delta // d], g, y] = 1
            else:
                onehot[32, g, y] = NEG
        for i in range(NK + 1):
            onehot[bucket[NK - i if i < NK else 0], g, RW + i] = 1
    sel = np.zeros((19, 9), np.float32)
    for i in range(9):
        sel[i, i] = sel[9 + i, i] = 1
    sel[18] = 1
    heads = np.zeros((HG, HG * DH), np.float32)
    for h in range(HG):
        heads[h, h * DH:(h + 1) * DH] = 1
    counts = np.zeros((P, 4, 16), np.float32)
    for i, w in enumerate(WIN):
        counts[:, i] = (1.0 / np.minimum(np.arange(16) + 1, w)).astype(np.float32)
    return {"ident": np.eye(P, dtype=np.float32), "onehot": onehot, "sel": sel, "heads": heads, "counts": counts}


class Step:

    def __init__(self, eng, sem):
        self.eng, self.sem, self.base, self.it, self.per, self.k = eng, sem, 0, 0, 0, 0

    def enter(self, it, per):
        self.base, self.it, self.per, self.k = self.base + self.k, it, per, 0

    def leave(self, times):
        assert self.k == self.per, ("steps of the loop's body", self.k)
        self.base, self.it, self.per, self.k = self.base + self.per * times, 0, 0, 0

    def __call__(self, ins):
        ins.then_inc(self.sem, 1)
        self.k += 1

    def settle(self):
        self.eng.wait_ge(self.sem, self.it * self.per + (self.base + self.k))


class Unit:

    def __init__(self, base, per, it, l):
        self.n = it * per + (base + l)
        self.raw = (base + l) % RAW
        self.spl = (base + l) % SPL
        self.turn = it * (per // RAW) + (base + l) // RAW

    raw_free = property(lambda s: s.n + 1)
    arrived = property(lambda s: s.turn * 16 + 16)
    spl_free = property(lambda s: s.n + 1)
    hi_done = property(lambda s: s.n + 1)
    lo_done = property(lambda s: s.n + 5)
    used = property(lambda s: s.n + 3)


def layer(nc, a, out):
    at = {"top": -(-nc.sbuf_base // 32) * 32}

    def place(name, shape, dt=F32, off=None):
        size = int(np.prod(shape[1:])) * 4
        o = at["top"] if off is None else off
        if off is None:
            at["top"] += -(-size // 32) * 32
        return nc.alloc_sbuf_tensor_at(name, shape, dt, offset=o).ap()

    def region(start, *items):
        o, made = start, []
        for name, shape, dt in items:
            made.append(place(name, shape, dt, off=o))
            o += -(-int(np.prod(shape[1:])) * 4 // 32) * 32
        return made, o

    ident = place("ident", [P, P])
    ones = place("ones", [P, P])
    sel = place("sel", [19, 9])
    heads_mask = place("heads_mask", [HG, HG * DH])
    counts = place("counts", [P, 4, 16])
    eps = place("eps", [P, 1])
    cols = place("cols", [P, 80])
    ffn_w = place("ffn_w", [P, 3, 2 * FCH])
    st_conv = place("st_conv", [P, 4, NS, 2])
    st_pool = place("st_pool", [P, 4, NS, 15])
    mods = place("mods", [P, 6 * KD, 9])
    coef = place("coef", [P, KD, 9])
    cT = place("cT", [P, KD, 18], F32R)
    mod_rows = place("mod_rows", [19, 512])
    raw = place("raw", [P, RAW, UNIT])
    whi = place("whi", [P, SPL, UNIT], F32R)
    wlo = place("wlo", [P, SPL, UNIT], F32R)
    H0 = at["top"]
    hH = place("hH", [P, KD, T], F32R)
    hL = place("hL", [P, KD, T], F32R)
    L0 = at["top"]
    (xN, xs, cc, csig), e = region(H0, ("xN", [P, NB, D], F32), ("xs", [NS, D], F32), ("cc", [9, D], F32), ("csig", [9, D], F32))
    assert e <= L0
    (xT, xr, rb, rows1, rowsF, rowsC, rowsP, relb, onehot, brows, sqj, ssq, rs, diag), end0 = region(
        L0, ("xT", [P, KD, T], F32), ("xr", [P, KD, T], F32), ("rb", [P, T], F32),
        ("rows1", [80, P], F32), ("rowsF", [88, 3, P], F32), ("rowsC", [16, CC], F32), ("rowsP", [120, PW], F32),
        ("relb", [33, 12], F32), ("onehot_s", [33, G, BW], F32), ("brows", [HG, G, BW], F32),
        ("sqj", [P, D], F32), ("ssq", [P, 5], F32), ("rs", [P, 5], F32), ("diag", [P, 5, P], F32))
    (ns, vn, qk, stage, qB), e1 = region(
        L0, ("ns", [NS, 3 * AW], F32), ("vn", [P, G, NB, 256], F32),
        ("qk", [P, 2 * QCH, TP], F32), ("stage", [P, 2, T], F32), ("qB", [P, 2, AW], F32))
    (u_bias, sc_p, pT_t, q2, osb), e2 = region(
        e1, ("u_bias", [P, 2, 5 * 256], F32), ("scores", [P, 5 * 256], F32), ("probsT", [P, 10, P], F32),
        ("q2", [P, 2, G, P], F32), ("osb", [P, 2, DH], F32))
    (cS, sc_s, k_s, mx, nm, ls, rl, utail), e3 = region(
        e2, ("cS", [P, T], F32), ("sc_s", [P, NS, 12], F32), ("k_s", [P, 2, AW], F32),
        ("mx", [P, 2], F32), ("nm", [P, 2], F32), ("ls", [P, 2], F32), ("rl", [P, 2], F32), ("utail", [P, 4, 10], F32))
    (pT, bcv, aT), e = region(e3, ("pT", [P, 4, T], F32), ("bcv", [P, 4, T], F32), ("aT", [P, 2, T], F32))
    (kn,), e_ = region(e3 + 4 * T * 4, ("kn", [P, G, NB, 256], F32))
    uS, yS = stage[:, 0, :], stage[:, 1, :]
    LIM = nc.sbuf_usable_end
    assert max(e, e_) <= LIM and end0 <= LIM, (L0, e, e_, end0, LIM)
    (ss, bS, n8, smx, sls, srl, t8, nv8, pTs, mk, w_grp), e = region(
        e1, ("ss", [NS, HG, G, NK + 1], F32), ("bS", [NS, HG * G, NK + 1], F32), ("n8", [NS, 12], F32),
        ("smx", [NS, HG], F32), ("sls", [NS, HG], F32), ("srl", [NS, HG], F32),
        ("t8", [NS, AW], F32), ("nv8", [NS, 256], F32), ("pTs", [P, G, NS, HG], F32), ("mk", [HG, 2, 256], F32),
        ("w_grp", [P, 4, P], F32))
    assert e <= e2, (e, e2)
    v_s = k_s
    (t_tails,), e = region(e1 - 2 * AW * 4, ("t_tails", [23, 2, 512], F32))
    assert e <= e1
    (merged,), e = region(L0, ("merged", [P, KD, T], F32))
    (bH, bL), e = region(e, ("bH", [P, 10, T], F32R), ("bL", [P, 10, T], F32R))
    (sg, mt), eM = region(e, ("sg", [P, 3, T], F32), ("mt", [P, 2, T], F32))
    assert eM <= e3, (eM, e3)
    mixT = merged
    (xR, sacc, rbn, sqc), eO = region(L0 + KD * T * 4, ("xR", [P, KD, T], F32), ("sacc", [P, T], F32), ("rbn", [P, T], F32), ("sqc", [P, 2, T], F32))
    (acc, fH, fL, us, cv, ft, trow, st_rows, st_f, sqf, rbf), eF = region(
        L0, ("acc", [P, KD, T], F32), ("fH", [P, FPR, T], F32R), ("fL", [P, FPR, T], F32R),
        ("us", [P, 2, T], F32), ("cv", [P, 2, T], F32), ("ft", [P, T], F32),
        ("trow", [10, 2, 512], F32), ("st_rows", [16, 2, 512], F32), ("st_f", [P, 2, 4, NS, 2], F32),
        ("sqf", [P, 2, T], F32), ("rbf", [P, T], F32))
    assert eF <= LIM, (eF, LIM)
    (x1, yN, yNs), e = region(H0, ("x1", [P, KD, T], F32), ("yN", [P, 2, D], F32), ("yNs", [NS, D], F32))
    assert e <= L0

    X = nc.alloc_psum_tensor("X", [P, 2, 512], F32).ap()
    Y = nc.alloc_psum_tensor("Y", [P, 2, 512], F32).ap()
    BA = nc.alloc_psum_tensor("BA", [P, 512], F32).ap()
    BT = nc.alloc_psum_tensor("BT", [P, 512], F32).ap()
    BS = nc.alloc_psum_tensor("BS", [P, 512], F32).ap()
    BO = nc.alloc_psum_tensor("BO", [P, 512], F32).ap()
    PAIR = (X, Y)
    half = lambda t, h: t[:, h * HALF:(h + 1) * HALF]

    d_x = nc.dram_tensor("d_x", (P, KD * T), F32, kind="Internal").ap()
    d_x1 = nc.dram_tensor("d_x1", (P, KD * T), F32, kind="Internal").ap()
    d_bias = nc.dram_tensor("d_bias", (HG, G, BW), F32, kind="Internal").ap()
    d_table = nc.dram_tensor("d_table", (HG, P, G, RW), F32, kind="Internal").ap()
    d_q = nc.dram_tensor("d_q", (NS, AW), F32, kind="Internal").ap()

    sems = {}

    def sem(name):
        sems[name] = nc.alloc_semaphore(name)
        return sems[name]

    w_raw = [sem(f"w_raw{i}") for i in range(RAW)]
    w_hi, w_lo, w_used, w_attn = sem("w_hi"), sem("w_lo"), sem("w_used"), sem("w_attn")
    x_free, y_free = sem("x_free"), sem("y_free")
    free = (x_free, y_free)
    act_step, dve_step = sem("act_step"), sem("dve_step")
    c_in, k_in, x_in, row_in, bias_in = sem("c_in"), sem("k_in"), sem("x_in"), sem("row_in"), sem("bias_in")
    set_up, silu, c_tr, c_split = sem("set_up"), sem("silu"), sem("c_tr"), sem("c_split")
    par_tr, par_out, b_mm, b_out = sem("par_tr"), sem("par_out"), sem("b_mm"), sem("b_out")
    x_tr, x_out, ssq_done, diag_done, rb_mm, rb_done = sem("x_tr"), sem("x_out"), sem("ssq_done"), sem("diag_done"), sem("rb_mm"), sem("rb_done")
    rt_done = sem("rt_done")
    mod_mm, mod_row, mod_bias, mod_tr, mod_out = sem("mod_mm"), sem("mod_row"), sem("mod_bias"), sem("mod_tr"), sem("mod_out")
    h_pre, h_hi, h_lo = sem("h_pre"), sem("h_hi"), sem("h_lo")
    bias_st, table_st, xT_st, q_st = sem("bias_st"), sem("table_st"), sem("xT_st"), sem("q_st")
    stage_in, nat_tr, qk_out, nat_out = sem("stage_in"), sem("nat_tr"), sem("qk_out"), sem("nat_out")
    kv_st, out_st = sem("kv_st"), sem("out_st")
    u_in, q2_in, u_used = sem("u_in"), sem("q2_in"), sem("u_used")
    s_mm, s_soft, s_exp, p_tr, p_out, o_mm, o_out, oT_tr, oT_out = (
        sem(n) for n in ("s_mm", "s_soft", "s_exp", "p_tr", "p_out", "o_mm", "o_out", "oT_tr", "oT_out"))
    c_cp, ks_used = sem("c_cp"), sem("ks_used")
    qB_in, ks_in, vs_in = ([sem(f"{n}{i}") for i in range(2)] for n in ("qB_in", "ks_in", "vs_in"))
    ss_tr, ss_in, ss_max, ss_exp, ss_norm, pts_tr, pts_out, vs_mm, vs_out, nv_out, oTs_mm, oTs_out = (
        sem(n) for n in ("ss_tr", "ss_in", "ss_max", "ss_exp", "ss_norm", "pts_tr", "pts_out", "vs_mm", "vs_out", "nv_out", "oTs_mm", "oTs_out"))
    tail_free = sem("tail_free")
    bS_in, branch_turn, st_seen = sem("bS_in"), sem("branch_turn"), sem("st_seen")
    ptail_tr, ptail_out, pool_done, grp_in, grp_mm, grp_out, b_hi, b_lo = (
        sem(n) for n in ("ptail_tr", "ptail_out", "pool_done", "grp_in", "grp_mm", "grp_out", "b_hi", "b_lo"))
    gate_out, br_mm, br_out = sem("gate_out"), sem("br_mm"), sem("br_out")
    m_hi, m_lo = sem("m_hi"), sem("m_lo")
    mix_out, sacc_done, rbn_mm, rt2, x_back, x1_done, sq_in, sq_mm = (
        sem(n) for n in ("mix_out", "sacc_done", "rbn_mm", "rt2", "x_back", "x1_done", "sq_in", "sq_mm"))
    h2_pre, h2_hi, h2_lo = sem("h2_pre"), sem("h2_hi"), sem("h2_lo")
    st_in, st_tr, st_out, us_in, us_c, cv_done, gelu_done, f_done, f_hi, f_lo = (
        sem(n) for n in ("st_in", "st_tr", "st_out", "us_in", "us_c", "cv_done", "gelu_done", "f_done", "f_hi", "f_lo"))
    tail_tr, tail_out, tail_st, down_mm, down_out = (sem(n) for n in ("tail_tr", "tail_out", "tail_st", "down_mm", "down_out"))
    x1_st, x1_back, sqf_in, sqf_mm, rbf_mm, rt3, y_done, y_tr, y_nat = (
        sem(n) for n in ("x1_st", "x1_back", "sqf_in", "sqf_mm", "rbf_mm", "rt3", "y_done", "y_tr", "y_nat"))
    y_st = [sem(f"y_st{i}") for i in range(3)]

    kview = lambda w: w.rearrange("(k p) n -> p k n", p=P)
    w_ada, w_in, w_o, w_up, w_down = (kview(a[n][0]) for n in ("w_ada", "w_in", "w_o", "w_up", "w_down"))
    w_pool_br, w_conv_br, w_attn_br = (kview(a[n][0]) for n in ("w_pool_br", "w_conv_br", "w_attn_br"))

    def sync_program(sp):
        def load(u, dst, src, free=False):
            if not free:
                sp.wait_ge(w_lo, u.raw_free)
            sp.dma_start(dst, src).then_inc(w_raw[u.raw], 16)

        def slab(u, w, k0, col, k=8, width=P, off=0, free=False):
            dst = raw[:, u.raw, off * P:(off + k * width // P) * P].rearrange("p (k n) -> p k n", n=width)
            load(u, dst, w[:, k0:k0 + k, bass.ds(col, width)], free)

        def ada_tile(base, per, it, l0, tile):
            for l in range(8):
                slab(Unit(base, per, it, l0 + l), w_ada, 2 * l, tile * 512, k=2, width=512)

        sp.dma_start(ident, a["ident"]).then_inc(c_in, 16)
        sp.dma_start(cc[0:1, :], a["c_prompt"]).then_inc(c_in, 16)
        sp.dma_start(cc[1:9, :], a["c_sample"]).then_inc(c_in, 16)
        with sp.Fori(0, 8) as it:
            ada_tile(U_ADA, 8, it, 0, it)
        with sp.Fori(0, 9) as it:
            for l in range(4):
                slab(Unit(U_QKV, 4, it, l), w_in, 8 * (l % 2), it * 256 + l // 2 * P)
        with sp.Fori(0, 2) as it:
            for c, col in enumerate((COL_P, COL_P + P, COL_C, COL_H, COL_B, COL_C + P, COL_H + P, COL_B + P)):
                for l in range(2):
                    slab(Unit(U_PC, 16, it, 2 * c + l), w_in, 8 * l, it * 256 + col)
        with sp.Fori(0, KD) as it:
            for l in range(6):
                slab(Unit(U_M, 16, it, l), w_in, 8 * (l % 2), it * P + (COL_G + l // 2 * D))
            ada_tile(U_M, 16, it, 6, it + 8)
            u = Unit(U_M, 16, it, 14)
            sp.wait_ge(w_lo, u.raw_free)
            sp.sem_inc(branch_turn, 1)
            slab(u, w_pool_br, 0, it * P, k=4, free=True)
            sp.dma_start(raw[:, u.raw, 4 * P:6 * P].rearrange("p (k n) -> p k n", n=P),
                         w_attn_br[:, 0:2, bass.ds(it * P, P)]).then_inc(w_attn, 16)
            slab(Unit(U_M, 16, it, 15), w_conv_br, 0, it * P, k=4)
        with sp.Fori(0, 8) as it:
            for l in range(4):
                slab(Unit(U_O, 4, it, l), w_o, 8 * (l % 2), it * 256 + l // 2 * P)

        def up(base, per, it, l0, rnd, pair):
            for l in range(4):
                slab(Unit(base, per, it, l0 + l), w_up, 8 * (l % 2), rnd * 512 + (pair * P + l // 2 * DFF))

        def down(base, per, it, l0, rnd):
            rows = a["w_down"][0].rearrange("(r k p) n -> r p k n", p=P, k=FPR)
            for l in range(8):
                u = Unit(base, per, it, l0 + l)
                load(u, raw[:, u.raw, :].rearrange("p (k n) -> p k n", n=256),
                     rows[bass.ds(rnd, 1), :, :, l * 256:(l + 1) * 256].rearrange("r p k n -> (r p) k n"))

        for pair in range(FPR):
            up(U_F0, 16, 0, 4 * pair, 0, pair)
        with sp.Fori(0, 10) as it:
            up(U_F, 24, it, 0, it + 1, 0)
            down(U_F, 24, it, 4, it)
            for pair in range(1, FPR):
                up(U_F, 24, it, 8 + 4 * pair, it + 1, pair)
        down(U_END, 8, 0, 0, ROUNDS - 1)

    def pool_program(gp):
        big = lambda w: w.rearrange("(b p) n -> p b n", p=P)
        gp.dma_start(rows1[0:64, :], a["norm_g"][0].rearrange("n (k p) -> (n k) p", p=P)).then_inc(row_in, 16)
        gp.dma_start(rows1[64:76, :], a["conv_w"][0].rearrange("n (k p) -> (n k) p", p=P)).then_inc(row_in, 16)
        gp.dma_start(rows1[76:80, :], a["pool_scale"][0].rearrange("(k p) -> k p", p=P)).then_inc(row_in, 16)
        gp.dma_start(rowsF, a["ffn_conv_w"][0].rearrange("t (k p) -> k t p", p=P)).then_inc(row_in, 16)
        gp.dma_start(rowsC, a["state_conv"][0].rearrange("b r n -> (b r) n")).then_inc(row_in, 16)
        gp.dma_start(rowsP, a["state_pool"][0].rearrange("b r n -> (b r) n")).then_inc(row_in, 16)
        gp.wait_ge(set_up, 1)
        gp.dma_start(relb[0:32, :], a["rel_bias"]).then_inc(bias_in, 16)
        gp.dma_start(onehot, a["onehot"]).then_inc(bias_in, 16)
        gp.dma_start(sel, a["sel"]).then_inc(k_in, 16)
        gp.dma_start(heads_mask, a["heads"]).then_inc(k_in, 16)
        gp.dma_start(counts, a["counts"]).then_inc(k_in, 16)
        for b in range(NB):
            gp.dma_start(xN[:, b, :], a["x_prompt"][0, b * P:(b + 1) * P, :]).then_inc(x_in, 16)
        gp.dma_start(xs, a["x_sample"].rearrange("b t n -> (b t) n")).then_inc(x_in, 16)
        gp.dma_start(out["pool_s"][0, :, 0:14, :], a["state_pool"][0, :, 1:15, :]).then_inc(out_st, 16)
        gp.dma_start(out["conv_s"][0, :, 0, :], a["state_conv"][0, :, 1, :]).then_inc(out_st, 16)
        gp.dma_start(out["ffn_s"][0, :, 0, :], a["state_ffn_conv"][0, :, 1, :]).then_inc(out_st, 16)
        gp.wait_ge(b_out, 6)
        gp.dma_start(d_bias, brows).then_inc(bias_st, 16)
        gp.wait_ge(bias_st, 16)
        for h in range(HG):
            gp.dma_start(d_table[h], d_bias[h, :, 0:RW].unsqueeze(0).to_broadcast([P, G, RW])).then_inc(table_st, 16)
        gp.wait_ge(x_out, 17)
        gp.dma_start(d_x, xT.rearrange("p k t -> p (k t)")).then_inc(xT_st, 16)

        def mod_bias_row(tile):
            gp.dma_start(mod_rows[18:19, :], a["b_ada"][0:1, bass.ds(tile * 512, 512)]).then_inc(mod_bias, 16)

        mod_bias_row(0)
        with gp.Fori(0, 7) as it:
            gp.wait_ge(mod_tr, it + 2)
            mod_bias_row(it + 1)
        gp.wait_ge(nat_out, QCH + 2)
        gp.dma_start(d_q, ns[:, 0:AW]).then_inc(q_st, 16)
        gp.wait_ge(nat_out, 2 * QCH + 2)
        for g, name in enumerate(("kv128_p", "kv512_p", "kv2048_p")):
            store_kv(gp, kn, 0, g, name)
        gp.wait_ge(nat_out, 3 * QCH + 2)
        for g, name in enumerate(("kv128_p", "kv512_p", "kv2048_p")):
            store_kv(gp, vn, 1, g, name)
            for kv in range(2):
                c0 = (1 + kv) * AW + g * 256
                gp.dma_start(out[name[:-1] + "s"][0, :, 0, kv, :, :].rearrange("b h d -> b (h d)"),
                             ns[:, c0:c0 + 256]).then_inc(kv_st, 16)
        gp.wait_ge(q_st, 16)
        gp.wait_ge(table_st, 16 * HG)
        caches = [a[n] for n in ("cache_kv_w128", "cache_kv_w512", "cache_kv_w2048")]

        def cache_rows(dst, b, kv, done):
            for g in range(G):
                rows = caches[g][0].rearrange("b (i d) v h e -> b i d v (h e)", d=DIL[g])[bass.ds(b, 1), :, 0, kv, :]
                gp.dma_start(dst[:, g * 256:(g + 1) * 256], rows.rearrange("b i e -> (b i) e")).then_inc(done, 16)

        with gp.Fori(0, 2) as it:
            gp.wait_ge(u_used, it + 1)
            for h in range(2):
                for g0, n, w, c in ((0, 1, 256, 0), (1, 2, 512, 256)):
                    rows = bass.AP(d_table.tensor, g0 * RW + P - 1 + 512 - w,
                                   [[P * G * RW, HG], [G * RW - 1, P], [RW, n], [1, w]])
                    gp.dma_start(u_bias[:, h, c:c + n * w].rearrange("p (g n) -> p g n", n=w),
                                 rows[bass.ds(it * 2 + h, 1)].rearrange("h p g n -> (h p) g n")).then_inc(u_in, 16)
            for b in range(4):
                s = b % 2
                gp.wait_ge(ks_used, it * 4 + b + 1)
                gp.dma_start(qB[:, s, :], d_q[bass.ds(it * 4 + b, 1), :].to_broadcast([P, AW])).then_inc(qB_in[s], 16)
                cache_rows(k_s[:, s, :], it * 4 + b, 0, ks_in[s])
        gp.wait_ge(u_used, 3)
        gp.wait_ge(oT_out, 8)
        gp.dma_start(bS, d_bias[:, :, RW:BW].rearrange("h g n -> (h g) n").unsqueeze(0).to_broadcast([NS, HG * G, NK + 1])
                     ).then_inc(bS_in, 16)
        gp.dma_start(w_grp, a["w_pool_grp"][0].rearrange("g c e -> c g e")).then_inc(grp_in, 16)
        gp.wait_ge(ks_used, 10)
        for b in range(NS):
            if b >= 2:
                gp.wait_ge(vs_mm, b - 1)
            cache_rows(v_s[:, b % 2, :], b, 1, vs_in[b % 2])
        gp.wait_ge(ptail_out, 2)
        gp.dma_start(out["pool_p"][0, 0], t_tails[0:15, 0, :]).then_inc(out_st, 16)
        gp.dma_start(out["pool_s"][0, :, 14, :], t_tails[15:23, 0, :]).then_inc(out_st, 16)
        gp.dma_start(out["conv_p"][0, 0], t_tails[0:2, 1, :]).then_inc(out_st, 16)
        gp.dma_start(out["conv_s"][0, :, 1, :], t_tails[2:10, 1, :]).then_inc(out_st, 16)
        with gp.Fori(0, KD) as it:
            gp.wait_ge(mod_tr, it + 9)
            mod_bias_row(it + 8)
        gp.wait_ge(xT_st, 16)
        gp.wait_ge(w_used, Unit(U_M, 16, KD - 1, 15).used)
        gp.wait_ge(br_out, 3 * KD + 1)
        gp.dma_start(xR.rearrange("p k t -> p (k t)"), d_x).then_inc(x_back, 16)
        gp.wait_ge(x1_done, KD)
        gp.dma_start(d_x1, xR.rearrange("p k t -> p (k t)")).then_inc(x1_st, 16)
        gp.wait_ge(x1_st, 16)

        def state_rows(rnd):
            for v in range(2):
                gp.dma_start(st_rows[:, v, :], a["state_ffn_conv"][0, :, :, bass.ds(rnd * 512 + v * DFF, 512)]
                             .rearrange("b r n -> (b r) n")).then_inc(st_in, 16)

        def store_tails(rnd):
            for v in range(2):
                col = bass.ds(rnd * 512 + v * DFF, 512)
                gp.dma_start(out["ffn_p"][0, 0, :, col], trow[0:2, v, :]).then_inc(tail_st, 16)
                gp.dma_start(out["ffn_s"][0, :, 1, col], trow[2:10, v, :]).then_inc(tail_st, 16)

        gp.wait_ge(h2_lo, KD)
        state_rows(0)
        with gp.Fori(0, 10) as it:
            gp.wait_ge(st_tr, it + 1)
            state_rows(it + 1)
            gp.wait_ge(tail_out, it * 4 + 5)
            store_tails(it)
            gp.wait_ge(tail_st, it * 64 + 64)
            gp.sem_inc(tail_free, 4)
        gp.wait_ge(tail_out, 4 * ROUNDS + 1)
        store_tails(ROUNDS - 1)
        gp.wait_ge(w_used, Unit(U_F, 24, 9, 23).used)
        gp.dma_start(x1.rearrange("p k t -> p (k t)"), d_x1).then_inc(x1_back, 16)
        for b in range(NB):
            gp.wait_ge(y_nat, 4 * b + 4)
            gp.dma_start(out["y_p"][0, b * P:(b + 1) * P, :], yN[:, b % 2, :]).then_inc(y_st[b % 2], 16)
        gp.wait_ge(y_nat, 20)
        gp.dma_start(out["y_s"].rearrange("b t n -> (b t) n"), yNs).then_inc(y_st[2], 16)
        for s, n in enumerate((2, 2, 1)):
            gp.wait_ge(y_st[s], 16 * n)
        gp.wait_ge(out_st, 16 * 7)
        gp.wait_ge(kv_st, 16 * 12)
        gp.wait_ge(tail_st, 16 * 4 * ROUNDS)

    def store_kv(gp, nat, kv, g, name):
        dst = out[name][0, 0, :, kv, :, :].rearrange("t h d -> t (h d)")
        if g == 0:
            gp.dma_start(dst, nat[:, g, NB - 1, :]).then_inc(kv_st, 16)
        else:
            gp.dma_start(dst.rearrange("(b p) n -> p b n", p=P), nat[:, g, :, :]).then_inc(kv_st, 16)

    def scalar_program(act):
        step = Step(act, act_step)

        def hi(u):
            act.wait_ge(w_raw[u.raw], u.arrived)
            act.wait_ge(w_used, u.spl_free)
            nc.scalar.copy(whi[:, u.spl, :], raw[:, u.raw, :]).then_inc(w_hi, 1)

        def lead(base, per, it, l):
            hi(Unit(base, per, it, l + 2))

        act.wait_ge(c_in, 48)
        nc.scalar.activation(csig, cc, ACT.Sigmoid).then_inc(silu, 1)
        act.wait_ge(x_in, 16 * 5)
        for b in range(NB):
            nc.scalar.activation(sqj, xN[:, b, :], ACT.Square, accum_out=ssq[:, b:b + 1]).then_inc(ssq_done, 1)
            act.wait_ge(ssq_done, b + 1)
        nc.scalar.activation(sqj[0:NS, :], xs, ACT.Square, accum_out=ssq[0:NS, 4:5]).then_inc(ssq_done, 1)
        act.wait_ge(ssq_done, 5)
        act.wait_ge(set_up, 1)
        nc.scalar.activation(rs[:, 0:4], ssq[:, 0:4], ACT.Sqrt, bias=eps, scale=1.0 / D).then_inc(rt_done, 1)
        nc.scalar.activation(rs[0:NS, 4:5], ssq[0:NS, 4:5], ACT.Sqrt, bias=eps[0:NS], scale=1.0 / D).then_inc(rt_done, 1)
        for i, (g, n0, n1) in enumerate(BIAS_MM):
            act.wait_ge(b_mm, i + 1)
            nc.scalar.copy(brows[:, g, n0:n1], BIAS_BANK[i][0:HG, 0:n1 - n0]).then_inc(b_out, 1)
        act.wait_ge(x_tr, 17)
        act.wait_ge(rb_mm, 1)
        nc.scalar.copy(rb[:, :TP], X[:, 0, :]).then_inc(rb_done, 1)
        nc.scalar.copy(rb[:, TP:], X[:, 1, 0:NS]).then_inc(rb_done, 1)

        for l in range(2):
            hi(Unit(0, 0, 0, l))
        with act.Fori(0, 8) as it:
            for l in range(8):
                lead(U_ADA, 8, it, l)
            act.wait_ge(w_used, Unit(U_ADA, 8, it, 7).used)
            act.wait_ge(mod_tr, it + 1)
            nc.scalar.copy(mod_rows[0:18, :], BA[0:18, :]).then_inc(mod_row, 1)
        for k in range(KD):
            act.wait_ge(h_pre, k + 1)
            nc.scalar.copy(hH[:, k, :], xr[:, k, :]).then_inc(h_hi, 1)
        for part in range(3):
            with act.Fori(0, 3) as it:
                for l in range(4):
                    lead(U_QKV + 12 * part, 4, it, l)
                    if l % 2:
                        c = it * 2 + (l // 2 + 6 * part)
                        act.wait_ge(w_used, Unit(U_QKV + 12 * part, 4, it, l).used)
                        act.wait_ge(nat_tr, c + 1)
                        act.wait_ge(qk_out, c + 1)
                        act.copy(half(stage[:, l // 2, :], 0), PAIR[l // 2][:, 0, 0:HALF])
                        act.copy(half(stage[:, l // 2, :], 1), PAIR[l // 2][:, 1, 0:HALF]).then_inc(free[l // 2], 1)
        with act.Fori(0, 2) as it:
            for c in range(8):
                h, qb = c % 2, c // 2
                w0, w = min(qb + 1, 2) * P, (qb + 1) * P
                wide = w0 + 2 * w
                m = it * 8 + c
                act.wait_ge(s_soft, m + 1)
                act.wait_ge(o_out, m + 1)
                nc.scalar.activation(sc_p[:, 0:wide], sc_p[:, 0:wide], ACT.Exp, bias=nm[:, h:h + 1],
                                     accum_out=ls[:, h:h + 1]).then_inc(s_exp, 1)
                lead(U_PC, 16, it, 2 * c)
                act.wait_ge(p_tr, m + 1)
                nt = wide // P
                act.wait_ge(o_mm, m + 1)
                for i, bank in enumerate((BT, BS, BA)):
                    n = min(4, nt - 4 * i)
                    if n > 0:
                        ins = act.copy(pT_t[:, 4 * i:4 * i + n, :], bank[:, 0:n * P].rearrange("p (n q) -> p n q", q=P))
                ins.then_inc(p_out, 1)
                lead(U_PC, 16, it, 2 * c + 1)
                pair = PAIR[c % 2]
                act_chunk = (c < 2) or c in (2, 5)
                if act_chunk:
                    act.wait_ge(w_used, Unit(U_PC, 16, it, 2 * c + 1).used)
                if c < 2:
                    for hf in range(2):
                        dst = pT[:, bass.ds(it * 2 + c, 1), hf * HALF:(hf + 1) * HALF].rearrange("p k t -> p (k t)")
                        ins = act.copy(dst, pair[:, hf, 0:HALF])
                    ins.then_inc(free[c % 2], 1)
                if c in (2, 5):
                    act.wait_ge(c_cp, it * 2 + (1 if c == 2 else 2))
                    act.copy(half(cS, 0), pair[:, 0, 0:HALF])
                    act.copy(half(cS, 1), pair[:, 1, 0:HALF]).then_inc(free[c % 2], 1)
        act.wait_ge(ss_max, 1)
        for h in range(HG):
            nc.scalar.activation(ss[:, h, :, :], ss[:, h, :, :], ACT.Exp, bias=smx[:, h:h + 1],
                                 accum_out=sls[:, h:h + 1]).then_inc(ss_exp, 1)
        act.wait_ge(grp_out, 4)
        act.wait_ge(oTs_out, 1)
        act.wait_ge(out_st, 16 * 7)
        for i in range(4):
            nc.scalar.copy(bH[:, i, :], pT[:, i, :]).then_inc(b_hi, 1)
        for i in range(2):
            nc.scalar.copy(bH[:, 4 + i, :], aT[:, i, :]).then_inc(b_hi, 1)
        for i in range(4):
            nc.scalar.copy(bH[:, 6 + i, :], bcv[:, i, :]).then_inc(b_hi, 1)
        with act.Fori(0, KD) as it:
            for l in range(16):
                if l == 12:
                    act.wait_ge(w_attn, it * 16 + 16)
                lead(U_M, 16, it, l)
                if l in (1, 3, 5):
                    i = l // 2
                    act.wait_ge(w_used, Unit(U_M, 16, it, l).used)
                    act.wait_ge(br_out, it * 3 + 1)
                    for hf in range(2):
                        ins = nc.scalar.activation(half(sg[:, i, :], hf), PAIR[i % 2][:, hf, 0:HALF], ACT.Sigmoid)
                    ins.then_inc(free[i % 2], 1)
                if l == 13:
                    act.wait_ge(w_used, Unit(U_M, 16, it, 13).used)
                    act.wait_ge(mod_tr, it + 9)
                    nc.scalar.copy(mod_rows[0:18, :], BA[0:18, :]).then_inc(mod_row, 1)
        act.wait_ge(w_used, Unit(U_M, 16, KD - 1, 5).used)
        act.wait_ge(br_out, 3 * KD + 1)
        for k in range(KD):
            nc.scalar.copy(hH[:, k, :], merged[:, k, :]).then_inc(m_hi, 1)
        act.wait_ge(m_lo, KD)
        with act.Fori(0, 8) as it:
            for l in range(4):
                lead(U_O, 4, it, l)
                if l % 2:
                    act.wait_ge(w_used, Unit(U_O, 4, it, l).used)
                    dst = mixT[:, bass.ds(it * 2 + l // 2, 1), :].rearrange("p k t -> p (k t)")
                    act.copy(half(dst, 0), PAIR[l // 2][:, 0, 0:HALF]).then_inc(mix_out, 1)
                    act.copy(half(dst, 1), PAIR[l // 2][:, 1, 0:HALF]).then_inc(free[l // 2], 1)
        norm_root(act, rbn_mm, 1, rbn, rt2)
        for k in range(KD):
            act.wait_ge(x1_done, k + 1)
            if k >= 2:
                act.wait_ge(sq_mm, k - 1)
            nc.scalar.activation(sqc[:, k % 2, :], xR[:, k, :], ACT.Square).then_inc(sq_in, 1)
        act.wait_ge(h2_pre, 1)
        norm_root(act, sq_mm, KD, rbn, rt2)
        for k in range(KD):
            act.wait_ge(h2_pre, k + 2)
            nc.scalar.copy(hH[:, k, :], mixT[:, k, :]).then_inc(h2_hi, 1)

        act.wait_ge(x1_st, 16)
        act.wait_ge(h2_lo, KD)

        def up_pair(base, per, it, l0, rnd4, late=False):
            for l in range(4):
                if base == U_F0 or l0 + l < 24:
                    lead(base, per, it, l0 + l)
                if l % 2:
                    v = l // 2
                    act.wait_ge(w_used, Unit(base, per, it, l0 + l).used)
                    act.wait_ge(tail_tr, rnd4 + 1)
                    act.wait_ge(cv_done, rnd4 * 2 + (v + 1))
                    act.copy(half(us[:, v, :], 0), PAIR[v][:, 0, 0:HALF])
                    act.copy(half(us[:, v, :], 1), PAIR[v][:, 1, 0:HALF]).then_inc(free[v], 1)
                    act.wait_ge(free[v], CF(rnd4) + 2)
                    act.wait_ge(f_done, rnd4 + 1)
                    nc.scalar.mul(cv[:, v, :], us[:, v, :], tap(2, v, rnd4)).then_inc(us_c, 1)
            act.wait_ge(cv_done, rnd4 * 2 + 3)
            nc.scalar.activation(cv[:, 0, :], cv[:, 0, :], ACT.Gelu_apprx_tanh).then_inc(gelu_done, 1)
            if not late:
                f_split(rnd4)

        def f_split(rnd4, p=None):
            act.wait_ge(f_done, rnd4 + 2)
            nc.scalar.copy(fH[:, PAIRNO[0] if p is None else p, :], ft).then_inc(f_hi, 1)

        for pair in range(FPR):
            PAIRNO[0] = pair
            up_pair(U_F0, 16, 0, 4 * pair, pair)
        with act.Fori(0, 10) as it:
            r4 = it * 4 + 4
            up_pair(U_F, 24, it, 0, r4, late=True)
            for l in range(4, 12):
                lead(U_F, 24, it, l)
            act.wait_ge(w_used, Unit(U_F, 24, it, 11).used)
            f_split(r4, 0)
            for pair in range(1, FPR):
                PAIRNO[0] = pair
                up_pair(U_F, 24, it, 8 + 4 * pair, r4 + pair)
        for l in range(6):
            lead(U_END, 8, 0, l)
        for k in range(KD):
            act.wait_ge(down_out, 2 * (10 * KD + k) + 6)
            if k >= 2:
                act.wait_ge(sqf_mm, k - 1)
            nc.scalar.activation(sqf[:, k % 2, :], acc[:, k, :], ACT.Square).then_inc(sqf_in, 1)
        norm_root(act, sqf_mm, KD, rbf, rt3)

    PAIRNO = [0]
    CF = lambda rnd4: rnd4 + C_F0

    def tap(i, v, rnd4):
        return ffn_w[:, i, bass.ds(rnd4 + v * FCH, 1)]

    def norm_root(act, s, n, dst, done):
        act.wait_ge(s, n)
        act.activation(dst[:, 0:HALF], X[:, 0, 0:HALF], ACT.Sqrt, bias=eps, scale=1.0 / D)
        act.activation(dst[:, HALF:T], X[:, 1, 0:HALF], ACT.Sqrt, bias=eps, scale=1.0 / D).then_inc(done, 1)

    BIAS_MM = [(g, n0, n1) for g in range(G) for n0, n1 in ((0, 385), (385, BW))]
    BIAS_BANK = [BT, BS, BO, BA, Y[:, 0, :], Y[:, 1, :]]

    def vector_program(dve):
        step = Step(dve, dve_step)

        def lo(u):
            dve.wait_ge(w_hi, u.hi_done)
            dve.tensor_tensor(wlo[:, u.spl, :], raw[:, u.raw, :], whi[:, u.spl, :], ALU.subtract).then_inc(w_lo, 1)

        def lead(base, per, it, l):
            lo(Unit(base, per, it, l + 2))

        for s, n in ((w_lo, 4), (w_used, 2), (x_free, 1), (y_free, 1), (mod_tr, 1), (mod_row, 1), (mod_out, 1),
                     (nat_tr, 2), (qk_out, 2), (nat_out, 2), (o_out, 1), (o_mm, 1), (oT_tr, 1), (c_cp, 1), (ks_used, 2),
                     (u_used, 1), (p_out, 1), (tail_tr, 1), (tail_out, 1), (cv_done, 2), (f_done, 1), (f_hi, 1),
                     (tail_free, 4), (down_out, 4)):
            dve.sem_inc(s, n)
        dve.memset(ones, 1.0)
        dve.memset(eps, EPS)
        dve.memset(relb, 1.0).then_inc(set_up, 1)
        dve.wait_ge(silu, 1)
        step(dve.tensor_tensor(cc, cc, csig, ALU.mult))
        step.settle()
        dve.sem_inc(c_split, 1)
        dve.wait_ge(c_tr, 1)
        cps = BA[:, 0:KD * 9].rearrange("p (k n) -> p k n", n=9)
        step(dve.tensor_copy(cT[:, :, 0:9], cps))
        step.settle()
        dve.tensor_tensor(cT[:, :, 9:18], cps, cT[:, :, 0:9], ALU.subtract).then_inc(c_split, 1)
        dve.wait_ge(par_tr, 1)
        dve.tensor_copy(cols, BT[:, 0:80]).then_inc(par_out, 1)
        dve.tensor_copy(ffn_w, BS[:, 0:3 * 88].rearrange("p (t k) -> p t k", t=3)).then_inc(par_out, 1)
        dve.tensor_copy(st_conv, BO[:, 0:64].rearrange("p (k b r) -> p k b r", k=4, b=NS)).then_inc(par_out, 1)
        dve.tensor_copy(st_pool, X[:, 0, 0:480].rearrange("p (k b r) -> p k b r", k=4, b=NS)).then_inc(par_out, 1)
        for n in range(17):
            dve.wait_ge(x_tr, n + 1)
            bank = (X[:, 1, :], BT, BS, X[:, 0, :])[n % 4] if n < 16 else BO
            if n < 16:
                b, q = n // 4, n % 4
                dve.tensor_copy(xT[:, 4 * q:4 * q + 4, b * P:(b + 1) * P], bank.rearrange("p (k t) -> p k t", t=P)).then_inc(x_out, 1)
            else:
                dve.tensor_copy(xT[:, :, SA], bank[:, 0:KD * NS].rearrange("p (k t) -> p k t", t=NS)).then_inc(x_out, 1)
        dve.wait_ge(rt_done, 2)
        step(dve.reciprocal(rs[:, 0:4], rs[:, 0:4]))
        step(dve.reciprocal(rs[0:NS, 4:5], rs[0:NS, 4:5]))
        step.settle()
        for b in range(NB):
            step(dve.tensor_scalar(diag[:, b, :], ident, rs[:, b:b + 1], None, ALU.mult))
        dve.tensor_scalar(diag[0:NS, 4, 0:NS], ident[0:NS, 0:NS], rs[0:NS, 4:5], None, ALU.mult).then_inc(diag_done, 1)
        dve.wait_ge(rb_done, 2)
        for l in range(2):
            lo(Unit(0, 0, 0, l))
        with dve.Fori(0, 8) as it:
            step.enter(it, 2)
            for l in range(8):
                lead(U_ADA, 8, it, l)
                if l in (2, 5):
                    k = bass.ds(it * 2 + l // 3, 1)
                    flat = lambda t: t[:, k, :].rearrange("p k t -> p (k t)")
                    step(dve.tensor_tensor(flat(xr), flat(xT), rb, ALU.mult))
            mod_columns(dve, it, it + 1)
            step.leave(8)
        step.settle()
        dve.wait_ge(mod_out, 9)
        modulate(dve, step, xr, 0, 1, 0, h_pre, h_hi, h_lo, 1)
        for part in range(3):
            with dve.Fori(0, 3) as it:
                step.enter(it, 0)
                for l in range(4):
                    lead(U_QKV + 12 * part, 4, it, l)
                    i = l // 2
                    c = it * 2 + (i + 6 * part)
                    if l % 2:
                        dve.wait_ge(free[i], it + (3 * part + 2))
                        if part < 2:
                            dst = qk[:, bass.ds(c, 1), :].rearrange("p k t -> p (k t)")
                            dve.tensor_copy(dst, stage[:, i, 0:TP]).then_inc(qk_out, 1)
                        else:
                            dve.sem_inc(qk_out, 1)
                        dve.wait_ge(nat_tr, c + 3)
                        nat_rows = dve.tensor_copy(ns[:, bass.ds(c * P, P)], (BO, BA)[i][0:NS, 0:P])
                        if part == 0:
                            nat_rows.then_inc(nat_out, 1)
                        else:
                            nat = (kn, vn)[part - 1][:, bass.ds(it, 1), :, i * P:(i + 1) * P].rearrange("p g b n -> p (g b) n")
                            dve.tensor_copy(nat, (BT, BS)[i].rearrange("p (b n) -> p b n", n=P)).then_inc(nat_out, 1)
                step.leave(3)
        step(dve.memset(q2, 0.0))
        step.settle()
        with dve.Fori(0, 2) as it:
            step.enter(it, 58)
            def queries(c):
                h, qb = c % 2, c // 2
                src = qk[64 * h:64 * h + 64, 0:QCH, qb * P:(qb + 1) * P].rearrange("p (g j) q -> p j g q", j=2)
                dve.tensor_copy(q2[64 * h:64 * h + 64, h, :, :], src[:, bass.ds(it, 1)].rearrange("p j g q -> p (j g) q")).then_inc(q2_in, 1)

            queries(0)
            dve.wait_ge(u_in, it * 64 + 64)
            for c in range(8):
                h, qb = c % 2, c // 2
                m = it * 8 + c
                wg = [min(qb + 1, 2) * P, (qb + 1) * P, (qb + 1) * P]
                wide = sum(wg)
                dve.wait_ge(s_mm, m + 1)
                o = 0
                for g, bank in enumerate((BT, BS, BA)):
                    end = 256 if g == 0 else 256 + 512 * g
                    step(dve.scalar_tensor_tensor(out=sc_p[:, o:o + wg[g]], in0=bank[:, 0:wg[g]], scalar=SCALE,
                                                  in1=u_bias[:, h, end - wg[g]:end], op0=ALU.mult, op1=ALU.add))
                    o += wg[g]
                step.settle()
                step(dve.tensor_reduce(mx[:, h:h + 1], sc_p[:, 0:wide], AX.X, ALU.max))
                step.settle()
                dve.tensor_scalar(nm[:, h:h + 1], mx[:, h:h + 1], -1.0, None, ALU.mult).then_inc(s_soft, 1)
                if c < 7:
                    queries(c + 1)
                lead(U_PC, 16, it, 2 * c)
                if c % 2 == 0:
                    b = c // 2
                    s = b % 2
                    dve.wait_ge(qB_in[s], it * 32 + (b // 2 + 1) * 16)
                    dve.wait_ge(ks_in[s], it * 96 + (b // 2 + 1) * 48)
                    prod = k_s[:, s, :]
                    step(dve.tensor_tensor(prod, prod, qB[:, s, :], ALU.mult))
                    step.settle()
                    dst = sc_s[:, bass.ds(it * 4 + b, 1), :].rearrange("p b n -> p (b n)")
                    dve.tensor_reduce(dst, prod.rearrange("p (n e) -> p n e", e=DH), AX.X, ALU.add).then_inc(ks_used, 1)
                    dve.wait_ge(ks_used, it * 4 + b + 3)
                lead(U_PC, 16, it, 2 * c + 1)
                pair = PAIR[c % 2]
                kind, i = ("p", c) if c < 2 else ("chb"[(c - 2) % 3], (c - 2) // 3)
                if kind in "hb":
                    dve.wait_ge(w_used, Unit(U_PC, 16, it, 2 * c + 1).used)
                if kind == "h":
                    dve.wait_ge(free[(c - 1) % 2], it * 4 + (C_PC + (c - 1) // 2 + 2))
                    step(dve.tensor_tensor(half(uS, 0), half(cS, 0), pair[:, 0, 0:HALF], ALU.mult))
                    dve.tensor_tensor(half(uS, 1), half(cS, 1), pair[:, 1, 0:HALF], ALU.mult).then_inc(free[c % 2], 1)
                    step.settle()
                    dve.wait_ge(free[c % 2], it * 4 + (C_PC + c // 2 + 2))
                    dve.sem_inc(c_cp, 1)
                    ci = it * 2 + i
                    w = lambda t: cols[:, bass.ds(ci + (64 + 4 * t), 1)]
                    st = lambda r: st_conv[:, bass.ds(ci, 1), :, r].rearrange("p k b -> p (k b)")
                    step(dve.tensor_copy(utail[:, bass.ds(ci, 1), :].rearrange("p k t -> p (k t)"), uS[:, TP - 2:T]))
                    step(dve.tensor_scalar(yS, uS, w(2), None, ALU.mult))
                    step.settle()
                    stt = lambda o, x_, w_: dve.scalar_tensor_tensor(out=o, in0=x_, scalar=w_, in1=o, op0=ALU.mult, op1=ALU.add)
                    step(stt(yS[:, 1:TP], uS[:, 0:TP - 1], w(1)))
                    step(stt(yS[:, SA], st(1), w(1)))
                    step.settle()
                    step(stt(yS[:, 2:TP], uS[:, 0:TP - 2], w(0)))
                    step(stt(yS[:, SA], st(0), w(0)))
                    step.settle()
                if kind == "b":
                    for hf in range(2):
                        dst = bcv[:, bass.ds(it * 2 + i, 1), hf * HALF:(hf + 1) * HALF].rearrange("p k t -> p (k t)")
                        ins = dve.tensor_tensor(dst, half(yS, hf), pair[:, hf, 0:HALF], ALU.mult)
                    ins.then_inc(free[c % 2], 1)
                dve.wait_ge(s_exp, m + 1)
                step(dve.reciprocal(rl[:, h:h + 1], ls[:, h:h + 1]))
                step.settle()
                dve.wait_ge(o_mm, m + 2)
                if h == 0:
                    dve.wait_ge(oT_tr, it * 4 + (qb + 1))
                dve.tensor_scalar(osb[:, h, :], BO[:, 0:DH], rl[:, h:h + 1], None, ALU.mult).then_inc(o_out, 1)
                if h == 1:
                    dve.wait_ge(oT_tr, it * 4 + (qb + 2))
                    dst = aT[:, bass.ds(it, 1), qb * P:(qb + 1) * P].rearrange("p k t -> p (k t)")
                    dve.tensor_copy(dst, BO[:, P:2 * P]).then_inc(oT_out, 1)
            dve.sem_inc(u_used, 1)
            step.leave(2)
        dve.wait_ge(oT_out, 8)
        dve.wait_ge(bS_in, 16)
        bv = bS.rearrange("p (h g) n -> p h g n", g=G)
        dve.wait_ge(ss_tr, 1)
        n = 0
        for h in range(HG):
            for g in range(G):
                bank = (BT, BS, BA)[n // 4]
                step(dve.scalar_tensor_tensor(out=ss[:, h, g, 0:NK], in0=bank[0:NS, n % 4 * P:(n % 4 + 1) * P], scalar=SCALE,
                                              in1=bv[:, h, g, 0:NK], op0=ALU.mult, op1=ALU.add))
                n += 1
        step(dve.tensor_tensor(t8, ns[:, 0:AW], ns[:, AW:2 * AW], ALU.mult))
        step.settle()
        step(dve.tensor_reduce(n8, t8.rearrange("p (n e) -> p n e", e=DH), AX.X, ALU.add))
        step.settle()
        step(dve.scalar_tensor_tensor(out=ss[:, :, :, NK], in0=n8.rearrange("p (g h) -> p h g", g=G), scalar=SCALE,
                                      in1=bv[:, :, :, NK], op0=ALU.mult, op1=ALU.add))
        step.settle()
        step(dve.tensor_reduce(smx, ss.rearrange("p h g n -> p h (g n)"), AX.X, ALU.max))
        step.settle()
        dve.tensor_scalar(smx, smx, -1.0, None, ALU.mult).then_inc(ss_max, 1)
        dve.wait_ge(ss_exp, HG)
        step(dve.reciprocal(srl, sls))
        step.settle()
        for h in range(HG):
            ins = dve.tensor_scalar(ss[:, h, :, :], ss[:, h, :, :], srl[:, h:h + 1], None, ALU.mult)
            if h < HG - 1:
                step(ins)
        ins.then_inc(ss_norm, 1)
        dve.wait_ge(ss_norm, 1)
        v4 = ns[:, 2 * AW:3 * AW].rearrange("p (g h e) -> p g h e", g=G, h=HG)
        t4 = t8.rearrange("p (g h e) -> p g h e", g=G, h=HG)
        for g in range(G):
            step(dve.tensor_tensor(t4[:, g], v4[:, g], ss[:, :, g, NK:NK + 1].to_broadcast([NS, HG, DH]), ALU.mult))
        step.settle()
        step(dve.tensor_tensor(nv8, t8[:, 0:256], t8[:, 256:512], ALU.add))
        step.settle()
        dve.tensor_tensor(nv8, nv8, t8[:, 512:768], ALU.add).then_inc(nv_out, 1)
        dve.wait_ge(pts_tr, 1)
        pts = BT[:, 0:12 * NS].rearrange("p (h g b) -> p h g b", h=HG, g=G)
        for h in range(HG):
            ins = dve.tensor_copy(pTs[:, :, :, h], pts[:, h])
        ins.then_inc(pts_out, 1)
        for b in range(NS):
            dve.wait_ge(vs_mm, b + 1)
            bank = (BS, BA)[b % 2]
            dve.tensor_tensor(mk[:, b % 2, :], bank[0:HG, 0:256], heads_mask, ALU.mult).then_inc(vs_out, 1)
        dve.wait_ge(oTs_mm, 1)
        dve.tensor_copy(aT[:, :, SA], BO[:, 0:2 * NS].rearrange("p (c b) -> p c b", c=2)).then_inc(oTs_out, 1)
        dve.wait_ge(ptail_tr, 1)
        dve.tensor_copy(t_tails[:, 0, :], X[0:23, 0, :]).then_inc(ptail_out, 1)
        dve.tensor_copy(t_tails[0:10, 1, :], X[0:10, 1, :]).then_inc(ptail_out, 1)
        for i, w in enumerate(WIN):
            pc = pT[:, i, :]
            a_, b_ = stage[:, 0, :], stage[:, 1, :]
            src, width = pc, 1
            while width < w:
                dst = a_ if src is not a_ else b_
                step(dve.tensor_tensor(dst[:, width:TP], src[:, width:TP], src[:, 0:TP - width], ALU.add))
                step(dve.tensor_copy(dst[:, 0:width], src[:, 0:width]))
                step.settle()
                src, width = dst, 2 * width
            oth = a_ if src is not a_ else b_
            step(dve.tensor_tensor(oth[:, 0:16], src[:, 0:16], counts[:, i, :], ALU.mult))
            step(dve.tensor_reduce(oth[:, TP:T], st_pool[:, i, :, 16 - w:15], AX.X, ALU.add))
            step.settle()
            step(dve.tensor_tensor(oth[:, TP:T], oth[:, TP:T], pc[:, SA], ALU.add))
            step.settle()
            step(dve.scalar_tensor_tensor(out=pc[:, 16:TP], in0=src[:, 16:TP], scalar=1.0 / w, in1=pc[:, 16:TP],
                                          op0=ALU.mult, op1=ALU.subtract))
            step(dve.tensor_tensor(pc[:, 0:16], oth[:, 0:16], pc[:, 0:16], ALU.subtract))
            dve.scalar_tensor_tensor(out=pc[:, SA], in0=oth[:, TP:T], scalar=1.0 / w, in1=pc[:, SA],
                                     op0=ALU.mult, op1=ALU.subtract).then_inc(pool_done, 1)
            step.settle()
            dve.wait_ge(pool_done, i + 1)
        for i in range(4):
            pair = PAIR[i % 2]
            dve.wait_ge(grp_mm, i + 1)
            step(dve.tensor_scalar(half(pT[:, i, :], 0), pair[:, 0, 0:HALF], cols[:, 76 + i:77 + i], None, ALU.mult))
            dve.tensor_scalar(half(pT[:, i, :], 1), pair[:, 1, 0:HALF], cols[:, 76 + i:77 + i], None, ALU.mult).then_inc(grp_out, 1)
        for i in range(10):
            dve.wait_ge(b_hi, i + 1)
            src = pT[:, i, :] if i < 4 else aT[:, i - 4, :] if i < 6 else bcv[:, i - 6, :]
            dve.tensor_tensor(bL[:, i, :], src, bH[:, i, :], ALU.subtract).then_inc(b_lo, 1)
        dve.wait_ge(b_lo, 10)
        dve.wait_ge(kv_st, 16 * 12)
        dve.sem_inc(br_out, 1)
        with dve.Fori(0, KD) as it:
            step.enter(it, 3)
            dst = merged[:, bass.ds(it, 1), :].rearrange("p k t -> p (k t)")
            for l in range(14):
                lead(U_M, 16, it, l)
            for n, (i, pr) in enumerate(((0, 1), (2, 0), (1, 1))):
                if n == 0:
                    dve.wait_ge(br_mm, it + 1)
                    dve.wait_ge(x_free, it * 3 + (C_M + 3))
                    dve.wait_ge(y_free, it * 3 + (C_M + 2))
                else:
                    lead(U_M, 16, it, 13 + n)
                    dve.wait_ge(w_used, Unit(U_M, 16, it, 13 + n).used)
                for hf in range(2):
                    o = half(dst, hf) if n == 0 else half(mt[:, n - 1, :], hf)
                    ins = dve.tensor_tensor(o, half(sg[:, i, :], hf), PAIR[pr][:, hf, 0:HALF], ALU.mult)
                    if hf == 0:
                        step(ins)
                ins.then_inc(free[pr], 1)
                dve.wait_ge(free[pr], it * 3 + (C_M + (3 if n == 0 else 4)))
                if n == 0:
                    dve.sem_inc(br_out, 1)
                else:
                    dve.tensor_tensor(dst, dst, mt[:, n - 1, :], ALU.add).then_inc(br_out, 1)
                    dve.wait_ge(br_out, it * 3 + (n + 2))
                if n == 1:
                    mod_columns(dve, it + 8, it + 9)
            step.leave(KD)
        for k in range(KD):
            dve.wait_ge(m_hi, k + 1)
            dve.tensor_tensor(hL[:, k, :], merged[:, k, :], hH[:, k, :], ALU.subtract).then_inc(m_lo, 1)
        dve.wait_ge(w_used, Unit(U_M, 16, KD - 1, 15).used)
        step(dve.memset(sacc, 0.0))
        with dve.Fori(0, 8) as it:
            step.enter(it, 4)
            for l in range(4):
                lead(U_O, 4, it, l)
                if l % 2:
                    dve.wait_ge(free[l // 2], it + (C_O + 2))
                    src = mixT[:, bass.ds(it * 2 + l // 2, 1), :].rearrange("p k t -> p (k t)")
                    step(dve.tensor_tensor(sqc[:, 0, :], src, src, ALU.mult))
                    step.settle()
                    step(dve.tensor_tensor(sacc, sacc, sqc[:, 0, :], ALU.add))
                    step.settle()
            step.leave(8)
        dve.sem_inc(sacc_done, 1)
        coefficients(dve, step, 1, 2, False)
        dve.wait_ge(rt2, 1)
        step(dve.reciprocal(rbn, rbn))
        step.settle()
        dve.wait_ge(x_back, 16)
        residual(dve, step, mixT, rbn, xR, x1_done)
        dve.wait_ge(x1_done, KD)
        coefficients(dve, step, 2, 4, True)
        dve.sem_inc(h2_pre, 1)
        dve.wait_ge(rt2, 2)
        step(dve.reciprocal(rbn, rbn))
        step.settle()
        for k in range(KD):
            step(dve.tensor_tensor(mixT[:, k, :], xR[:, k, :], rbn, ALU.mult))
        step.settle()
        modulate(dve, step, mixT, 2, 4, 3, h2_pre, h2_hi, h2_lo, 2)
        dve.wait_ge(h2_lo, KD)
        step(dve.memset(acc, 0.0))
        step.settle()

        def states(rnd):
            dve.wait_ge(st_tr, rnd + 1)
            ins = dve.tensor_copy(st_f, BO[:, 0:128].rearrange("p (v k b r) -> p v k b r", v=2, k=4, b=NS))
            ins.then_inc(st_out, 1)
            dve.wait_ge(st_out, rnd + 1)

        def tails(rnd4, p):
            dve.wait_ge(tail_tr, rnd4 + 2)
            dve.wait_ge(tail_free, TAILS_FREE(rnd4, p))
            ins = dve.tensor_copy(trow[:, :, p * P:(p + 1) * P], BA[0:10, 0:256].rearrange("p (v n) -> p v n", v=2))
            ins.then_inc(tail_out, 1)

        def convolve(base, per, it, l0, rnd4, p, after={}):
            for l in range(4):
                lead(base, per, it, l0 + l)
                if l in after:
                    after[l]()
                if l % 2:
                    v = l // 2
                    st = lambda r: st_f[:, v, p, :, r]
                    stt = lambda o, x_, w_: dve.scalar_tensor_tensor(out=o, in0=x_, scalar=w_, in1=o, op0=ALU.mult, op1=ALU.add)
                    dve.wait_ge(us_c, rnd4 * 2 + (v + 1))
                    step(stt(cv[:, v, 1:TP], us[:, v, 0:TP - 1], tap(1, v, rnd4)))
                    step(stt(cv[:, v, SA], st(1), tap(1, v, rnd4)))
                    step.settle()
                    step(stt(cv[:, v, 2:TP], us[:, v, 0:TP - 2], tap(0, v, rnd4)))
                    stt(cv[:, v, SA], st(0), tap(0, v, rnd4)).then_inc(cv_done, 1)
            dve.wait_ge(gelu_done, rnd4 + 1)
            dve.wait_ge(cv_done, rnd4 * 2 + 4)
            step.settle()
            dve.wait_ge(f_hi, rnd4 + 1)
            dve.tensor_tensor(ft, cv[:, 0, :], cv[:, 1, :], ALU.mult).then_inc(f_done, 1)

        def f_lo_part(rnd4, p):
            dve.wait_ge(f_hi, rnd4 + 2)
            dve.tensor_tensor(fL[:, p, :], ft, fH[:, p, :], ALU.subtract).then_inc(f_lo, 1)

        def accumulate(rnd, l, done, between):
            for i in range(2):
                m = 2 * l + i
                if i == 0:
                    dve.wait_ge(down_mm, rnd * 8 + (l + 1))
                else:
                    dve.wait_ge(w_used, done)
                for hf, bank in enumerate(((BA, BT), (BS, BO))[i]):
                    o = half(acc[:, m, :], hf)
                    dve.tensor_tensor(o, o, bank[:, 0:HALF], ALU.add).then_inc(down_out, 1)
                if i == 0 and between:
                    between()

        dve.wait_ge(x1_st, 16)
        states(0)
        for p in range(FPR):
            convolve(U_F0, 16, 0, 4 * p, p, p, {0: lambda: tails(p - 1, p - 1)} if p else {})
            f_lo_part(p, p)
        with dve.Fori(0, 10) as it:
            step.enter(it, 24)
            r4 = it * 4 + 4
            convolve(U_F, 24, it, 0, r4, 0, {0: lambda: tails(it * 4 + 3, 3), 1: lambda: states(it + 1)})
            for l in range(8):
                accumulate(it, l, Unit(U_F, 24, it, 4 + l).used, lambda: lead(U_F, 24, it, 4 + l))
            f_lo_part(r4, 0)
            for p in range(1, FPR):
                convolve(U_F, 24, it, 8 + 4 * p, r4 + p, p, {0: lambda: tails(r4 + (p - 1), p - 1)})
                f_lo_part(r4 + p, p)
            step.leave(10)
        tails(4 * ROUNDS - 1, 3)
        for l in range(8):
            accumulate(ROUNDS - 1, l, Unit(U_END, 8, 0, l).used, (lambda: lead(U_END, 8, 0, l)) if l < 6 else None)
        coefficients(dve, step, 3, 5, False)
        dve.wait_ge(rt3, 1)
        step(dve.reciprocal(rbf, rbf))
        step.settle()
        dve.wait_ge(x1_back, 16)
        dve.wait_ge(down_out, 2 * ROUNDS * KD + 4)
        residual(dve, step, acc, rbf, x1, y_done)
        for n in range(17):
            dve.wait_ge(y_tr, n + 1)
            bank = (BA, BT, BS, BO)[n % 4] if n < 16 else None
            if n < 16:
                b, q = n // 4, n % 4
                if b >= 2:
                    dve.wait_ge(y_st[b % 2], 16)
                dve.tensor_copy(yN[:, b % 2, q * 512:(q + 1) * 512], bank).then_inc(y_nat, 1)
            else:
                for q in range(4):
                    src = (X[0:NS, 0, :], X[0:NS, 1, :], Y[0:NS, 0, :], Y[0:NS, 1, :])[q]
                    dve.tensor_copy(yNs[:, q * 512:(q + 1) * 512], src).then_inc(y_nat, 1)

    TAILS_FREE = lambda rnd4, p: (rnd4 - p) + 4

    def mod_columns(dve, tile, n):
        dve.wait_ge(mod_tr, n + 1)
        dst = mods[:, bass.ds(tile * 4, 4), :]
        dve.tensor_copy(dst, BT[:, 0:36].rearrange("p (k n) -> p k n", n=9)).then_inc(mod_out, 1)

    def coefficients(dve, step, norm, mod, plus_one):
        gcol = cols[:, norm * KD:(norm + 1) * KD].unsqueeze(2).to_broadcast([P, KD, 9])
        step(dve.scalar_tensor_tensor(out=coef, in0=mods[:, mod * KD:(mod + 1) * KD, :], scalar=1.0 if plus_one else 0.0,
                                      in1=gcol, op0=ALU.add, op1=ALU.mult))
        step.settle()

    def modulate(dve, step, x, norm, scale, shift, pre, hi_, lo_, extra):
        if extra == 1:
            coefficients(dve, step, norm, scale, True)
        sh = mods[:, shift * KD:(shift + 1) * KD, :]
        step(dve.tensor_tensor(x[:, :, SA], x[:, :, SA], coef[:, :, 1:9], ALU.mult))
        step.settle()
        step(dve.tensor_tensor(x[:, :, SA], x[:, :, SA], sh[:, :, 1:9], ALU.add))
        step.settle()
        for k in range(KD + 1):
            if k < KD:
                dve.tensor_scalar(x[:, k, PR], x[:, k, PR], coef[:, k, 0:1], sh[:, k, 0:1], ALU.mult, ALU.add).then_inc(pre, 1)
            if k:
                dve.wait_ge(hi_, k)
                dve.tensor_tensor(hL[:, k - 1, :], x[:, k - 1, :], hH[:, k - 1, :], ALU.subtract).then_inc(lo_, 1)

    def residual(dve, step, f, root, x, done):
        for k in range(KD):
            step(dve.tensor_tensor(f[:, k, :], f[:, k, :], root, ALU.mult))
        step.settle()
        step(dve.tensor_tensor(f[:, :, SA], f[:, :, SA], coef[:, :, 1:9], ALU.mult))
        step.settle()
        step(dve.tensor_tensor(x[:, :, SA], x[:, :, SA], f[:, :, SA], ALU.add))
        step.settle()
        for k in range(KD):
            dve.scalar_tensor_tensor(out=x[:, k, PR], in0=f[:, k, PR], scalar=coef[:, k, 0:1], in1=x[:, k, PR],
                                     op0=ALU.mult, op1=ALU.add).then_inc(done, 1)

    def tensor_program(pe):
        def three(ps, u, w0, xh, xl, first, last, wn=P):
            h, l = whi[:, u.spl, w0:w0 + wn], wlo[:, u.spl, w0:w0 + wn]
            pe.matmul(ps, h, xh, start=first, stop=False)
            pe.matmul(ps, h, xl, start=False, stop=False)
            return pe.matmul(ps, l, xh, start=False, stop=last)

        def ready(u):
            pe.wait_ge(w_lo, u.lo_done)

        def chunk(base, per, it, l0, pair, fr, before, between=None, split=None):
            pe.wait_ge(fr, before + 1)
            for l in range(2):
                u = Unit(base, per, it, l0 + l)
                ready(u)
                for hf in range(2):
                    for k in range(8):
                        kk = 8 * l + k
                        if split is not None and hf == 0:
                            pe.wait_ge(split, kk + 1)
                        m = three(pair[:, hf, 0:HALF], u, k * P, half(hH[:, kk, :], hf), half(hL[:, kk, :], hf),
                                  kk == 0, kk == 15)
                m.then_inc(w_used, 1)
                if l == 0 and between:
                    between()

        def ada(base, per, it, l0, n):
            pe.wait_ge(mod_row, n + 1)
            for l in range(8):
                u = Unit(base, per, it, l0 + l)
                ready(u)
                for k in range(2):
                    for part in (whi, wlo):
                        kk = 2 * l + k
                        m = pe.matmul(BA[0:18, :], cT[:, kk, :], part[:, u.spl, k * 512:(k + 1) * 512],
                                      start=(kk == 0 and part is whi), stop=(kk == 15 and part is wlo))
                m.then_inc(w_used, 1)

        def turn_mods(n):
            pe.wait_ge(mod_row, n + 2)
            pe.wait_ge(mod_bias, n * 16 + 16)
            pe.wait_ge(mod_out, n + 1)
            for i in range(4):
                m = pe.matmul(BT[:, 9 * i:9 * i + 9], mod_rows[:, i * P:(i + 1) * P], sel, start=True, stop=True)
            m.then_inc(mod_tr, 1)

        pe.wait_ge(c_split, 1)
        for k in range(KD):
            m = pe.transpose(BA[:, 9 * k:9 * k + 9], cc[:, k * P:(k + 1) * P], ident[0:9, 0:9])
        m.then_inc(c_tr, 1)
        pe.wait_ge(row_in, 16 * 6)
        pe.transpose(BT[:, 0:80], rows1, ident[0:80, 0:80])
        for t in range(3):
            pe.transpose(BS[:, 88 * t:88 * t + 88], rowsF[:, t, :], ident[0:88, 0:88])
        for k in range(4):
            pe.transpose(BO[:, 16 * k:16 * k + 16], rowsC[:, k * P:(k + 1) * P], ident[0:16, 0:16])
        for k in range(4):
            m = pe.transpose(X[:, 0, 120 * k:120 * k + 120], rowsP[:, k * P:(k + 1) * P], ident[0:120, 0:120])
        m.then_inc(par_tr, 1)
        pe.wait_ge(bias_in, 32)
        pe.wait_ge(par_out, 4)
        pe.wait_ge(c_split, 2)
        for i, (g, n0, n1) in enumerate(BIAS_MM):
            pe.matmul(BIAS_BANK[i][0:HG, 0:n1 - n0], relb[:, 4 * g:4 * g + 4], onehot[:, g, n0:n1],
                      start=True, stop=True).then_inc(b_mm, 1)
        pe.wait_ge(x_in, 16 * 5)
        pe.wait_ge(b_out, 6)
        for n in range(16):
            bank = (X[:, 1, :], BT, BS, X[:, 0, :])[n % 4]
            b, q = n // 4, n % 4
            if n >= 4:
                pe.wait_ge(x_out, n - 3)
            for i in range(4):
                k = 4 * q + i
                m = pe.transpose(bank[:, i * P:(i + 1) * P], xN[:, b, k * P:(k + 1) * P], ident)
            m.then_inc(x_tr, 1)
        for k in range(KD):
            m = pe.transpose(BO[:, NS * k:NS * k + NS], xs[:, k * P:(k + 1) * P], ident[0:NS, 0:NS])
        m.then_inc(x_tr, 1)
        pe.wait_ge(diag_done, 1)
        pe.wait_ge(x_out, 17)
        for b in range(NB):
            pe.matmul(X[:, 0, b * P:(b + 1) * P], ones, diag[:, b, :], start=True, stop=True)
        pe.matmul(X[:, 1, 0:NS], ones[0:NS, :], diag[0:NS, 4, 0:NS], start=True, stop=True).then_inc(rb_mm, 1)
        pe.wait_ge(k_in, 48)
        with pe.Fori(0, 8) as it:
            ada(U_ADA, 8, it, 0, it)
            turn_mods(it)
        pe.wait_ge(rb_done, 2)
        for part in range(3):
            def turn(it, i):
                c = it * 2 + (i + 6 * part)
                pe.wait_ge(free[i], it + (3 * part + 2))
                pe.wait_ge(nat_out, c + 1)
                if part:
                    for b in range(NB):
                        pe.transpose((BT, BS)[i][:, b * P:(b + 1) * P], stage[:, i, b * P:(b + 1) * P], ident)
                pe.transpose((BO, BA)[i][0:NS, 0:P], stage[:, i, SA], ident).then_inc(nat_tr, 1)

            with pe.Fori(0, 3) as it:
                base = U_QKV + 12 * part
                chunk(base, 4, it, 0, X, x_free, it + (C_QKV + 3 * part), split=h_lo if part == 0 else None)
                chunk(base, 4, it, 2, Y, y_free, it + (C_QKV + 3 * part), between=lambda: turn(it, 0))
                turn(it, 1)
        pe.wait_ge(nat_out, 3 * QCH + 2)
        with pe.Fori(0, 2) as it:
            def turn_outputs(qb):
                pe.wait_ge(o_out, it * 8 + (2 * qb + 3))
                pe.transpose(BO[:, P:2 * P], osb.rearrange("p h e -> p (h e)"), ident).then_inc(oT_tr, 1)

            for c in range(8):
                h, qb = c % 2, c // 2
                m = it * 8 + c
                lo_kb = (max(qb - 1, 0), 0, 0)
                pe.wait_ge(q2_in, m + 1)
                pe.wait_ge(p_out, m + 1)
                for g, bank in enumerate((BT, BS, BA)):
                    keys = qk[:, bass.ds(it + (QCH + 2 * g), 1), lo_kb[g] * P:(qb + 1) * P].rearrange("p k t -> p (k t)")
                    ins = pe.matmul(bank[:, 0:(qb + 1 - lo_kb[g]) * P], q2[:, h, g, :], keys, start=True, stop=True)
                ins.then_inc(s_mm, 1)
                if c and c % 2 == 0:
                    turn_outputs(qb - 1)

                blocks = [(g, kb) for g in range(G) for kb in range(lo_kb[g], qb + 1)]

                def turn_probs():
                    pe.wait_ge(s_exp, m + 1)
                    for n in range(len(blocks)):
                        t = pe.transpose((BT, BS, BA)[n // 4][:, n % 4 * P:(n % 4 + 1) * P], sc_p[:, n * P:(n + 1) * P], ident)
                    t.then_inc(p_tr, 1)

                chunk(U_PC, 16, it, 2 * c, PAIR[c % 2], free[c % 2], it * 4 + (C_PC + c // 2), between=turn_probs)
                pe.wait_ge(p_out, m + 2)
                pe.wait_ge(o_out, m + 1)
                if qb:
                    pe.wait_ge(oT_out, it * 4 + qb)
                for n, (g, kb) in enumerate(blocks):
                    v = vn[:, g, kb, :].rearrange("p (j n) -> p j n", j=2)[:, bass.ds(it, 1), h * DH:(h + 1) * DH]
                    t = pe.matmul(BO[:, 0:DH], pT_t[:, n, :], v.rearrange("p j n -> p (j n)"), start=(n == 0), stop=(n == len(blocks) - 1))
                t.then_inc(o_mm, 1)
            turn_outputs(NB - 1)
        pe.wait_ge(ks_used, 10)
        pe.wait_ge(p_out, 17)
        pe.wait_ge(oT_out, 8)
        for h in range(HG):
            for g in range(G):
                n = h * G + g
                t = pe.transpose((BT, BS, BA)[n // 4][0:NS, n % 4 * P:(n % 4 + 1) * P], sc_s[:, :, g * HG + h], ident)
        t.then_inc(ss_tr, 1)
        pe.wait_ge(ss_norm, 1)
        for n in range(12):
            t = pe.transpose(BT[:, n * NS:(n + 1) * NS], ss[:, n // G, n % G, 0:NK], ident[0:NS, 0:NS])
        t.then_inc(pts_tr, 1)
        pe.wait_ge(nv_out, 1)
        pe.wait_ge(pts_out, 1)

        def gather(b):
            pe.wait_ge(vs_out, b + 1)
            for c in range(2):
                t = pe.matmul(BO[:, c * NS + b:c * NS + b + 1], mk[:, b % 2, c * P:(c + 1) * P], ones[0:HG, 0:1],
                              start=False, stop=(b == NS - 1 and c == 1), skip_group_check=True)
            return t

        for c in range(2):
            pe.matmul(BO[:, c * NS:(c + 1) * NS], nv8[:, c * P:(c + 1) * P], ident[0:NS, 0:NS],
                      start=(c == 0), stop=False, skip_group_check=True)
        for b in range(NS):
            pe.wait_ge(vs_in[b % 2], 48 * (b // 2 + 1))
            if b >= 2:
                gather(b - 2)
            for g in range(G):
                t = pe.matmul((BS, BA)[b % 2][0:HG, 0:256], pTs[:, g, b, :], v_s[:, b % 2, g * 256:(g + 1) * 256],
                              start=(g == 0), stop=(g == G - 1))
            t.then_inc(vs_mm, 1)
        gather(NS - 2)
        gather(NS - 1).then_inc(oTs_mm, 1)
        pe.wait_ge(x_free, C_M + 1)
        pe.wait_ge(y_free, C_M + 1)
        for k in range(4):
            pe.transpose(X[0:23, 0, k * P:(k + 1) * P], pT[:, k, TP - 15:T], ident)
        for k in range(4):
            t = pe.transpose(X[0:10, 1, k * P:(k + 1) * P], utail[:, k, :], ident)
        t.then_inc(ptail_tr, 1)
        pe.wait_ge(grp_in, 16)
        pe.wait_ge(ptail_out, 2)
        for i in range(4):
            pe.wait_ge(pool_done, i + 1)
            if i >= 2:
                pe.wait_ge(grp_out, i - 1)
            for hf in range(2):
                t = pe.matmul(PAIR[i % 2][:, hf, 0:HALF], w_grp[:, i, :], half(pT[:, i, :], hf), start=True, stop=True)
            t.then_inc(grp_mm, 1)
        pe.wait_ge(grp_out, 4)
        with pe.Fori(0, KD) as it:
            chunk(U_M, 16, it, 0, X, x_free, it * 3 + C_M)
            chunk(U_M, 16, it, 2, Y, y_free, it * 3 + C_M)
            chunk(U_M, 16, it, 4, X, x_free, it * 3 + (C_M + 1))
            ada(U_M, 16, it, 6, it + 8)
            pe.wait_ge(b_lo, 10)

            def branch(u, pair, fr, before, w0, k0, n):
                pe.wait_ge(fr, before + 1)
                for hf in range(2):
                    for k in range(n):
                        t = three(pair[:, hf, 0:HALF], u, (w0 + k) * P, half(bH[:, k0 + k, :], hf), half(bL[:, k0 + k, :], hf),
                                  k == 0, k == n - 1)
                return t

            u = Unit(U_M, 16, it, 14)
            ready(u)
            branch(u, Y, y_free, it * 3 + (C_M + 1), 0, 0, 4).then_inc(br_mm, 1)
            branch(u, X, x_free, it * 3 + (C_M + 2), 4, 4, 2).then_inc(w_used, 1)
            turn_mods(it + 8)
            u = Unit(U_M, 16, it, 15)
            ready(u)
            branch(u, Y, y_free, it * 3 + (C_M + 2), 0, 6, 4).then_inc(w_used, 1)
        with pe.Fori(0, 8) as it:
            chunk(U_O, 4, it, 0, X, x_free, it + C_O, split=m_lo)
            chunk(U_O, 4, it, 2, Y, y_free, it + C_O)

        def column_sums(src, done, last=True, first=True):
            for hf in range(2):
                t = pe.matmul(X[:, hf, 0:HALF], ones, half(src, hf), start=first, stop=last, skip_group_check=True)
            t.then_inc(done, 1)

        pe.wait_ge(sacc_done, 1)
        pe.wait_ge(x_free, C_F0 + 1)
        column_sums(sacc, rbn_mm)
        pe.wait_ge(rt2, 1)
        for k in range(KD):
            pe.wait_ge(sq_in, k + 1)
            column_sums(sqc[:, k % 2, :], sq_mm, k == KD - 1, k == 0)
        pe.wait_ge(rt2, 2)

        def states(rnd):
            pe.wait_ge(st_in, rnd * 32 + 32)
            pe.sem_inc(st_seen, 1)
            for v in range(2):
                for k in range(4):
                    n = (v * 4 + k) * 16
                    t = pe.transpose(BO[:, n:n + 16], st_rows[:, v, k * P:(k + 1) * P], ident[0:16, 0:16])
            t.then_inc(st_tr, 1)

        def tails(rnd4):
            pe.wait_ge(us_c, rnd4 * 2 + 2)
            pe.wait_ge(tail_out, rnd4 + 1)
            for v in range(2):
                t = pe.transpose(BA[0:10, v * P:(v + 1) * P], us[:, v, TP - 2:T], ident)
            t.then_inc(tail_tr, 1)

        def up(base, per, it, l0, rnd4, split=None, gate_between=None, val_between=None):
            chunk(base, per, it, l0, X, x_free, CF(rnd4), between=gate_between, split=split)
            chunk(base, per, it, l0 + 2, Y, y_free, CF(rnd4), between=val_between)

        def down(base, per, it, l0, rnd):
            pe.wait_ge(f_lo, rnd * 4 + 4)
            for l in range(8):
                u = Unit(base, per, it, l0 + l)
                ready(u)
                for i in range(2):
                    pe.wait_ge(down_out, (rnd * KD) * 2 + (2 * (2 * l + i) + 2))
                    for hf, bank in enumerate(((BA, BT), (BS, BO))[i]):
                        for k in range(FPR):
                            t = three(bank[:, 0:HALF], u, (2 * k + i) * P, half(fH[:, k, :], hf), half(fL[:, k, :], hf),
                                      k == 0, k == FPR - 1)
                    t.then_inc(w_used if i else down_mm, 1)

        states(0)
        for p in range(FPR):
            up(U_F0, 16, 0, 4 * p, p, split=None if p else h2_lo, gate_between=(lambda: tails(p - 1)) if p else None)
        with pe.Fori(0, 10) as it:
            r4 = it * 4 + 4

            def next_states():
                pe.wait_ge(st_out, it + 1)
                states(it + 1)

            up(U_F, 24, it, 0, r4, gate_between=lambda: tails(it * 4 + 3), val_between=next_states)
            pe.wait_ge(tail_out, it * 4 + 5)
            pe.wait_ge(st_out, it + 2)
            down(U_F, 24, it, 4, it)
            pe.wait_ge(down_out, it * (2 * KD) + (2 * KD + 4))
            for p in range(1, FPR):
                up(U_F, 24, it, 8 + 4 * p, r4 + p, gate_between=lambda: tails(r4 + (p - 1)))
        tails(4 * ROUNDS - 1)
        pe.wait_ge(tail_out, 4 * ROUNDS + 1)
        down(U_END, 8, 0, 0, ROUNDS - 1)
        pe.wait_ge(x_free, C_F + 40 + 1)
        for k in range(KD):
            pe.wait_ge(sqf_in, k + 1)
            column_sums(sqf[:, k % 2, :], sqf_mm, k == KD - 1, k == 0)
        pe.wait_ge(y_done, KD)
        pe.wait_ge(rt3, 1)
        pe.wait_ge(down_out, 2 * ROUNDS * KD + 4)
        for n in range(16):
            b, q = n // 4, n % 4
            if n >= 4:
                pe.wait_ge(y_nat, n - 3)
            for i in range(4):
                t = pe.transpose((BA, BT, BS, BO)[n % 4][:, i * P:(i + 1) * P], x1[:, 4 * q + i, b * P:(b + 1) * P], ident)
            t.then_inc(y_tr, 1)
        for q in range(4):
            for i in range(4):
                bank = (X[:, 0, :], X[:, 1, :], Y[:, 0, :], Y[:, 1, :])[q]
                t = pe.transpose(bank[0:NS, i * P:(i + 1) * P], x1[:, 4 * q + i, SA], ident)
        t.then_inc(y_tr, 1)

    with nc.Block() as block:
        block.sync(sync_program)
        block.gpsimd(pool_program)
        block.scalar(scalar_program)
        block.vector(vector_program)
        block.tensor(tensor_program)


INS = ["x_prompt", "x_sample", "c_prompt", "c_sample", "cache_kv_w128", "cache_kv_w512", "cache_kv_w2048",
       "state_pool", "state_conv", "state_ffn_conv", "rel_bias", "norm_g", "w_ada", "b_ada", "w_in", "w_attn_br",
       "w_pool_grp", "pool_scale", "w_pool_br", "conv_w", "w_conv_br", "w_o", "w_up", "ffn_conv_w", "w_down"]
OUTS = [("y_p", (1, TP, D)), ("y_s", (NS, 1, D)),
        ("kv128_p", (1, 1, 128, 2, HG, DH)), ("kv512_p", (1, 1, 512, 2, HG, DH)), ("kv2048_p", (1, 1, 512, 2, HG, DH)),
        ("pool_p", (1, 1, 15, PW)), ("conv_p", (1, 1, 2, CC)), ("ffn_p", (1, 1, 2, 2 * DFF)),
        ("kv128_s", (1, NS, 1, 2, HG, DH)), ("kv512_s", (1, NS, 1, 2, HG, DH)), ("kv2048_s", (1, NS, 1, 2, HG, DH)),
        ("pool_s", (1, NS, 15, PW)), ("conv_s", (1, NS, 2, CC)), ("ffn_s", (1, NS, 2, 2 * DFF))]


def kernel(**inputs):
    import concourse.bacc as bacc
    from concourse.bass_utils import run_bass_kernel_spmd

    nc = bacc.Bacc("TRN2", target_bir_lowering=False, num_devices=1, dynamic_dma_scratch_size=4096)
    arrays, ins, outs = {}, {}, {}
    for name, x in [(n, inputs[n]) for n in INS] + list(constants().items()):
        x = np.ascontiguousarray(x)
        arrays[f"in_{name}"] = x
        ins[name] = nc.dram_tensor(f"in_{name}", x.shape, mybir.dt.from_np(x.dtype), kind="ExternalInput").ap()
    for name, shape in OUTS:
        outs[name] = nc.dram_tensor(f"out_{name}", shape, F32, kind="ExternalOutput").ap()
    layer(nc, ins, outs)
    r = run_bass_kernel_spmd(nc, [arrays], core_ids=[0])
    return tuple(r.results[0][f"out_{name}"] for name, _ in OUTS)
```

```python
import math
import numpy as np
import concourse.bass as bass
from concourse import mybir

F32 = mybir.dt.float32
F32R = mybir.dt.float32r
ALU = mybir.AluOpType
ACT = mybir.ActivationFunctionType
AX = mybir.AxisListType
P = 128

D = 2048
KD = D // P
TP, NS = 512, 8
T = TP + NS
HALF = T // 2
NB = TP // P
G, HG, DH = 3, 4, 64
DIL = (1, 4, 16)
NK = 128
AW = G * HG * DH
QCH = AW // P
PW, CC = 512, 512
WIN = (2, 4, 8, 16)
DFF = 5632
FCH = DFF // P
ROUNDS, FPR = FCH // 4, 4
SCALE = DH ** -0.5
EPS = 1e-6
NEG = -1e30
RW = 5 * P
BW = RW + NK + 1
COL_P, COL_B, COL_C, COL_H, COL_G = 3 * AW, 3 * AW + PW, 3 * AW + PW + CC, 3 * AW + PW + 2 * CC, 3 * AW + PW + 3 * CC
PR, SA = slice(0, TP), slice(TP, T)
RAW = 4
SPLIT = (2, 4)
UNIT = 8 * P

U_ADA, N_ADA = 0, 8
U_QKV = U_ADA + 8 * N_ADA
U_PC = U_QKV + 9 * 4
U_M = U_PC + 2 * 16
U_O = U_M + 16 * 16
U_F0 = U_O + 8 * 4
U_F = U_F0 + 16
U_END = U_F + 10 * 24
UNITS = U_END + 8
M_GATE, M_ADA, M_BR, M_CONV = (0, 2, 4, 7, 9, 11), (1, 3, 5, 6, 8, 10, 12, 14), 13, 15
C_QKV, C_PC, C_M, C_O, C_F0, C_F = 0, 9, 17, 65, 73, 77


def constants():
    n = np.arange(NK + 1)
    onehot = np.zeros((33, G, BW), np.float32)
    for g, d in enumerate(DIL):
        dist = n * d
        large = 16 + (np.log(np.maximum(dist, 1) / 16) / math.log(2048 / 16) * 16).astype(np.int32)
        bucket = np.where(dist < 16, dist, np.minimum(large, 31))
        for y in range(RW):
            delta = TP - 1 - y
            if delta >= 0 and delta % d == 0 and delta // d <= NK:
                onehot[bucket[delta // d], g, y] = 1
            else:
                onehot[32, g, y] = NEG
        for i in range(NK + 1):
            onehot[bucket[NK - i if i < NK else 0], g, RW + i] = 1
    sel = np.zeros((19, 9), np.float32)
    for i in range(9):
        sel[i, i] = sel[9 + i, i] = 1
    sel[18] = 1
    heads = np.zeros((HG, HG * DH), np.float32)
    for h in range(HG):
        heads[h, h * DH:(h + 1) * DH] = 1
    counts = np.zeros((P, 4, 16), np.float32)
    for i, w in enumerate(WIN):
        counts[:, i] = (1.0 / np.minimum(np.arange(16) + 1, w)).astype(np.float32)
    return {"ident": np.eye(P, dtype=np.float32), "onehot": onehot, "sel": sel, "heads": heads, "counts": counts}


class Step:

    def __init__(self, eng, sem):
        self.eng, self.sem, self.base, self.it, self.per, self.k = eng, sem, 0, 0, 0, 0

    def enter(self, it, per):
        self.base, self.it, self.per, self.k = self.base + self.k, it, per, 0

    def leave(self, times):
        assert self.k == self.per, ("steps of the loop's body", self.k)
        self.base, self.it, self.per, self.k = self.base + self.per * times, 0, 0, 0

    def __call__(self, ins):
        ins.then_inc(self.sem, 1)
        self.k += 1

    def settle(self, but=0):
        self.eng.wait_ge(self.sem, self.it * self.per + (self.base + self.k - but))


class Unit:

    def __init__(self, base, per, it, l):
        self.n = it * per + (base + l)
        self.raw = (base + l) % RAW
        self.ring = SPLIT[base >= U_M]
        self.spl = (base + l) % self.ring
        self.turn = it * (per // RAW) + (base + l) // RAW

    raw_free = property(lambda s: s.n + 1)
    arrived = property(lambda s: s.turn * 16 + 16)
    spl_free = property(lambda s: s.n + 3 - s.ring)
    hi_done = property(lambda s: s.n + 1)
    lo_done = property(lambda s: s.n + 5)
    used = property(lambda s: s.n + 3)


def layer(nc, a, out):
    at = {"top": -(-nc.sbuf_base // 32) * 32}

    def place(name, shape, dt=F32, off=None):
        size = int(np.prod(shape[1:])) * 4
        o = at["top"] if off is None else off
        if off is None:
            at["top"] += -(-size // 32) * 32
        return nc.alloc_sbuf_tensor_at(name, shape, dt, offset=o).ap()

    def region(start, *items):
        o, made = start, []
        for name, shape, dt in items:
            made.append(place(name, shape, dt, off=o))
            o += -(-int(np.prod(shape[1:])) * 4 // 32) * 32
        return made, o

    ident = place("ident", [P, P])
    ones = place("ones", [P, P])
    sel = place("sel", [19, 9])
    heads_mask = place("heads_mask", [HG, HG * DH])
    counts = place("counts", [P, 4, 16])
    eps = place("eps", [P, 1])
    cols = place("cols", [P, 80])
    ffn_w = place("ffn_w", [P, 3, 2 * FCH])
    st_conv = place("st_conv", [P, 4, NS, 2])
    st_pool = place("st_pool", [P, 4, NS, 15])
    mods = place("mods", [P, 6 * KD, 9])
    coef = place("coef", [P, KD, 9])
    cT = place("cT", [P, KD, 18], F32R)
    mod_rows = place("mod_rows", [19, 512])
    raw = place("raw", [P, RAW, UNIT])
    whi, wlo = ([place(f"{n}{i}", [P, UNIT], F32R) for i in range(2)] for n in ("whi", "wlo"))
    H0 = at["top"]
    hH = place("hH", [P, KD, T], F32R)
    hL = place("hL", [P, KD, T], F32R)
    L0 = at["top"]
    (xN, xs, cc, csig), e = region(H0, ("xN", [P, NB, D], F32), ("xs", [NS, D], F32), ("cc", [9, D], F32), ("csig", [9, D], F32))
    assert e <= L0
    (xT, xr, rb, rows1, rowsF, rowsC, rowsP, relb, onehot, brows, sqj, ssq, rs, diag), end0 = region(
        L0, ("xT", [P, KD, T], F32), ("xr", [P, KD, T], F32), ("rb", [P, T], F32),
        ("rows1", [80, P], F32), ("rowsF", [88, 3, P], F32), ("rowsC", [16, CC], F32), ("rowsP", [120, PW], F32),
        ("relb", [33, 12], F32), ("onehot_s", [33, G, BW], F32), ("brows", [HG, G, BW], F32),
        ("sqj", [P, D], F32), ("ssq", [P, 5], F32), ("rs", [P, 5], F32), ("diag", [P, 5, P], F32))
    (ns, vn, qk, stage, qB), e1 = region(
        L0, ("ns", [NS, 3 * AW], F32), ("vn", [P, G, NB, 256], F32),
        ("qk", [P, 2 * QCH, TP], F32), ("stage", [P, 2, T], F32), ("qB", [P, 2, AW], F32))
    (u_bias, sc_p, pT_t, q2, osb), e2 = region(
        e1, ("u_bias", [P, 2, 5 * 256], F32), ("scores", [P, 5 * 256], F32), ("probsT", [P, 10, P], F32),
        ("q2", [P, 2, G, P], F32), ("osb", [P, 2, DH], F32))
    (cS, sc_s, k_s, mx, nm, ls, rl, utail), e3 = region(
        e2, ("cS", [P, T], F32), ("sc_s", [P, NS, 12], F32), ("k_s", [P, 2, AW], F32),
        ("mx", [P, 2], F32), ("nm", [P, 2], F32), ("ls", [P, 2], F32), ("rl", [P, 2], F32), ("utail", [P, 4, 10], F32))
    (pT, bcv, aT), e = region(e3, ("pT", [P, 4, T], F32), ("bcv", [P, 4, T], F32), ("aT", [P, 2, T], F32))
    (kn,), e_ = region(e3 + 4 * T * 4, ("kn", [P, G, NB, 256], F32))
    uS, yS = stage[:, 0, :], stage[:, 1, :]
    LIM = nc.sbuf_usable_end
    assert max(e, e_) <= LIM and end0 <= LIM, (L0, e, e_, end0, LIM)
    (ss, bS, n8, smx, sls, srl, t8, nv8, pTs, mk, w_grp), e = region(
        e1, ("ss", [NS, HG, G, NK + 1], F32), ("bS", [NS, HG * G, NK + 1], F32), ("n8", [NS, 12], F32),
        ("smx", [NS, HG], F32), ("sls", [NS, HG], F32), ("srl", [NS, HG], F32),
        ("t8", [NS, AW], F32), ("nv8", [NS, 256], F32), ("pTs", [P, G, NS, HG], F32), ("mk", [HG, 2, 256], F32),
        ("w_grp", [P, 4, P], F32))
    assert e <= e2, (e, e2)
    v_s = k_s
    (t_tails,), e = region(e1 - 2 * AW * 4, ("t_tails", [23, 2, 512], F32))
    assert e <= e1
    (merged,), e = region(L0, ("merged", [P, KD, T], F32))
    (bH, bL), e = region(e, ("bH", [P, 10, T], F32R), ("bL", [P, 10, T], F32R))
    (sg, mt), eM = region(e, ("sg", [P, 3, T], F32), ("mt", [P, 2, T], F32))
    assert eM <= e3, (eM, e3)
    mixT = merged
    WM = (LIM - 4 * UNIT * 4) // 32 * 32
    more, e = region(WM, *[(f"{n}{i}", [P, UNIT], F32R) for n in ("whi", "wlo") for i in (2, 3)])
    assert eM <= WM and e <= LIM
    whi, wlo = whi + more[:2], wlo + more[2:]
    (xR, sacc, rbn, sqc), eO = region(L0 + KD * T * 4, ("xR", [P, KD, T], F32), ("sacc", [P, T], F32), ("rbn", [P, T], F32), ("sqc", [P, 2, T], F32))
    (acc, fH, fL, us, cv, ft, sqf, rbf, fsum), eF = region(
        L0, ("acc", [P, KD, T], F32), ("fH", [P, FPR, T], F32R), ("fL", [P, FPR, T], F32R),
        ("us", [P, 2, T], F32), ("cv", [P, 2, T], F32), ("ft", [P, T], F32),
        ("sqf", [P, 2, T], F32), ("rbf", [P, T], F32), ("fsum", [P, T], F32))
    assert max(eF, eO) <= WM, (eF, eO, WM)
    (x1, yN), e = region(H0, ("x1", [P, KD, T], F32), ("yN", [P, NB, D], F32))
    (yNs, trow, st_rows, st_f), e_ = region(
        max(eO, eF), ("yNs", [NS, D], F32), ("trow", [10, 2, 512], F32), ("st_rows", [16, 2, 512], F32),
        ("st_f", [P, 2, 4, NS, 2], F32))
    assert e_ <= WM
    assert e <= L0

    X = nc.alloc_psum_tensor("X", [P, 2, 512], F32).ap()
    Y = nc.alloc_psum_tensor("Y", [P, 2, 512], F32).ap()
    BA = nc.alloc_psum_tensor("BA", [P, 512], F32).ap()
    BT = nc.alloc_psum_tensor("BT", [P, 512], F32).ap()
    BS = nc.alloc_psum_tensor("BS", [P, 512], F32).ap()
    BO = nc.alloc_psum_tensor("BO", [P, 512], F32).ap()
    PAIR = (X, Y)
    half = lambda t, h: t[:, h * HALF:(h + 1) * HALF]

    d_x = nc.dram_tensor("d_x", (P, KD * T), F32, kind="Internal").ap()
    d_x1 = nc.dram_tensor("d_x1", (P, KD * T), F32, kind="Internal").ap()
    d_bias = nc.dram_tensor("d_bias", (HG, G, BW), F32, kind="Internal").ap()
    d_table = nc.dram_tensor("d_table", (HG, P, G, RW), F32, kind="Internal").ap()
    d_q = nc.dram_tensor("d_q", (NS, AW), F32, kind="Internal").ap()

    sems = {}

    def sem(name):
        sems[name] = nc.alloc_semaphore(name)
        return sems[name]

    w_raw = [sem(f"w_raw{i}") for i in range(RAW)]
    w_hi, w_lo, w_used, w_attn = sem("w_hi"), sem("w_lo"), sem("w_used"), sem("w_attn")
    x_free, y_free = sem("x_free"), sem("y_free")
    free = (x_free, y_free)
    act_step, dve_step = sem("act_step"), sem("dve_step")
    c_in, k_in, x_in, row_in, bias_in = sem("c_in"), sem("k_in"), sem("x_in"), sem("row_in"), sem("bias_in")
    set_up, silu, c_tr, c_split = sem("set_up"), sem("silu"), sem("c_tr"), sem("c_split")
    par_tr, par_out, b_mm, b_out = sem("par_tr"), sem("par_out"), sem("b_mm"), sem("b_out")
    x_tr, x_out, ssq_done, diag_done, rb_mm, rb_done = sem("x_tr"), sem("x_out"), sem("ssq_done"), sem("diag_done"), sem("rb_mm"), sem("rb_done")
    rt_done = sem("rt_done")
    mod_mm, mod_row, mod_bias, mod_tr, mod_out = sem("mod_mm"), sem("mod_row"), sem("mod_bias"), sem("mod_tr"), sem("mod_out")
    h_pre, h_hi, h_lo = sem("h_pre"), sem("h_hi"), sem("h_lo")
    bias_st, table_st, xT_st, q_st = sem("bias_st"), sem("table_st"), sem("xT_st"), sem("q_st")
    stage_in, nat_tr, qk_out, nat_out = sem("stage_in"), sem("nat_tr"), sem("qk_out"), sem("nat_out")
    k_st, v_st, out_st = sem("k_st"), sem("v_st"), sem("out_st")
    u_in, q2_in, u_used = sem("u_in"), sem("q2_in"), sem("u_used")
    s_mm, s_soft, s_exp, p_tr, p_out, o_mm, o_out, oT_tr, oT_out = (
        sem(n) for n in ("s_mm", "s_soft", "s_exp", "p_tr", "p_out", "o_mm", "o_out", "oT_tr", "oT_out"))
    c_cp, ks_used = sem("c_cp"), sem("ks_used")
    qB_in, ks_in, vs_in = ([sem(f"{n}{i}") for i in range(2)] for n in ("qB_in", "ks_in", "vs_in"))
    ss_tr, ss_in, ss_max, ss_exp, ss_norm, pts_tr, pts_out, vs_mm, vs_out, nv_out, oTs_mm, oTs_out = (
        sem(n) for n in ("ss_tr", "ss_in", "ss_max", "ss_exp", "ss_norm", "pts_tr", "pts_out", "vs_mm", "vs_out", "nv_out", "oTs_mm", "oTs_out"))
    tail_free = sem("tail_free")
    bS_in, branch_turn, st_seen = sem("bS_in"), sem("branch_turn"), sem("st_seen")
    ptail_tr, ptail_out, pool_done, grp_in, grp_mm, grp_out, b_hi, b_lo = (
        sem(n) for n in ("ptail_tr", "ptail_out", "pool_done", "grp_in", "grp_mm", "grp_out", "b_hi", "b_lo"))
    gate_out, br_mm, br_out = sem("gate_out"), sem("br_mm"), sem("br_out")
    m_hi, m_lo = sem("m_hi"), sem("m_lo")
    mix_out, sacc_done, rbn_mm, rt2, x_back, x1_done, sq_in, sq_mm = (
        sem(n) for n in ("mix_out", "sacc_done", "rbn_mm", "rt2", "x_back", "x1_done", "sq_in", "sq_mm"))
    h2_pre, h2_hi, h2_lo = sem("h2_pre"), sem("h2_hi"), sem("h2_lo")
    st_in, st_tr, st_out, us_in, us_c, cv_done, gelu_done, f_done, f_hi, f_lo = (
        sem(n) for n in ("st_in", "st_tr", "st_out", "us_in", "us_c", "cv_done", "gelu_done", "f_done", "f_hi", "f_lo"))
    tail_tr, tail_out, tail_st, down_mm, down_out = (sem(n) for n in ("tail_tr", "tail_out", "tail_st", "down_mm", "down_out"))
    x1_st, x1_back, sqf_in, sqf_mm, rbf_mm, rt3, y_done, y_tr, y_nat = (
        sem(n) for n in ("x1_st", "x1_back", "sqf_in", "sqf_mm", "rbf_mm", "rt3", "y_done", "y_tr", "y_nat"))
    y_st, sqf_used = sem("y_st"), sem("sqf_used")

    kview = lambda w: w.rearrange("(k p) n -> p k n", p=P)
    w_ada, w_in, w_o, w_up, w_down = (kview(a[n][0]) for n in ("w_ada", "w_in", "w_o", "w_up", "w_down"))
    w_pool_br, w_conv_br, w_attn_br = (kview(a[n][0]) for n in ("w_pool_br", "w_conv_br", "w_attn_br"))

    def sync_program(sp):
        def load(u, dst, src, free=False):
            if not free:
                sp.wait_ge(w_lo, u.raw_free)
            sp.dma_start(dst, src).then_inc(w_raw[u.raw], 16)

        def slab(u, w, k0, col, k=8, width=P, off=0, free=False):
            dst = raw[:, u.raw, off * P:(off + k * width // P) * P].rearrange("p (k n) -> p k n", n=width)
            load(u, dst, w[:, k0:k0 + k, bass.ds(col, width)], free)

        def ada_unit(u, tile, j):
            slab(u, w_ada, 2 * j, tile * 512, k=2, width=512)

        sp.dma_start(ident, a["ident"]).then_inc(c_in, 16)
        sp.dma_start(cc[0:1, :], a["c_prompt"]).then_inc(c_in, 16)
        sp.dma_start(cc[1:9, :], a["c_sample"]).then_inc(c_in, 16)
        with sp.Fori(0, 8) as it:
            for l in range(8):
                ada_unit(Unit(U_ADA, 8, it, l), it, l)
        with sp.Fori(0, 9) as it:
            for l in range(4):
                slab(Unit(U_QKV, 4, it, l), w_in, 8 * (l % 2), it * 256 + l // 2 * P)
        with sp.Fori(0, 2) as it:
            for c, col in enumerate((COL_P, COL_P + P, COL_C, COL_H, COL_B, COL_C + P, COL_H + P, COL_B + P)):
                for l in range(2):
                    slab(Unit(U_PC, 16, it, 2 * c + l), w_in, 8 * l, it * 256 + col)
        with sp.Fori(0, KD) as it:
            for l in range(13):
                if l in M_GATE:
                    slab(Unit(U_M, 16, it, l), w_in, 8 * (M_GATE.index(l) % 2), it * P + (COL_G + M_GATE.index(l) // 2 * D))
                else:
                    ada_unit(Unit(U_M, 16, it, l), it + 8, M_ADA.index(l))
            u = Unit(U_M, 16, it, M_BR)
            sp.wait_ge(w_lo, u.raw_free)
            sp.sem_inc(branch_turn, 1)
            slab(u, w_pool_br, 0, it * P, k=4, free=True)
            sp.dma_start(raw[:, u.raw, 4 * P:6 * P].rearrange("p (k n) -> p k n", n=P),
                         w_attn_br[:, 0:2, bass.ds(it * P, P)]).then_inc(w_attn, 16)
            ada_unit(Unit(U_M, 16, it, 14), it + 8, 7)
            slab(Unit(U_M, 16, it, M_CONV), w_conv_br, 0, it * P, k=4)
        with sp.Fori(0, 8) as it:
            for l in range(4):
                slab(Unit(U_O, 4, it, l), w_o, 8 * (l % 2), it * 256 + l // 2 * P)

        def up(base, per, it, l0, rnd, pair):
            for l in range(4):
                slab(Unit(base, per, it, l0 + l), w_up, 8 * (l % 2), rnd * 512 + (pair * P + l // 2 * DFF))

        def down(base, per, it, l0, rnd):
            rows = a["w_down"][0].rearrange("(r k p) n -> r p k n", p=P, k=FPR)
            for l in range(8):
                u = Unit(base, per, it, l0 + l)
                load(u, raw[:, u.raw, :].rearrange("p (k n) -> p k n", n=256),
                     rows[bass.ds(rnd, 1), :, :, l * 256:(l + 1) * 256].rearrange("r p k n -> (r p) k n"))

        for pair in range(FPR):
            up(U_F0, 16, 0, 4 * pair, 0, pair)
        with sp.Fori(0, 10) as it:
            up(U_F, 24, it, 0, it + 1, 0)
            down(U_F, 24, it, 4, it)
            for pair in range(1, FPR):
                up(U_F, 24, it, 8 + 4 * pair, it + 1, pair)
        down(U_END, 8, 0, 0, ROUNDS - 1)
        for n, (q, b) in enumerate(Y_TILES):
            sp.wait_ge(y_nat, n + 1)
            if b < NB:
                sp.dma_start(out["y_p"][0, b * P:(b + 1) * P, q * 512:(q + 1) * 512],
                             yN[:, b, q * 512:(q + 1) * 512]).then_inc(y_st, 16)
            elif q == 3:
                sp.dma_start(out["y_s"].rearrange("b t n -> (b t) n"), yNs).then_inc(y_st, 16)
        sp.wait_ge(y_st, 16 * (4 * NB + 1))

    def pool_program(gp):
        big = lambda w: w.rearrange("(b p) n -> p b n", p=P)
        gp.dma_start(rows1[0:64, :], a["norm_g"][0].rearrange("n (k p) -> (n k) p", p=P)).then_inc(row_in, 16)
        gp.dma_start(rows1[64:76, :], a["conv_w"][0].rearrange("n (k p) -> (n k) p", p=P)).then_inc(row_in, 16)
        gp.dma_start(rows1[76:80, :], a["pool_scale"][0].rearrange("(k p) -> k p", p=P)).then_inc(row_in, 16)
        gp.dma_start(rowsF, a["ffn_conv_w"][0].rearrange("t (k p) -> k t p", p=P)).then_inc(row_in, 16)
        gp.dma_start(rowsC, a["state_conv"][0].rearrange("b r n -> (b r) n")).then_inc(row_in, 16)
        gp.dma_start(rowsP, a["state_pool"][0].rearrange("b r n -> (b r) n")).then_inc(row_in, 16)
        gp.wait_ge(set_up, 1)
        gp.dma_start(relb[0:32, :], a["rel_bias"]).then_inc(bias_in, 16)
        gp.dma_start(onehot, a["onehot"]).then_inc(bias_in, 16)
        gp.dma_start(sel, a["sel"]).then_inc(k_in, 16)
        gp.dma_start(heads_mask, a["heads"]).then_inc(k_in, 16)
        gp.dma_start(counts, a["counts"]).then_inc(k_in, 16)
        for b in range(NB):
            gp.dma_start(xN[:, b, :], a["x_prompt"][0, b * P:(b + 1) * P, :]).then_inc(x_in, 16)
        gp.dma_start(xs, a["x_sample"].rearrange("b t n -> (b t) n")).then_inc(x_in, 16)
        gp.dma_start(out["pool_s"][0, :, 0:14, :], a["state_pool"][0, :, 1:15, :]).then_inc(out_st, 16)
        gp.dma_start(out["conv_s"][0, :, 0, :], a["state_conv"][0, :, 1, :]).then_inc(out_st, 16)
        gp.dma_start(out["ffn_s"][0, :, 0, :], a["state_ffn_conv"][0, :, 1, :]).then_inc(out_st, 16)
        gp.wait_ge(b_out, 6)
        gp.dma_start(d_bias, brows).then_inc(bias_st, 16)
        gp.wait_ge(bias_st, 16)
        for h in range(HG):
            gp.dma_start(d_table[h], d_bias[h, :, 0:RW].unsqueeze(0).to_broadcast([P, G, RW])).then_inc(table_st, 16)
        gp.wait_ge(x_out, 17)
        gp.dma_start(d_x, xT.rearrange("p k t -> p (k t)")).then_inc(xT_st, 16)

        def mod_bias_row(tile):
            gp.dma_start(mod_rows[18:19, :], a["b_ada"][0:1, bass.ds(tile * 512, 512)]).then_inc(mod_bias, 16)

        mod_bias_row(0)
        with gp.Fori(0, 7) as it:
            gp.wait_ge(mod_tr, it + 2)
            mod_bias_row(it + 1)
        gp.wait_ge(nat_out, QCH + 2)
        gp.dma_start(d_q, ns[:, 0:AW]).then_inc(q_st, 16)
        caches = [a[n] for n in ("cache_kv_w128", "cache_kv_w512", "cache_kv_w2048")]

        def cache_rows(dst, b, kv, done):
            for g in range(G):
                rows = caches[g][0].rearrange("b (i d) v h e -> b i d v (h e)", d=DIL[g])[b, :, 0, kv, :]
                gp.dma_start(dst[:, g * 256:(g + 1) * 256], rows).then_inc(done, 16)

        def bias_tables(pair):
            for h in range(2):
                for g0, n, w, c in ((0, 1, 256, 0), (1, 2, 512, 256)):
                    rows = bass.AP(d_table.tensor, (2 * pair + h) * P * G * RW + g0 * RW + P - 1 + 512 - w,
                                   [[G * RW - 1, P], [RW, n], [1, w]])
                    gp.dma_start(u_bias[:, h, c:c + n * w].rearrange("p (g n) -> p g n", n=w), rows).then_inc(u_in, 16)

        def sample_keys(b):
            gp.dma_start(qB[:, b % 2, :], d_q[b:b + 1, :].to_broadcast([P, AW])).then_inc(qB_in[b % 2], 16)
            cache_rows(k_s[:, b % 2, :], b, 0, ks_in[b % 2])

        gp.wait_ge(table_st, 16 * HG)
        bias_tables(0)
        gp.wait_ge(q_st, 16)
        sample_keys(0)
        sample_keys(1)
        gp.wait_ge(nat_out, 2 * QCH + 2)
        for g, name in enumerate(("kv128_p", "kv512_p", "kv2048_p")):
            store_kv(gp, kn, 0, g, name)
            kv = 0
            gp.dma_start(out[name[:-1] + "s"][0, :, 0, kv, :, :].rearrange("b h d -> b (h d)"),
                         ns[:, AW + g * 256:AW + g * 256 + 256]).then_inc((k_st, v_st)[kv], 16)
        gp.wait_ge(nat_out, 3 * QCH + 2)
        for g, name in enumerate(("kv128_p", "kv512_p", "kv2048_p")):
            store_kv(gp, vn, 1, g, name)
            kv = 1
            gp.dma_start(out[name[:-1] + "s"][0, :, 0, kv, :, :].rearrange("b h d -> b (h d)"),
                         ns[:, 2 * AW + g * 256:2 * AW + g * 256 + 256]).then_inc((k_st, v_st)[kv], 16)
        for b in range(2, NS):
            if b == 4:
                gp.wait_ge(u_used, 2)
                bias_tables(1)
            gp.wait_ge(ks_used, b + 1)
            sample_keys(b)
        gp.wait_ge(u_used, 3)
        gp.wait_ge(oT_out, 8)
        gp.dma_start(bS, d_bias[:, :, RW:BW].rearrange("h g n -> (h g) n").unsqueeze(0).to_broadcast([NS, HG * G, NK + 1])
                     ).then_inc(bS_in, 16)
        gp.dma_start(w_grp, a["w_pool_grp"][0].rearrange("g c e -> c g e")).then_inc(grp_in, 16)
        gp.wait_ge(ks_used, 10)
        for b in range(NS):
            if b >= 2:
                gp.wait_ge(vs_mm, b - 1)
            cache_rows(v_s[:, b % 2, :], b, 1, vs_in[b % 2])
        gp.wait_ge(ptail_out, 2)
        gp.dma_start(out["pool_p"][0, 0], t_tails[0:15, 0, :]).then_inc(out_st, 16)
        gp.dma_start(out["pool_s"][0, :, 14, :], t_tails[15:23, 0, :]).then_inc(out_st, 16)
        gp.dma_start(out["conv_p"][0, 0], t_tails[0:2, 1, :]).then_inc(out_st, 16)
        gp.dma_start(out["conv_s"][0, :, 1, :], t_tails[2:10, 1, :]).then_inc(out_st, 16)
        with gp.Fori(0, KD) as it:
            gp.wait_ge(mod_tr, it + 9)
            mod_bias_row(it + 8)
        gp.wait_ge(xT_st, 16)
        gp.wait_ge(w_used, Unit(U_M, 16, KD - 1, 15).used)
        gp.wait_ge(br_out, 3 * KD + 1)
        gp.dma_start(xR.rearrange("p k t -> p (k t)"), d_x).then_inc(x_back, 16)

        def state_rows(rnd):
            for v in range(2):
                gp.dma_start(st_rows[:, v, :], a["state_ffn_conv"][0, :, :, bass.ds(rnd * 512 + v * DFF, 512)]
                             .rearrange("b r n -> (b r) n")).then_inc(st_in, 16)

        state_rows(0)
        gp.wait_ge(x1_done, KD)
        gp.dma_start(d_x1, xR.rearrange("p k t -> p (k t)")).then_inc(x1_st, 16)
        gp.wait_ge(x1_st, 16)

        def store_tails(rnd):
            for v in range(2):
                col = bass.ds(rnd * 512 + v * DFF, 512)
                gp.dma_start(out["ffn_p"][0, 0, :, col], trow[0:2, v, :]).then_inc(tail_st, 16)
                gp.dma_start(out["ffn_s"][0, :, 1, col], trow[2:10, v, :]).then_inc(tail_st, 16)

        with gp.Fori(0, 10) as it:
            gp.wait_ge(st_tr, it + 1)
            state_rows(it + 1)
            gp.wait_ge(tail_out, it * 4 + 5)
            store_tails(it)
            gp.wait_ge(tail_st, it * 64 + 64)
            gp.sem_inc(tail_free, 4)
        gp.wait_ge(tail_out, 4 * ROUNDS + 1)
        store_tails(ROUNDS - 1)
        gp.wait_ge(w_used, Unit(U_F, 24, 9, 23).used)
        gp.dma_start(x1.rearrange("p k t -> p (k t)"), d_x1).then_inc(x1_back, 16)
        gp.wait_ge(out_st, 16 * 7)
        gp.wait_ge(k_st, 16 * 6)
        gp.wait_ge(v_st, 16 * 6)
        gp.wait_ge(tail_st, 16 * 4 * ROUNDS)

    def store_kv(gp, nat, kv, g, name):
        dst = out[name][0, 0, :, kv, :, :].rearrange("t h d -> t (h d)")
        if g == 0:
            gp.dma_start(dst, nat[:, g, NB - 1, :]).then_inc((k_st, v_st)[kv], 16)
        else:
            gp.dma_start(dst.rearrange("(b p) n -> p b n", p=P), nat[:, g, :, :]).then_inc((k_st, v_st)[kv], 16)

    def scalar_program(act):
        step = Step(act, act_step)

        def hi(u):
            act.wait_ge(w_raw[u.raw], u.arrived)
            act.wait_ge(w_used, u.spl_free)
            nc.scalar.copy(whi[u.spl], raw[:, u.raw, :]).then_inc(w_hi, 1)

        def lead(base, per, it, l):
            hi(Unit(base, per, it, l + 2))

        act.wait_ge(c_in, 48)
        nc.scalar.activation(csig, cc, ACT.Sigmoid).then_inc(silu, 1)
        act.wait_ge(x_in, 16 * 5)
        for b in range(NB):
            nc.scalar.activation(sqj, xN[:, b, :], ACT.Square, accum_out=ssq[:, b:b + 1]).then_inc(ssq_done, 1)
            act.wait_ge(ssq_done, b + 1)
        nc.scalar.activation(sqj[0:NS, :], xs, ACT.Square, accum_out=ssq[0:NS, 4:5]).then_inc(ssq_done, 1)
        act.wait_ge(ssq_done, 5)
        act.wait_ge(set_up, 1)
        nc.scalar.activation(rs[:, 0:4], ssq[:, 0:4], ACT.Sqrt, bias=eps, scale=1.0 / D).then_inc(rt_done, 1)
        nc.scalar.activation(rs[0:NS, 4:5], ssq[0:NS, 4:5], ACT.Sqrt, bias=eps[0:NS], scale=1.0 / D).then_inc(rt_done, 1)
        for i, (g, n0, n1) in enumerate(BIAS_MM):
            act.wait_ge(b_mm, i + 1)
            nc.scalar.copy(brows[:, g, n0:n1], BIAS_BANK[i][0:HG, 0:n1 - n0]).then_inc(b_out, 1)
        act.wait_ge(x_tr, 17)
        act.wait_ge(rb_mm, 1)
        nc.scalar.copy(rb[:, :TP], X[:, 0, :]).then_inc(rb_done, 1)
        nc.scalar.copy(rb[:, TP:], X[:, 1, 0:NS]).then_inc(rb_done, 1)

        for l in range(2):
            hi(Unit(0, 0, 0, l))
        with act.Fori(0, 8) as it:
            for l in range(8):
                lead(U_ADA, 8, it, l)
            act.wait_ge(w_used, Unit(U_ADA, 8, it, 7).used)
            act.wait_ge(mod_tr, it + 1)
            nc.scalar.copy(mod_rows[0:18, :], BA[0:18, :]).then_inc(mod_row, 1)
        for k in range(KD):
            act.wait_ge(h_pre, k + 1)
            nc.scalar.copy(hH[:, k, :], xr[:, k, :]).then_inc(h_hi, 1)
        for part in range(3):
            with act.Fori(0, 3) as it:
                for l in range(4):
                    lead(U_QKV + 12 * part, 4, it, l)
                    if l % 2:
                        c = it * 2 + (l // 2 + 6 * part)
                        act.wait_ge(w_used, Unit(U_QKV + 12 * part, 4, it, l).used)
                        act.wait_ge(nat_tr, c + 1)
                        act.wait_ge(qk_out, c + 1)
                        act.copy(half(stage[:, l // 2, :], 0), PAIR[l // 2][:, 0, 0:HALF])
                        act.copy(half(stage[:, l // 2, :], 1), PAIR[l // 2][:, 1, 0:HALF]).then_inc(free[l // 2], 1)
        with act.Fori(0, 2) as it:
            for c in range(8):
                h, qb = c % 2, c // 2
                w0, w = min(qb + 1, 2) * P, (qb + 1) * P
                wide = w0 + 2 * w
                m = it * 8 + c
                act.wait_ge(s_soft, m + 1)
                act.wait_ge(o_out, m + 1)
                nc.scalar.activation(sc_p[:, 0:wide], sc_p[:, 0:wide], ACT.Exp, bias=nm[:, h:h + 1],
                                     accum_out=ls[:, h:h + 1]).then_inc(s_exp, 1)
                lead(U_PC, 16, it, 2 * c)
                act.wait_ge(p_tr, m + 1)
                nt = wide // P
                act.wait_ge(o_mm, m + 1)
                for i, bank in enumerate((BT, BS, BA)):
                    n = min(4, nt - 4 * i)
                    if n > 0:
                        ins = act.copy(pT_t[:, 4 * i:4 * i + n, :], bank[:, 0:n * P].rearrange("p (n q) -> p n q", q=P))
                ins.then_inc(p_out, 1)
                lead(U_PC, 16, it, 2 * c + 1)
                pair = PAIR[c % 2]
                act_chunk = (c < 2) or c in (2, 5)
                if act_chunk:
                    act.wait_ge(w_used, Unit(U_PC, 16, it, 2 * c + 1).used)
                if c < 2:
                    for hf in range(2):
                        dst = pT[:, bass.ds(it * 2 + c, 1), hf * HALF:(hf + 1) * HALF].rearrange("p k t -> p (k t)")
                        ins = act.copy(dst, pair[:, hf, 0:HALF])
                    ins.then_inc(free[c % 2], 1)
                if c in (2, 5):
                    act.wait_ge(c_cp, it * 2 + (1 if c == 2 else 2))
                    act.copy(half(cS, 0), pair[:, 0, 0:HALF])
                    act.copy(half(cS, 1), pair[:, 1, 0:HALF]).then_inc(free[c % 2], 1)
        act.wait_ge(ss_max, 1)
        for h in range(HG):
            nc.scalar.activation(ss[:, h, :, :], ss[:, h, :, :], ACT.Exp, bias=smx[:, h:h + 1],
                                 accum_out=sls[:, h:h + 1]).then_inc(ss_exp, 1)
        act.wait_ge(grp_out, 4)
        act.wait_ge(oTs_out, 1)
        act.wait_ge(out_st, 16 * 7)
        for i in range(4):
            nc.scalar.copy(bH[:, i, :], pT[:, i, :]).then_inc(b_hi, 1)
        for i in range(2):
            nc.scalar.copy(bH[:, 4 + i, :], aT[:, i, :]).then_inc(b_hi, 1)
        for i in range(4):
            nc.scalar.copy(bH[:, 6 + i, :], bcv[:, i, :]).then_inc(b_hi, 1)
        act.wait_ge(b_lo, 10)
        with act.Fori(0, KD) as it:
            for l in range(16):
                if l + 2 == M_BR:
                    act.wait_ge(w_attn, it * 16 + 16)
                lead(U_M, 16, it, l)
                if l in M_GATE[1::2]:
                    i = M_GATE.index(l) // 2
                    act.wait_ge(w_used, Unit(U_M, 16, it, l).used)
                    act.wait_ge(br_out, it * 3 + 1)
                    for hf in range(2):
                        ins = nc.scalar.activation(half(sg[:, i, :], hf), PAIR[i % 2][:, hf, 0:HALF], ACT.Sigmoid)
                    ins.then_inc(free[i % 2], 1)
                if l == M_ADA[-1]:
                    act.wait_ge(w_used, Unit(U_M, 16, it, l).used)
                    act.wait_ge(mod_tr, it + 9)
                    nc.scalar.copy(mod_rows[0:18, :], BA[0:18, :]).then_inc(mod_row, 1)
        act.wait_ge(w_used, Unit(U_M, 16, KD - 1, M_GATE[-1]).used)
        act.wait_ge(br_out, 3 * KD + 1)
        for k in range(KD):
            nc.scalar.copy(hH[:, k, :], merged[:, k, :]).then_inc(m_hi, 1)
        act.wait_ge(m_lo, KD)
        with act.Fori(0, 8) as it:
            for l in range(4):
                lead(U_O, 4, it, l)
                if l % 2:
                    act.wait_ge(w_used, Unit(U_O, 4, it, l).used)
                    dst = mixT[:, bass.ds(it * 2 + l // 2, 1), :].rearrange("p k t -> p (k t)")
                    act.copy(half(dst, 0), PAIR[l // 2][:, 0, 0:HALF]).then_inc(mix_out, 1)
                    act.copy(half(dst, 1), PAIR[l // 2][:, 1, 0:HALF]).then_inc(free[l // 2], 1)
        norm_root(act, rbn_mm, 1, rbn, rt2)
        for k in range(KD):
            act.wait_ge(x1_done, k + 1)
            if k >= 2:
                act.wait_ge(sq_mm, k - 1)
            nc.scalar.activation(sqc[:, k % 2, :], xR[:, k, :], ACT.Square).then_inc(sq_in, 1)
        act.wait_ge(h2_pre, 1)
        norm_root(act, sq_mm, KD, rbn, rt2)
        act.wait_ge(h2_pre, 2)
        nc.scalar.copy(hH[:, :, SA], mixT[:, :, SA]).then_inc(h2_hi, 1)
        for k in range(KD):
            act.wait_ge(h2_pre, k + 3)
            nc.scalar.activation(hH[:, k, PR], mixT[:, k, PR], ACT.Identity, bias=mods[:, 3 * KD + k, 0:1]).then_inc(h2_hi, 1)

        act.wait_ge(x1_st, 16)
        act.wait_ge(h2_lo, KD + 1)

        def up_pair(base, per, it, l0, rnd4, late=False):
            for l in range(4):
                if base == U_F0 or l0 + l < 24:
                    lead(base, per, it, l0 + l)
                if l % 2:
                    v = l // 2
                    act.wait_ge(w_used, Unit(base, per, it, l0 + l).used)
                    act.wait_ge(tail_tr, rnd4 + 1)
                    act.wait_ge(cv_done, rnd4 * 2 + (v + 1))
                    act.copy(half(us[:, v, :], 0), PAIR[v][:, 0, 0:HALF])
                    act.copy(half(us[:, v, :], 1), PAIR[v][:, 1, 0:HALF]).then_inc(free[v], 1)
                    act.wait_ge(free[v], CF(rnd4) + 2)
                    act.wait_ge(f_done, rnd4 + 1)
                    nc.scalar.mul(cv[:, v, :], us[:, v, :], tap(2, v, rnd4)).then_inc(us_c, 1)
            act.wait_ge(cv_done, rnd4 * 2 + 3)
            nc.scalar.activation(cv[:, 0, :], cv[:, 0, :], ACT.Gelu_apprx_tanh).then_inc(gelu_done, 1)
            if not late:
                f_split(rnd4)

        def f_split(rnd4, p=None):
            act.wait_ge(f_done, rnd4 + 2)
            nc.scalar.copy(fH[:, PAIRNO[0] if p is None else p, :], ft).then_inc(f_hi, 1)

        for pair in range(FPR):
            PAIRNO[0] = pair
            up_pair(U_F0, 16, 0, 4 * pair, pair)
        with act.Fori(0, 10) as it:
            r4 = it * 4 + 4
            up_pair(U_F, 24, it, 0, r4, late=True)
            for l in range(4, 12):
                lead(U_F, 24, it, l)
            act.wait_ge(w_used, Unit(U_F, 24, it, 11).used)
            f_split(r4, 0)
            for pair in range(1, FPR):
                PAIRNO[0] = pair
                up_pair(U_F, 24, it, 8 + 4 * pair, r4 + pair)
        for l in range(9):
            if l < 6:
                lead(U_END, 8, 0, l)
            for k in (2 * l - 2, 2 * l - 1) if l else ():
                act.wait_ge(down_out, 2 * (10 * KD + k) + 6)
                if k >= 2:
                    act.wait_ge(sqf_used, k - 1)
                nc.scalar.activation(sqf[:, k % 2, :], acc[:, k, :], ACT.Square).then_inc(sqf_in, 1)
        norm_root(act, sqf_mm, 1, rbf, rt3)
        for n, (q, b) in enumerate(Y_TILES):
            act.wait_ge(y_tr, n + 1)
            if b < NB:
                nc.scalar.copy(yN[:, b, q * 512:(q + 1) * 512], (BA, BT, BS, BO)[b]).then_inc(y_nat, 1)
            else:
                nc.scalar.copy(yNs[:, q * 512:(q + 1) * 512], PAIR[q // 2][0:NS, q % 2, :]).then_inc(y_nat, 1)

    Y_TILES = [(q, b) for q in range(4) for b in range(NB + 1)]
    PAIRNO = [0]
    CF = lambda rnd4: rnd4 + C_F0

    def tap(i, v, rnd4):
        return ffn_w[:, i, bass.ds(rnd4 + v * FCH, 1)]

    def norm_root(act, s, n, dst, done):
        act.wait_ge(s, n)
        act.activation(dst[:, 0:HALF], X[:, 0, 0:HALF], ACT.Sqrt, bias=eps, scale=1.0 / D)
        act.activation(dst[:, HALF:T], X[:, 1, 0:HALF], ACT.Sqrt, bias=eps, scale=1.0 / D).then_inc(done, 1)

    BIAS_MM = [(g, n0, n1) for g in range(G) for n0, n1 in ((0, 385), (385, BW))]
    BIAS_BANK = [BT, BS, BO, BA, Y[:, 0, :], Y[:, 1, :]]

    def vector_program(dve):
        step = Step(dve, dve_step)

        def lo(u):
            dve.wait_ge(w_hi, u.hi_done)
            dve.tensor_tensor(wlo[u.spl], raw[:, u.raw, :], whi[u.spl], ALU.subtract).then_inc(w_lo, 1)

        def lead(base, per, it, l):
            lo(Unit(base, per, it, l + 2))

        for s, n in ((w_lo, 4), (w_used, 2), (x_free, 1), (y_free, 1), (mod_tr, 1), (mod_row, 1), (mod_out, 1),
                     (nat_tr, 2), (qk_out, 2), (nat_out, 2), (o_out, 1), (o_mm, 1), (oT_tr, 1), (c_cp, 1), (ks_used, 2),
                     (u_used, 1), (p_out, 1), (tail_tr, 1), (tail_out, 1), (cv_done, 2), (f_done, 1), (f_hi, 1),
                     (tail_free, 4), (down_out, 4)):
            dve.sem_inc(s, n)
        dve.memset(ones, 1.0)
        dve.memset(eps, EPS)
        dve.memset(relb, 1.0).then_inc(set_up, 1)
        dve.wait_ge(silu, 1)
        step(dve.tensor_tensor(cc, cc, csig, ALU.mult))
        step.settle()
        dve.sem_inc(c_split, 1)
        dve.wait_ge(c_tr, 1)
        cps = BA[:, 0:KD * 9].rearrange("p (k n) -> p k n", n=9)
        step(dve.tensor_copy(cT[:, :, 0:9], cps))
        step.settle()
        dve.tensor_tensor(cT[:, :, 9:18], cps, cT[:, :, 0:9], ALU.subtract).then_inc(c_split, 1)
        dve.wait_ge(par_tr, 1)
        dve.tensor_copy(cols, BT[:, 0:80]).then_inc(par_out, 1)
        dve.tensor_copy(ffn_w, BS[:, 0:3 * 88].rearrange("p (t k) -> p t k", t=3)).then_inc(par_out, 1)
        dve.tensor_copy(st_conv, BO[:, 0:64].rearrange("p (k b r) -> p k b r", k=4, b=NS)).then_inc(par_out, 1)
        dve.tensor_copy(st_pool, X[:, 0, 0:480].rearrange("p (k b r) -> p k b r", k=4, b=NS)).then_inc(par_out, 1)
        for n in range(17):
            dve.wait_ge(x_tr, n + 1)
            bank = (X[:, 1, :], BT, BS, X[:, 0, :])[n % 4] if n < 16 else BO
            if n < 16:
                b, q = n // 4, n % 4
                dve.tensor_copy(xT[:, 4 * q:4 * q + 4, b * P:(b + 1) * P], bank.rearrange("p (k t) -> p k t", t=P)).then_inc(x_out, 1)
            else:
                dve.tensor_copy(xT[:, :, SA], bank[:, 0:KD * NS].rearrange("p (k t) -> p k t", t=NS)).then_inc(x_out, 1)
        dve.wait_ge(rt_done, 2)
        step(dve.reciprocal(rs[:, 0:4], rs[:, 0:4]))
        step(dve.reciprocal(rs[0:NS, 4:5], rs[0:NS, 4:5]))
        step.settle()
        for b in range(NB):
            step(dve.tensor_scalar(diag[:, b, :], ident, rs[:, b:b + 1], None, ALU.mult))
        dve.tensor_scalar(diag[0:NS, 4, 0:NS], ident[0:NS, 0:NS], rs[0:NS, 4:5], None, ALU.mult).then_inc(diag_done, 1)
        dve.wait_ge(rb_done, 2)
        for l in range(2):
            lo(Unit(0, 0, 0, l))
        with dve.Fori(0, 8) as it:
            step.enter(it, 2)
            for l in range(8):
                lead(U_ADA, 8, it, l)
                if l in (2, 5):
                    k = bass.ds(it * 2 + l // 3, 1)
                    flat = lambda t: t[:, k, :].rearrange("p k t -> p (k t)")
                    step(dve.tensor_tensor(flat(xr), flat(xT), rb, ALU.mult))
            mod_columns(dve, it, it + 1)
            step.leave(8)
        step.settle()
        dve.wait_ge(mod_out, 9)
        modulate(dve, step, xr, 0, 1, 0, h_pre, h_hi, h_lo, 1)
        for part in range(3):
            with dve.Fori(0, 3) as it:
                step.enter(it, 0)
                for l in range(4):
                    lead(U_QKV + 12 * part, 4, it, l)
                    i = l // 2
                    c = it * 2 + (i + 6 * part)
                    if l % 2:
                        dve.wait_ge(free[i], it + (3 * part + 2))
                        if part < 2:
                            dst = qk[:, bass.ds(c, 1), :].rearrange("p k t -> p (k t)")
                            dve.tensor_copy(dst, stage[:, i, 0:TP]).then_inc(qk_out, 1)
                        else:
                            dve.sem_inc(qk_out, 1)
                        dve.wait_ge(nat_tr, c + 3)
                        nat_rows = dve.tensor_copy(ns[:, bass.ds(c * P, P)], (BO, BA)[i][0:NS, 0:P])
                        if part == 0:
                            nat_rows.then_inc(nat_out, 1)
                        else:
                            nat = (kn, vn)[part - 1][:, bass.ds(it, 1), :, i * P:(i + 1) * P].rearrange("p g b n -> p (g b) n")
                            dve.tensor_copy(nat, (BT, BS)[i].rearrange("p (b n) -> p b n", n=P)).then_inc(nat_out, 1)
                step.leave(3)
        dve.wait_ge(k_st, 16 * 6)
        step(dve.memset(q2, 0.0))
        step.settle()
        with dve.Fori(0, 2) as it:
            step.enter(it, 58)
            def queries(c):
                h, qb = c % 2, c // 2
                src = qk[64 * h:64 * h + 64, 0:QCH, qb * P:(qb + 1) * P].rearrange("p (g j) q -> p j g q", j=2)
                dve.tensor_copy(q2[64 * h:64 * h + 64, h, :, :], src[:, bass.ds(it, 1)].rearrange("p j g q -> p (j g) q")).then_inc(q2_in, 1)

            queries(0)
            dve.wait_ge(u_in, it * 64 + 64)
            for c in range(8):
                h, qb = c % 2, c // 2
                m = it * 8 + c
                wg = [min(qb + 1, 2) * P, (qb + 1) * P, (qb + 1) * P]
                wide = sum(wg)
                dve.wait_ge(s_mm, m + 1)
                o = 0
                for g, bank in enumerate((BT, BS, BA)):
                    end = 256 if g == 0 else 256 + 512 * g
                    step(dve.scalar_tensor_tensor(out=sc_p[:, o:o + wg[g]], in0=bank[:, 0:wg[g]], scalar=SCALE,
                                                  in1=u_bias[:, h, end - wg[g]:end], op0=ALU.mult, op1=ALU.add))
                    o += wg[g]
                step.settle()
                step(dve.tensor_reduce(mx[:, h:h + 1], sc_p[:, 0:wide], AX.X, ALU.max))
                step.settle()
                dve.tensor_scalar(nm[:, h:h + 1], mx[:, h:h + 1], -1.0, None, ALU.mult).then_inc(s_soft, 1)
                if c < 7:
                    queries(c + 1)
                lead(U_PC, 16, it, 2 * c)
                if c % 2 == 0:
                    b = c // 2
                    s = b % 2
                    dve.wait_ge(qB_in[s], it * 32 + (b // 2 + 1) * 16)
                    dve.wait_ge(ks_in[s], it * 96 + (b // 2 + 1) * 48)
                    prod = k_s[:, s, :]
                    step(dve.tensor_tensor(prod, prod, qB[:, s, :], ALU.mult))
                    step.settle()
                    dst = sc_s[:, bass.ds(it * 4 + b, 1), :].rearrange("p b n -> p (b n)")
                    dve.tensor_reduce(dst, prod.rearrange("p (n e) -> p n e", e=DH), AX.X, ALU.add).then_inc(ks_used, 1)
                    dve.wait_ge(ks_used, it * 4 + b + 3)
                lead(U_PC, 16, it, 2 * c + 1)
                pair = PAIR[c % 2]
                kind, i = ("p", c) if c < 2 else ("chb"[(c - 2) % 3], (c - 2) // 3)
                if kind in "hb":
                    dve.wait_ge(w_used, Unit(U_PC, 16, it, 2 * c + 1).used)
                if kind == "h":
                    dve.wait_ge(free[(c - 1) % 2], it * 4 + (C_PC + (c - 1) // 2 + 2))
                    step(dve.tensor_tensor(half(uS, 0), half(cS, 0), pair[:, 0, 0:HALF], ALU.mult))
                    dve.tensor_tensor(half(uS, 1), half(cS, 1), pair[:, 1, 0:HALF], ALU.mult).then_inc(free[c % 2], 1)
                    step.settle()
                    dve.wait_ge(free[c % 2], it * 4 + (C_PC + c // 2 + 2))
                    dve.sem_inc(c_cp, 1)
                    ci = it * 2 + i
                    w = lambda t: cols[:, bass.ds(ci + (64 + 4 * t), 1)]
                    st = lambda r: st_conv[:, bass.ds(ci, 1), :, r].rearrange("p k b -> p (k b)")
                    step(dve.tensor_copy(utail[:, bass.ds(ci, 1), :].rearrange("p k t -> p (k t)"), uS[:, TP - 2:T]))
                    step(dve.tensor_scalar(yS, uS, w(2), None, ALU.mult))
                    step.settle()
                    stt = lambda o, x_, w_: dve.scalar_tensor_tensor(out=o, in0=x_, scalar=w_, in1=o, op0=ALU.mult, op1=ALU.add)
                    step(stt(yS[:, 1:TP], uS[:, 0:TP - 1], w(1)))
                    step(stt(yS[:, SA], st(1), w(1)))
                    step.settle()
                    step(stt(yS[:, 2:TP], uS[:, 0:TP - 2], w(0)))
                    step(stt(yS[:, SA], st(0), w(0)))
                    step.settle()
                if kind == "b":
                    for hf in range(2):
                        dst = bcv[:, bass.ds(it * 2 + i, 1), hf * HALF:(hf + 1) * HALF].rearrange("p k t -> p (k t)")
                        ins = dve.tensor_tensor(dst, half(yS, hf), pair[:, hf, 0:HALF], ALU.mult)
                    ins.then_inc(free[c % 2], 1)
                dve.wait_ge(s_exp, m + 1)
                step(dve.reciprocal(rl[:, h:h + 1], ls[:, h:h + 1]))
                step.settle()
                dve.wait_ge(o_mm, m + 2)
                if h == 0:
                    dve.wait_ge(oT_tr, it * 4 + (qb + 1))
                dve.tensor_scalar(osb[:, h, :], BO[:, 0:DH], rl[:, h:h + 1], None, ALU.mult).then_inc(o_out, 1)
                if h == 1:
                    dve.wait_ge(oT_tr, it * 4 + (qb + 2))
                    dst = aT[:, bass.ds(it, 1), qb * P:(qb + 1) * P].rearrange("p k t -> p (k t)")
                    dve.tensor_copy(dst, BO[:, P:2 * P]).then_inc(oT_out, 1)
            dve.sem_inc(u_used, 1)
            step.leave(2)
        dve.wait_ge(oT_out, 8)
        dve.wait_ge(bS_in, 16)
        bv = bS.rearrange("p (h g) n -> p h g n", g=G)
        dve.wait_ge(ss_tr, 1)
        n = 0
        for h in range(HG):
            for g in range(G):
                bank = (BT, BS, BA)[n // 4]
                step(dve.scalar_tensor_tensor(out=ss[:, h, g, 0:NK], in0=bank[0:NS, n % 4 * P:(n % 4 + 1) * P], scalar=SCALE,
                                              in1=bv[:, h, g, 0:NK], op0=ALU.mult, op1=ALU.add))
                n += 1
        step(dve.tensor_tensor(t8, ns[:, 0:AW], ns[:, AW:2 * AW], ALU.mult))
        step.settle()
        step(dve.tensor_reduce(n8, t8.rearrange("p (n e) -> p n e", e=DH), AX.X, ALU.add))
        step.settle()
        step(dve.scalar_tensor_tensor(out=ss[:, :, :, NK], in0=n8.rearrange("p (g h) -> p h g", g=G), scalar=SCALE,
                                      in1=bv[:, :, :, NK], op0=ALU.mult, op1=ALU.add))
        step.settle()
        step(dve.tensor_reduce(smx, ss.rearrange("p h g n -> p h (g n)"), AX.X, ALU.max))
        step.settle()
        dve.tensor_scalar(smx, smx, -1.0, None, ALU.mult).then_inc(ss_max, 1)
        dve.wait_ge(ss_exp, HG)
        step(dve.reciprocal(srl, sls))
        step.settle()
        for h in range(HG):
            ins = dve.tensor_scalar(ss[:, h, :, :], ss[:, h, :, :], srl[:, h:h + 1], None, ALU.mult)
            if h < HG - 1:
                step(ins)
        ins.then_inc(ss_norm, 1)
        dve.wait_ge(ss_norm, 1)
        v4 = ns[:, 2 * AW:3 * AW].rearrange("p (g h e) -> p g h e", g=G, h=HG)
        t4 = t8.rearrange("p (g h e) -> p g h e", g=G, h=HG)
        for g in range(G):
            step(dve.tensor_tensor(t4[:, g], v4[:, g], ss[:, :, g, NK:NK + 1].to_broadcast([NS, HG, DH]), ALU.mult))
        step.settle()
        step(dve.tensor_tensor(nv8, t8[:, 0:256], t8[:, 256:512], ALU.add))
        step.settle()
        dve.tensor_tensor(nv8, nv8, t8[:, 512:768], ALU.add).then_inc(nv_out, 1)
        dve.wait_ge(pts_tr, 1)
        pts = BT[:, 0:12 * NS].rearrange("p (h g b) -> p h g b", h=HG, g=G)
        for h in range(HG):
            ins = dve.tensor_copy(pTs[:, :, :, h], pts[:, h])
        ins.then_inc(pts_out, 1)
        for b in range(NS):
            dve.wait_ge(vs_mm, b + 1)
            bank = (BS, BA)[b % 2]
            dve.tensor_tensor(mk[:, b % 2, :], bank[0:HG, 0:256], heads_mask, ALU.mult).then_inc(vs_out, 1)
        dve.wait_ge(oTs_mm, 1)
        dve.tensor_copy(aT[:, :, SA], BO[:, 0:2 * NS].rearrange("p (c b) -> p c b", c=2)).then_inc(oTs_out, 1)
        dve.wait_ge(ptail_tr, 1)
        dve.tensor_copy(t_tails[:, 0, :], X[0:23, 0, :]).then_inc(ptail_out, 1)
        dve.tensor_copy(t_tails[0:10, 1, :], X[0:10, 1, :]).then_inc(ptail_out, 1)
        for i, w in enumerate(WIN):
            pc = pT[:, i, :]
            a_, b_ = stage[:, 0, :], stage[:, 1, :]
            src, width = pc, 1
            while width < w:
                dst = a_ if src is not a_ else b_
                step(dve.tensor_tensor(dst[:, width:TP], src[:, width:TP], src[:, 0:TP - width], ALU.add))
                step(dve.tensor_copy(dst[:, 0:width], src[:, 0:width]))
                step.settle()
                src, width = dst, 2 * width
            oth = a_ if src is not a_ else b_
            step(dve.tensor_tensor(oth[:, 0:16], src[:, 0:16], counts[:, i, :], ALU.mult))
            step(dve.tensor_reduce(oth[:, TP:T], st_pool[:, i, :, 16 - w:15], AX.X, ALU.add))
            step.settle()
            step(dve.tensor_tensor(oth[:, TP:T], oth[:, TP:T], pc[:, SA], ALU.add))
            step.settle()
            step(dve.scalar_tensor_tensor(out=pc[:, 16:TP], in0=src[:, 16:TP], scalar=1.0 / w, in1=pc[:, 16:TP],
                                          op0=ALU.mult, op1=ALU.subtract))
            step(dve.tensor_tensor(pc[:, 0:16], oth[:, 0:16], pc[:, 0:16], ALU.subtract))
            dve.scalar_tensor_tensor(out=pc[:, SA], in0=oth[:, TP:T], scalar=1.0 / w, in1=pc[:, SA],
                                     op0=ALU.mult, op1=ALU.subtract).then_inc(pool_done, 1)
            step.settle()
            dve.wait_ge(pool_done, i + 1)
        for i in range(4):
            pair = PAIR[i % 2]
            dve.wait_ge(grp_mm, i + 1)
            step(dve.tensor_scalar(half(pT[:, i, :], 0), pair[:, 0, 0:HALF], cols[:, 76 + i:77 + i], None, ALU.mult))
            dve.tensor_scalar(half(pT[:, i, :], 1), pair[:, 1, 0:HALF], cols[:, 76 + i:77 + i], None, ALU.mult).then_inc(grp_out, 1)
        for i in range(10):
            dve.wait_ge(b_hi, i + 1)
            src = pT[:, i, :] if i < 4 else aT[:, i - 4, :] if i < 6 else bcv[:, i - 6, :]
            dve.tensor_tensor(bL[:, i, :], src, bH[:, i, :], ALU.subtract).then_inc(b_lo, 1)
        dve.wait_ge(b_lo, 10)
        dve.wait_ge(k_st, 16 * 6)
        dve.wait_ge(v_st, 16 * 6)
        dve.sem_inc(br_out, 1)
        with dve.Fori(0, KD) as it:
            step.enter(it, 3)
            dst = merged[:, bass.ds(it, 1), :].rearrange("p k t -> p (k t)")
            for l in range(M_BR):
                lead(U_M, 16, it, l)
            for n, (i, pr) in enumerate(((0, 1), (2, 0), (1, 1))):
                if n == 0:
                    dve.wait_ge(br_mm, it + 1)
                    dve.wait_ge(x_free, it * 3 + (C_M + 3))
                    dve.wait_ge(y_free, it * 3 + (C_M + 2))
                else:
                    if n == 2:
                        lead(U_M, 16, it, 14)
                    last = (M_BR, M_CONV)[n - 1]
                    lead(U_M, 16, it, last)
                    dve.wait_ge(w_used, Unit(U_M, 16, it, last).used)
                for hf in range(2):
                    o = half(dst, hf) if n == 0 else half(mt[:, n - 1, :], hf)
                    ins = dve.tensor_tensor(o, half(sg[:, i, :], hf), PAIR[pr][:, hf, 0:HALF], ALU.mult)
                    if hf == 0:
                        step(ins)
                ins.then_inc(free[pr], 1)
                dve.wait_ge(free[pr], it * 3 + (C_M + (3 if n == 0 else 4)))
                if n == 0:
                    dve.sem_inc(br_out, 1)
                else:
                    dve.tensor_tensor(dst, dst, mt[:, n - 1, :], ALU.add).then_inc(br_out, 1)
                    dve.wait_ge(br_out, it * 3 + (n + 2))
            mod_columns(dve, it + 8, it + 9)
            step.leave(KD)
        for k in range(KD):
            dve.wait_ge(m_hi, k + 1)
            dve.tensor_tensor(hL[:, k, :], merged[:, k, :], hH[:, k, :], ALU.subtract).then_inc(m_lo, 1)
        dve.wait_ge(w_used, Unit(U_M, 16, KD - 1, 15).used)
        step(dve.memset(sacc, 0.0))
        with dve.Fori(0, 8) as it:
            step.enter(it, 4)
            for l in range(4):
                lead(U_O, 4, it, l)
                if l % 2:
                    dve.wait_ge(free[l // 2], it + (C_O + 2))
                    src = mixT[:, bass.ds(it * 2 + l // 2, 1), :].rearrange("p k t -> p (k t)")
                    step(dve.tensor_tensor(sqc[:, 0, :], src, src, ALU.mult))
                    step.settle()
                    step(dve.tensor_tensor(sacc, sacc, sqc[:, 0, :], ALU.add))
                    step.settle()
            step.leave(8)
        dve.sem_inc(sacc_done, 1)
        coefficients(dve, step, 1, 2, False)
        dve.wait_ge(rt2, 1)
        step(dve.reciprocal(rbn, rbn))
        step.settle()
        dve.wait_ge(x_back, 16)
        residual(dve, step, mixT, rbn, xR, x1_done)
        dve.wait_ge(x1_done, KD)
        coefficients(dve, step, 2, 4, True)
        dve.sem_inc(h2_pre, 1)
        dve.wait_ge(rt2, 2)
        step(dve.reciprocal(rbn, rbn))
        step.settle()
        rS, shift = rbn[:, SA].unsqueeze(1).to_broadcast([P, KD, NS]), mods[:, 3 * KD:4 * KD, :]
        step(dve.tensor_tensor(mixT[:, :, SA], xR[:, :, SA], coef[:, :, 1:9], ALU.mult))
        step.settle()
        step(dve.tensor_tensor(mixT[:, :, SA], mixT[:, :, SA], rS, ALU.mult))
        step.settle()
        dve.tensor_tensor(mixT[:, :, SA], mixT[:, :, SA], shift[:, :, 1:9], ALU.add).then_inc(h2_pre, 1)
        for k in range(KD + 1):
            if k < KD:
                dve.scalar_tensor_tensor(out=mixT[:, k, PR], in0=xR[:, k, PR], scalar=coef[:, k, 0:1], in1=rbn[:, PR],
                                         op0=ALU.mult, op1=ALU.mult).then_inc(h2_pre, 1)
            dve.wait_ge(h2_hi, k + 1)
            if k == 0:
                dve.tensor_tensor(hL[:, :, SA], mixT[:, :, SA], hH[:, :, SA], ALU.subtract).then_inc(h2_lo, 1)
            else:
                dve.scalar_tensor_tensor(out=hL[:, k - 1, PR], in0=mixT[:, k - 1, PR], scalar=shift[:, k - 1, 0:1],
                                         in1=hH[:, k - 1, PR], op0=ALU.add, op1=ALU.subtract).then_inc(h2_lo, 1)

        def states(rnd):
            dve.wait_ge(st_tr, rnd + 1)
            ins = dve.tensor_copy(st_f, BO[:, 0:128].rearrange("p (v k b r) -> p v k b r", v=2, k=4, b=NS))
            ins.then_inc(st_out, 1)
            dve.wait_ge(st_out, rnd + 1)

        def tails(rnd4, p):
            dve.wait_ge(tail_tr, rnd4 + 2)
            dve.wait_ge(tail_free, TAILS_FREE(rnd4, p))
            ins = dve.tensor_copy(trow[:, :, p * P:(p + 1) * P], BA[0:10, 0:256].rearrange("p (v n) -> p v n", v=2))
            ins.then_inc(tail_out, 1)

        def convolve(base, per, it, l0, rnd4, p, after={}):
            for l in range(4):
                lead(base, per, it, l0 + l)
                if l in after:
                    after[l]()
                if l % 2:
                    v = l // 2
                    st = lambda r: st_f[:, v, p, :, r]
                    stt = lambda o, x_, w_: dve.scalar_tensor_tensor(out=o, in0=x_, scalar=w_, in1=o, op0=ALU.mult, op1=ALU.add)
                    dve.wait_ge(us_c, rnd4 * 2 + (v + 1))
                    step(stt(cv[:, v, 1:TP], us[:, v, 0:TP - 1], tap(1, v, rnd4)))
                    step(stt(cv[:, v, SA], st(1), tap(1, v, rnd4)))
                    step.settle()
                    step(stt(cv[:, v, 2:TP], us[:, v, 0:TP - 2], tap(0, v, rnd4)))
                    stt(cv[:, v, SA], st(0), tap(0, v, rnd4)).then_inc(cv_done, 1)
            dve.wait_ge(gelu_done, rnd4 + 1)
            dve.wait_ge(cv_done, rnd4 * 2 + 4)
            step.settle()
            dve.wait_ge(f_hi, rnd4 + 1)
            dve.tensor_tensor(ft, cv[:, 0, :], cv[:, 1, :], ALU.mult).then_inc(f_done, 1)

        def f_lo_part(rnd4, p):
            dve.wait_ge(f_hi, rnd4 + 2)
            dve.tensor_tensor(fL[:, p, :], ft, fH[:, p, :], ALU.subtract).then_inc(f_lo, 1)

        def accumulate(rnd, l, done, between):
            for i in range(2):
                m = 2 * l + i
                if i == 0:
                    dve.wait_ge(down_mm, rnd * 8 + (l + 1))
                else:
                    dve.wait_ge(w_used, done)
                for hf, bank in enumerate(((BA, BT), (BS, BO))[i]):
                    o = half(acc[:, m, :], hf)
                    dve.tensor_tensor(o, o, bank[:, 0:HALF], ALU.add).then_inc(down_out, 1)
            if between:
                between()

        dve.wait_ge(x1_st, 16)
        states(0)
        for p in range(FPR):
            convolve(U_F0, 16, 0, 4 * p, p, p, {0: lambda: tails(p - 1, p - 1)} if p else {})
            f_lo_part(p, p)
            step(dve.memset(acc[:, 4 * p:4 * p + 4, :], 0.0))
        step.settle()
        with dve.Fori(0, 10) as it:
            step.enter(it, 24)
            r4 = it * 4 + 4
            convolve(U_F, 24, it, 0, r4, 0, {0: lambda: tails(it * 4 + 3, 3), 1: lambda: states(it + 1)})
            for l in range(8):
                accumulate(it, l, Unit(U_F, 24, it, 4 + l).used, lambda: lead(U_F, 24, it, 4 + l))
            f_lo_part(r4, 0)
            for p in range(1, FPR):
                convolve(U_F, 24, it, 8 + 4 * p, r4 + p, p, {0: lambda: tails(r4 + (p - 1), p - 1)})
                f_lo_part(r4 + p, p)
            step.leave(10)
        tails(4 * ROUNDS - 1, 3)
        def add_square(m):
            dve.wait_ge(sqf_in, m + 1)
            dve.tensor_tensor(fsum, fsum, sqf[:, m % 2, :], ALU.add).then_inc(sqf_used, 1)
            dve.wait_ge(sqf_used, m + 1)

        step(dve.memset(fsum, 0.0))
        step.settle()
        for l in range(8):
            def behind():
                if l < 6:
                    lead(U_END, 8, 0, l)
                for m in (2 * l - 2, 2 * l - 1):
                    if m >= 0:
                        add_square(m)

            accumulate(ROUNDS - 1, l, Unit(U_END, 8, 0, l).used, behind)
        add_square(KD - 2)
        add_square(KD - 1)
        coefficients(dve, step, 3, 5, False)
        dve.wait_ge(rt3, 1)
        step(dve.reciprocal(rbf, rbf))
        step.settle()
        dve.wait_ge(x1_back, 16)
        dve.wait_ge(down_out, 2 * ROUNDS * KD + 4)
        residual(dve, step, acc, rbf, x1, y_done)

    TAILS_FREE = lambda rnd4, p: (rnd4 - p) + 4

    def mod_columns(dve, tile, n):
        dve.wait_ge(mod_tr, n + 1)
        dst = mods[:, bass.ds(tile * 4, 4), :]
        dve.tensor_copy(dst, BT[:, 0:36].rearrange("p (k n) -> p k n", n=9)).then_inc(mod_out, 1)

    def coefficients(dve, step, norm, mod, plus_one):
        gcol = cols[:, norm * KD:(norm + 1) * KD].unsqueeze(2).to_broadcast([P, KD, 9])
        step(dve.scalar_tensor_tensor(out=coef, in0=mods[:, mod * KD:(mod + 1) * KD, :], scalar=1.0 if plus_one else 0.0,
                                      in1=gcol, op0=ALU.add, op1=ALU.mult))
        step.settle()

    def modulate(dve, step, x, norm, scale, shift, pre, hi_, lo_, extra):
        if extra == 1:
            coefficients(dve, step, norm, scale, True)
        sh = mods[:, shift * KD:(shift + 1) * KD, :]
        step(dve.tensor_tensor(x[:, :, SA], x[:, :, SA], coef[:, :, 1:9], ALU.mult))
        step.settle()
        step(dve.tensor_tensor(x[:, :, SA], x[:, :, SA], sh[:, :, 1:9], ALU.add))
        step.settle()
        for k in range(KD + 1):
            if k < KD:
                dve.tensor_scalar(x[:, k, PR], x[:, k, PR], coef[:, k, 0:1], sh[:, k, 0:1], ALU.mult, ALU.add).then_inc(pre, 1)
            if k:
                dve.wait_ge(hi_, k)
                dve.tensor_tensor(hL[:, k - 1, :], x[:, k - 1, :], hH[:, k - 1, :], ALU.subtract).then_inc(lo_, 1)

    def residual(dve, step, f, root, x, done):
        rS = root[:, SA].unsqueeze(1).to_broadcast([P, KD, NS])
        step(dve.tensor_tensor(f[:, :, SA], f[:, :, SA], coef[:, :, 1:9], ALU.mult))
        step.settle()
        step(dve.tensor_tensor(f[:, :, SA], f[:, :, SA], rS, ALU.mult))
        for k in range(KD + 1):
            if k < KD:
                step(dve.scalar_tensor_tensor(out=f[:, k, PR], in0=f[:, k, PR], scalar=coef[:, k, 0:1], in1=root[:, PR],
                                              op0=ALU.mult, op1=ALU.mult))
            if k:
                step.settle(1 if k < KD else 0)
                dve.tensor_tensor(x[:, k - 1, :], x[:, k - 1, :], f[:, k - 1, :], ALU.add).then_inc(done, 1)

    def tensor_program(pe):
        def three(ps, u, w0, xh, xl, first, last, wn=P):
            h, l = whi[u.spl][:, w0:w0 + wn], wlo[u.spl][:, w0:w0 + wn]
            pe.matmul(ps, h, xh, start=first, stop=False)
            pe.matmul(ps, h, xl, start=False, stop=False)
            return pe.matmul(ps, l, xh, start=False, stop=last)

        def ready(u):
            pe.wait_ge(w_lo, u.lo_done)

        def chunk(base, per, it, l0, pair, fr, before, between=None, split=None, apart=1, lag=1):
            pe.wait_ge(fr, before + 1)
            for l in range(2):
                u = Unit(base, per, it, l0 + l * apart)
                ready(u)
                for hf in range(2):
                    for k in range(8):
                        kk = 8 * l + k
                        if split is not None and hf == 0:
                            pe.wait_ge(split, kk + lag)
                        m = three(pair[:, hf, 0:HALF], u, k * P, half(hH[:, kk, :], hf), half(hL[:, kk, :], hf),
                                  kk == 0, kk == 15)
                m.then_inc(w_used, 1)
                if l == 0 and between:
                    between()

        def ada_unit(u, n, j):
            if j == 0:
                pe.wait_ge(mod_row, n + 1)
            ready(u)
            for k in range(2):
                for part in (whi, wlo):
                    kk = 2 * j + k
                    m = pe.matmul(BA[0:18, :], cT[:, kk, :], part[u.spl][:, k * 512:(k + 1) * 512],
                                  start=(kk == 0 and part is whi), stop=(kk == 15 and part is wlo), skip_group_check=True)
            m.then_inc(w_used, 1)

        def turn_mods(n):
            pe.wait_ge(mod_row, n + 2)
            pe.wait_ge(mod_bias, n * 16 + 16)
            pe.wait_ge(mod_out, n + 1)
            for i in range(4):
                m = pe.matmul(BT[:, 9 * i:9 * i + 9], mod_rows[:, i * P:(i + 1) * P], sel, start=True, stop=True)
            m.then_inc(mod_tr, 1)

        pe.wait_ge(c_split, 1)
        for k in range(KD):
            m = pe.transpose(BA[:, 9 * k:9 * k + 9], cc[:, k * P:(k + 1) * P], ident[0:9, 0:9])
        m.then_inc(c_tr, 1)
        pe.wait_ge(row_in, 16 * 6)
        pe.transpose(BT[:, 0:80], rows1, ident[0:80, 0:80])
        for t in range(3):
            pe.transpose(BS[:, 88 * t:88 * t + 88], rowsF[:, t, :], ident[0:88, 0:88])
        for k in range(4):
            pe.transpose(BO[:, 16 * k:16 * k + 16], rowsC[:, k * P:(k + 1) * P], ident[0:16, 0:16])
        for k in range(4):
            m = pe.transpose(X[:, 0, 120 * k:120 * k + 120], rowsP[:, k * P:(k + 1) * P], ident[0:120, 0:120])
        m.then_inc(par_tr, 1)
        pe.wait_ge(bias_in, 32)
        pe.wait_ge(par_out, 4)
        pe.wait_ge(c_split, 2)
        for i, (g, n0, n1) in enumerate(BIAS_MM):
            pe.matmul(BIAS_BANK[i][0:HG, 0:n1 - n0], relb[:, 4 * g:4 * g + 4], onehot[:, g, n0:n1],
                      start=True, stop=True).then_inc(b_mm, 1)
        pe.wait_ge(x_in, 16 * 5)
        pe.wait_ge(b_out, 6)
        for n in range(16):
            bank = (X[:, 1, :], BT, BS, X[:, 0, :])[n % 4]
            b, q = n // 4, n % 4
            if n >= 4:
                pe.wait_ge(x_out, n - 3)
            for i in range(4):
                k = 4 * q + i
                m = pe.transpose(bank[:, i * P:(i + 1) * P], xN[:, b, k * P:(k + 1) * P], ident)
            m.then_inc(x_tr, 1)
        for k in range(KD):
            m = pe.transpose(BO[:, NS * k:NS * k + NS], xs[:, k * P:(k + 1) * P], ident[0:NS, 0:NS])
        m.then_inc(x_tr, 1)
        pe.wait_ge(diag_done, 1)
        pe.wait_ge(x_out, 17)
        for b in range(NB):
            pe.matmul(X[:, 0, b * P:(b + 1) * P], ones, diag[:, b, :], start=True, stop=True)
        pe.matmul(X[:, 1, 0:NS], ones[0:NS, :], diag[0:NS, 4, 0:NS], start=True, stop=True).then_inc(rb_mm, 1)
        pe.wait_ge(k_in, 48)
        with pe.Fori(0, 8) as it:
            for l in range(8):
                ada_unit(Unit(U_ADA, 8, it, l), it, l)
            turn_mods(it)
        pe.wait_ge(rb_done, 2)
        last_turn = None
        for part in range(3):
            def turn(it, i, part=part):
                c = it * 2 + (i + 6 * part)
                pe.wait_ge(free[i], it + (3 * part + 2))
                pe.wait_ge(nat_out, c + 1)
                if part:
                    for b in range(NB):
                        pe.transpose((BT, BS)[i][:, b * P:(b + 1) * P], stage[:, i, b * P:(b + 1) * P], ident)
                pe.transpose((BO, BA)[i][0:NS, 0:P], stage[:, i, SA], ident).then_inc(nat_tr, 1)

            def two_chunks(it, before):
                base = U_QKV + 12 * part
                chunk(base, 4, it, 0, X, x_free, it + (C_QKV + 3 * part), between=before, split=h_lo if part == 0 else None)
                chunk(base, 4, it, 2, Y, y_free, it + (C_QKV + 3 * part), between=lambda: turn(it, 0))

            two_chunks(0, last_turn)
            with pe.Fori(1, 3) as it:
                two_chunks(it, lambda: turn(it - 1, 1))
            last_turn = lambda turn=turn: turn(2, 1)
        last_turn()
        pe.wait_ge(nat_out, 3 * QCH + 2)
        with pe.Fori(0, 2) as it:
            def turn_outputs(qb):
                pe.wait_ge(o_out, it * 8 + (2 * qb + 3))
                pe.transpose(BO[:, P:2 * P], osb.rearrange("p h e -> p (h e)"), ident).then_inc(oT_tr, 1)

            for c in range(8):
                h, qb = c % 2, c // 2
                m = it * 8 + c
                lo_kb = (max(qb - 1, 0), 0, 0)
                pe.wait_ge(q2_in, m + 1)
                pe.wait_ge(p_out, m + 1)
                for g, bank in enumerate((BT, BS, BA)):
                    keys = qk[:, bass.ds(it + (QCH + 2 * g), 1), lo_kb[g] * P:(qb + 1) * P].rearrange("p k t -> p (k t)")
                    ins = pe.matmul(bank[:, 0:(qb + 1 - lo_kb[g]) * P], q2[:, h, g, :], keys, start=True, stop=True)
                ins.then_inc(s_mm, 1)
                if c and c % 2 == 0:
                    turn_outputs(qb - 1)

                blocks = [(g, kb) for g in range(G) for kb in range(lo_kb[g], qb + 1)]

                def turn_probs():
                    pe.wait_ge(s_exp, m + 1)
                    for n in range(len(blocks)):
                        t = pe.transpose((BT, BS, BA)[n // 4][:, n % 4 * P:(n % 4 + 1) * P], sc_p[:, n * P:(n + 1) * P], ident)
                    t.then_inc(p_tr, 1)

                chunk(U_PC, 16, it, 2 * c, PAIR[c % 2], free[c % 2], it * 4 + (C_PC + c // 2), between=turn_probs)
                pe.wait_ge(p_out, m + 2)
                pe.wait_ge(o_out, m + 1)
                if qb:
                    pe.wait_ge(oT_out, it * 4 + qb)
                for n, (g, kb) in enumerate(blocks):
                    v = vn[:, g, kb, :].rearrange("p (j n) -> p j n", j=2)[:, bass.ds(it, 1), h * DH:(h + 1) * DH]
                    t = pe.matmul(BO[:, 0:DH], pT_t[:, n, :], v.rearrange("p j n -> p (j n)"), start=(n == 0), stop=(n == len(blocks) - 1))
                t.then_inc(o_mm, 1)
            turn_outputs(NB - 1)
        pe.wait_ge(ks_used, 10)
        pe.wait_ge(p_out, 17)
        pe.wait_ge(oT_out, 8)
        for h in range(HG):
            for g in range(G):
                n = h * G + g
                t = pe.transpose((BT, BS, BA)[n // 4][0:NS, n % 4 * P:(n % 4 + 1) * P], sc_s[:, :, g * HG + h], ident)
        t.then_inc(ss_tr, 1)
        pe.wait_ge(ss_norm, 1)
        for n in range(12):
            t = pe.transpose(BT[:, n * NS:(n + 1) * NS], ss[:, n // G, n % G, 0:NK], ident[0:NS, 0:NS])
        t.then_inc(pts_tr, 1)
        pe.wait_ge(nv_out, 1)
        pe.wait_ge(pts_out, 1)

        def gather(b):
            pe.wait_ge(vs_out, b + 1)
            for c in range(2):
                t = pe.matmul(BO[:, c * NS + b:c * NS + b + 1], mk[:, b % 2, c * P:(c + 1) * P], ones[0:HG, 0:1],
                              start=False, stop=(b == NS - 1 and c == 1), skip_group_check=True)
            return t

        for c in range(2):
            pe.matmul(BO[:, c * NS:(c + 1) * NS], nv8[:, c * P:(c + 1) * P], ident[0:NS, 0:NS],
                      start=(c == 0), stop=False, skip_group_check=True)
        for b in range(NS):
            pe.wait_ge(vs_in[b % 2], 48 * (b // 2 + 1))
            if b >= 2:
                gather(b - 2)
            for g in range(G):
                t = pe.matmul((BS, BA)[b % 2][0:HG, 0:256], pTs[:, g, b, :], v_s[:, b % 2, g * 256:(g + 1) * 256],
                              start=(g == 0), stop=(g == G - 1))
            t.then_inc(vs_mm, 1)
        gather(NS - 2)
        gather(NS - 1).then_inc(oTs_mm, 1)
        pe.wait_ge(x_free, C_M + 1)
        pe.wait_ge(y_free, C_M + 1)
        for k in range(4):
            pe.transpose(X[0:23, 0, k * P:(k + 1) * P], pT[:, k, TP - 15:T], ident)
        for k in range(4):
            t = pe.transpose(X[0:10, 1, k * P:(k + 1) * P], utail[:, k, :], ident)
        t.then_inc(ptail_tr, 1)
        pe.wait_ge(grp_in, 16)
        pe.wait_ge(ptail_out, 2)
        for i in range(4):
            pe.wait_ge(pool_done, i + 1)
            if i >= 2:
                pe.wait_ge(grp_out, i - 1)
            for hf in range(2):
                t = pe.matmul(PAIR[i % 2][:, hf, 0:HALF], w_grp[:, i, :], half(pT[:, i, :], hf), start=True, stop=True)
            t.then_inc(grp_mm, 1)
        pe.wait_ge(grp_out, 4)
        with pe.Fori(0, KD) as it:
            def mods(j):
                ada_unit(Unit(U_M, 16, it, M_ADA[j]), it + 8, j)

            chunk(U_M, 16, it, M_GATE[0], X, x_free, it * 3 + C_M, between=lambda: mods(0), apart=2)
            mods(1)
            chunk(U_M, 16, it, M_GATE[2], Y, y_free, it * 3 + C_M, between=lambda: (mods(2), mods(3)), apart=3)
            mods(4)
            chunk(U_M, 16, it, M_GATE[4], X, x_free, it * 3 + (C_M + 1), between=lambda: mods(5), apart=2)
            mods(6)
            pe.wait_ge(b_lo, 10)

            def branch(u, pair, fr, before, w0, k0, n):
                pe.wait_ge(fr, before + 1)
                for hf in range(2):
                    for k in range(n):
                        t = three(pair[:, hf, 0:HALF], u, (w0 + k) * P, half(bH[:, k0 + k, :], hf), half(bL[:, k0 + k, :], hf),
                                  k == 0, k == n - 1)
                return t

            u = Unit(U_M, 16, it, M_BR)
            ready(u)
            branch(u, Y, y_free, it * 3 + (C_M + 1), 0, 0, 4).then_inc(br_mm, 1)
            branch(u, X, x_free, it * 3 + (C_M + 2), 4, 4, 2).then_inc(w_used, 1)
            mods(7)
            u = Unit(U_M, 16, it, M_CONV)
            ready(u)
            branch(u, Y, y_free, it * 3 + (C_M + 2), 0, 6, 4).then_inc(w_used, 1)
            turn_mods(it + 8)
        with pe.Fori(0, 8) as it:
            chunk(U_O, 4, it, 0, X, x_free, it + C_O, split=m_lo)
            chunk(U_O, 4, it, 2, Y, y_free, it + C_O)

        def column_sums(src, done, last=True, first=True):
            for hf in range(2):
                t = pe.matmul(X[:, hf, 0:HALF], ones, half(src, hf), start=first, stop=last, skip_group_check=True)
            t.then_inc(done, 1)

        pe.wait_ge(sacc_done, 1)
        pe.wait_ge(x_free, C_F0 + 1)
        column_sums(sacc, rbn_mm)
        pe.wait_ge(rt2, 1)
        for k in range(KD):
            pe.wait_ge(sq_in, k + 1)
            column_sums(sqc[:, k % 2, :], sq_mm, k == KD - 1, k == 0)
        pe.wait_ge(rt2, 2)

        def states(rnd):
            pe.wait_ge(st_in, rnd * 32 + 32)
            pe.sem_inc(st_seen, 1)
            for v in range(2):
                for k in range(4):
                    n = (v * 4 + k) * 16
                    t = pe.transpose(BO[:, n:n + 16], st_rows[:, v, k * P:(k + 1) * P], ident[0:16, 0:16])
            t.then_inc(st_tr, 1)

        def tails(rnd4):
            pe.wait_ge(us_c, rnd4 * 2 + 2)
            pe.wait_ge(tail_out, rnd4 + 1)
            for v in range(2):
                t = pe.transpose(BA[0:10, v * P:(v + 1) * P], us[:, v, TP - 2:T], ident)
            t.then_inc(tail_tr, 1)

        def up(base, per, it, l0, rnd4, split=None, lag=1, gate_between=None, val_between=None):
            chunk(base, per, it, l0, X, x_free, CF(rnd4), between=gate_between, split=split, lag=lag)
            chunk(base, per, it, l0 + 2, Y, y_free, CF(rnd4), between=val_between)

        def down(base, per, it, l0, rnd):
            pe.wait_ge(f_lo, rnd * 4 + 4)
            for l in range(8):
                u = Unit(base, per, it, l0 + l)
                ready(u)
                for i in range(2):
                    pe.wait_ge(down_out, (rnd * KD) * 2 + (2 * (2 * l + i) + 2))
                    for hf, bank in enumerate(((BA, BT), (BS, BO))[i]):
                        for k in range(FPR):
                            t = three(bank[:, 0:HALF], u, (2 * k + i) * P, half(fH[:, k, :], hf), half(fL[:, k, :], hf),
                                      k == 0, k == FPR - 1)
                    t.then_inc(w_used if i else down_mm, 1)

        states(0)
        for p in range(FPR):
            up(U_F0, 16, 0, 4 * p, p, split=None if p else h2_lo, lag=2, gate_between=(lambda: tails(p - 1)) if p else None)
        with pe.Fori(0, 10) as it:
            r4 = it * 4 + 4

            def next_states():
                pe.wait_ge(st_out, it + 1)
                states(it + 1)

            up(U_F, 24, it, 0, r4, gate_between=lambda: tails(it * 4 + 3), val_between=next_states)
            pe.wait_ge(tail_out, it * 4 + 5)
            pe.wait_ge(st_out, it + 2)
            down(U_F, 24, it, 4, it)
            for p in range(1, FPR):
                def before_pair():
                    if p == 1:
                        pe.wait_ge(down_out, it * (2 * KD) + (2 * KD + 4))
                    tails(r4 + (p - 1))

                up(U_F, 24, it, 8 + 4 * p, r4 + p, gate_between=before_pair)
        tails(4 * ROUNDS - 1)
        pe.wait_ge(tail_out, 4 * ROUNDS + 1)
        down(U_END, 8, 0, 0, ROUNDS - 1)
        pe.wait_ge(x_free, C_F + 40 + 1)
        pe.wait_ge(sqf_used, KD)
        column_sums(fsum, sqf_mm)
        pe.wait_ge(rt3, 1)
        pe.wait_ge(down_out, 2 * ROUNDS * KD + 4)
        for n, (q, b) in enumerate(Y_TILES):
            if b == 0:
                pe.wait_ge(y_done, 4 * q + 4)
            if q and b < NB:
                pe.wait_ge(y_nat, n - NB)
            for i in range(4):
                if b < NB:
                    t = pe.transpose((BA, BT, BS, BO)[b][:, i * P:(i + 1) * P], x1[:, 4 * q + i, b * P:(b + 1) * P], ident)
                else:
                    t = pe.transpose(PAIR[q // 2][0:NS, q % 2, i * P:(i + 1) * P], x1[:, 4 * q + i, SA], ident)
            t.then_inc(y_tr, 1)

    with nc.Block() as block:
        block.sync(sync_program)
        block.gpsimd(pool_program)
        block.scalar(scalar_program)
        block.vector(vector_program)
        block.tensor(tensor_program)


INS = ["x_prompt", "x_sample", "c_prompt", "c_sample", "cache_kv_w128", "cache_kv_w512", "cache_kv_w2048",
       "state_pool", "state_conv", "state_ffn_conv", "rel_bias", "norm_g", "w_ada", "b_ada", "w_in", "w_attn_br",
       "w_pool_grp", "pool_scale", "w_pool_br", "conv_w", "w_conv_br", "w_o", "w_up", "ffn_conv_w", "w_down"]
OUTS = [("y_p", (1, TP, D)), ("y_s", (NS, 1, D)),
        ("kv128_p", (1, 1, 128, 2, HG, DH)), ("kv512_p", (1, 1, 512, 2, HG, DH)), ("kv2048_p", (1, 1, 512, 2, HG, DH)),
        ("pool_p", (1, 1, 15, PW)), ("conv_p", (1, 1, 2, CC)), ("ffn_p", (1, 1, 2, 2 * DFF)),
        ("kv128_s", (1, NS, 1, 2, HG, DH)), ("kv512_s", (1, NS, 1, 2, HG, DH)), ("kv2048_s", (1, NS, 1, 2, HG, DH)),
        ("pool_s", (1, NS, 15, PW)), ("conv_s", (1, NS, 2, CC)), ("ffn_s", (1, NS, 2, 2 * DFF))]


def kernel(**inputs):
    import concourse.bacc as bacc
    from concourse.bass_utils import run_bass_kernel_spmd

    nc = bacc.Bacc("TRN2", target_bir_lowering=False, num_devices=1, dynamic_dma_scratch_size=4096)
    arrays, ins, outs = {}, {}, {}
    for name, x in [(n, inputs[n]) for n in INS] + list(constants().items()):
        x = np.ascontiguousarray(x)
        arrays[f"in_{name}"] = x
        ins[name] = nc.dram_tensor(f"in_{name}", x.shape, mybir.dt.from_np(x.dtype), kind="ExternalInput").ap()
    for name, shape in OUTS:
        outs[name] = nc.dram_tensor(f"out_{name}", shape, F32, kind="ExternalOutput").ap()
    layer(nc, ins, outs)
    r = run_bass_kernel_spmd(nc, [arrays], core_ids=[0])
    return tuple(r.results[0][f"out_{name}"] for name, _ in OUTS)
```

```python
import math
import numpy as np
import concourse.bass as bass
from concourse import mybir

F32 = mybir.dt.float32
F32R = mybir.dt.float32r
ALU = mybir.AluOpType
ACT = mybir.ActivationFunctionType
AX = mybir.AxisListType
P = 128

D = 2048
KD = D // P
TP, NS = 512, 8
T = TP + NS
HALF = T // 2
NB = TP // P
G, HG, DH = 3, 4, 64
DIL = (1, 4, 16)
NK = 128
AW = G * HG * DH
QCH = AW // P
PW, CC = 512, 512
WIN = (2, 4, 8, 16)
DFF = 5632
FCH = DFF // P
ROUNDS, FPR = FCH // 4, 4
SCALE = DH ** -0.5
EPS = 1e-6
NEG = -1e30
RW = 5 * P
BW = RW + NK + 1
COL_P, COL_B, COL_C, COL_H, COL_G = 3 * AW, 3 * AW + PW, 3 * AW + PW + CC, 3 * AW + PW + 2 * CC, 3 * AW + PW + 3 * CC
PR, SA = slice(0, TP), slice(TP, T)
RAW = 4
SPLIT = (2, 4)
ADA_PARTS = (0, 2, 4, 6, 8)
UNIT = 8 * P

U_ADA, N_ADA = 0, 8
U_QKV = U_ADA + 8 * N_ADA
U_PC = U_QKV + 9 * 4
U_M = U_PC + 2 * 16
U_O = U_M + 16 * 16
U_F0 = U_O + 8 * 4
U_F = U_F0 + 16
U_END = U_F + 10 * 24
UNITS = U_END + 8
M_GATE, M_ADA, M_BR, M_CONV = (0, 2, 4, 7, 9, 11), (1, 3, 5, 6, 8, 10, 12, 14), 13, 15
C_QKV, C_PC, C_M, C_O, C_F0, C_F = 0, 9, 17, 65, 73, 77


def constants():
    n = np.arange(NK + 1)
    onehot = np.zeros((33, G, BW), np.float32)
    for g, d in enumerate(DIL):
        dist = n * d
        large = 16 + (np.log(np.maximum(dist, 1) / 16) / math.log(2048 / 16) * 16).astype(np.int32)
        bucket = np.where(dist < 16, dist, np.minimum(large, 31))
        for y in range(RW):
            delta = TP - 1 - y
            if delta >= 0 and delta % d == 0 and delta // d <= NK:
                onehot[bucket[delta // d], g, y] = 1
            else:
                onehot[32, g, y] = NEG
        for i in range(NK + 1):
            onehot[bucket[NK - i if i < NK else 0], g, RW + i] = 1
    sel = np.zeros((19, 9), np.float32)
    for i in range(9):
        sel[i, i] = sel[9 + i, i] = 1
    sel[18] = 1
    heads = np.zeros((HG, HG * DH), np.float32)
    for h in range(HG):
        heads[h, h * DH:(h + 1) * DH] = 1
    counts = np.zeros((P, 4, 16), np.float32)
    for i, w in enumerate(WIN):
        counts[:, i] = (1.0 / np.minimum(np.arange(16) + 1, w)).astype(np.float32)
    return {"ident": np.eye(P, dtype=np.float32), "onehot": onehot, "sel": sel, "heads": heads, "counts": counts}


class Step:

    def __init__(self, eng, sem):
        self.eng, self.sem, self.base, self.it, self.per, self.k = eng, sem, 0, 0, 0, 0

    def enter(self, it, per):
        self.base, self.it, self.per, self.k = self.base + self.k, it, per, 0

    def leave(self, times):
        assert self.k == self.per, ("steps of the loop's body", self.k)
        self.base, self.it, self.per, self.k = self.base + self.per * times, 0, 0, 0

    def __call__(self, ins):
        ins.then_inc(self.sem, 1)
        self.k += 1

    def settle(self, but=0):
        self.eng.wait_ge(self.sem, self.it * self.per + (self.base + self.k - but))


class Unit:

    def __init__(self, base, per, it, l):
        self.n = it * per + (base + l)
        self.raw = (base + l) % RAW
        first = base == U_M and isinstance(it, int) and l < 18
        self.ring = SPLIT[(base < U_QKV or base >= U_M) and not first]
        self.spl = (base + l) % self.ring
        self.turn = it * (per // RAW) + (base + l) // RAW

    raw_free = property(lambda s: s.n + 1)
    arrived = property(lambda s: s.turn * 16 + 16)
    spl_free = property(lambda s: s.n + 3 - s.ring)
    hi_done = property(lambda s: s.n + 1)
    lo_done = property(lambda s: s.n + 5)
    used = property(lambda s: s.n + 3)


def layer(nc, a, out):
    at = {"top": -(-nc.sbuf_base // 32) * 32}

    def place(name, shape, dt=F32, off=None):
        size = int(np.prod(shape[1:])) * 4
        o = at["top"] if off is None else off
        if off is None:
            at["top"] += -(-size // 32) * 32
        return nc.alloc_sbuf_tensor_at(name, shape, dt, offset=o).ap()

    def region(start, *items):
        o, made = start, []
        for name, shape, dt in items:
            made.append(place(name, shape, dt, off=o))
            o += -(-int(np.prod(shape[1:])) * 4 // 32) * 32
        return made, o

    ident = place("ident", [P, P])
    ones = place("ones", [P, P])
    sel = place("sel", [19, 9])
    heads_mask = place("heads_mask", [HG, HG * DH])
    counts = place("counts", [P, 4, 16])
    eps = place("eps", [P, 1])
    cols = place("cols", [P, 80])
    ffn_w = place("ffn_w", [P, 3, 2 * FCH])
    st_conv = place("st_conv", [P, 4, NS, 2])
    st_pool = place("st_pool", [P, 4, NS, 15])
    mods = place("mods", [P, 6 * KD, 9])
    coef = place("coef", [P, KD, 9])
    cT = place("cT", [P, KD, 18], F32R)
    mod_rows = place("mod_rows", [19, 512])
    raw = place("raw", [P, RAW, UNIT])
    whi, wlo = ([place(f"{n}{i}", [P, UNIT], F32R) for i in range(2)] for n in ("whi", "wlo"))
    H0 = at["top"]
    hH = place("hH", [P, KD, T], F32R)
    hL = place("hL", [P, KD, T], F32R)
    L0 = at["top"]
    (xN, xs, cc, sqj), e = region(H0, ("xN", [P, NB, D], F32), ("xs", [NS, D], F32), ("cc", [9, D], F32), ("sqj", [P, D], F32))
    assert e <= L0
    (xr, rb, rows1, rowsF, rowsC, rowsP, relb, onehot, brows, ssq, rs, diag, xT), end0 = region(
        L0, ("xr", [P, KD, T], F32), ("rb", [P, T], F32),
        ("rows1", [80, P], F32), ("rowsF", [88, 3, P], F32), ("rowsC", [16, CC], F32), ("rowsP", [120, PW], F32),
        ("relb", [33, 12], F32), ("onehot_s", [33, G, BW], F32), ("brows", [HG, G, BW], F32),
        ("ssq", [P, 5], F32), ("rs", [P, 5], F32), ("diag", [P, 5, P], F32), ("xT", [P, KD, T], F32))
    csig = sqj[0:9, :]
    (ns, vn, qk, stage, qB), e1 = region(
        L0, ("ns", [NS, 3 * AW], F32), ("vn", [P, G, NB, 256], F32),
        ("qk", [P, 2 * QCH, TP], F32), ("stage", [P, 2, T], F32), ("qB", [P, 2, AW], F32))
    (u_bias, sc_p, pT_t, q2, osb), e2 = region(
        e1, ("u_bias", [P, 2, 5 * 256], F32), ("scores", [P, 5 * 256], F32), ("probsT", [P, 10, P], F32),
        ("q2", [P, 2, G, P], F32), ("osb", [P, 2, DH], F32))
    (cS, sc_s, k_s, mx, nm, ls, rl, utail), e3 = region(
        e2, ("cS", [P, T], F32), ("sc_s", [P, NS, 12], F32), ("k_s", [P, 2, AW], F32),
        ("mx", [P, 2], F32), ("nm", [P, 2], F32), ("ls", [P, 2], F32), ("rl", [P, 2], F32), ("utail", [P, 4, 10], F32))
    (pT, bcv, aT), e = region(e3, ("pT", [P, 4, T], F32), ("bcv", [P, 4, T], F32), ("aT", [P, 2, T], F32))
    (kn,), e_ = region(e3 + 4 * T * 4, ("kn", [P, G, NB, 256], F32))
    uS, yS = stage[:, 0, :], stage[:, 1, :]
    LIM = nc.sbuf_usable_end
    assert max(e, e_) <= LIM and end0 <= LIM, (L0, e, e_, end0, LIM)
    (ss, bS, n8, smx, sls, srl, t8, nv8, pTs, mk, w_grp), e = region(
        e1, ("ss", [NS, HG, G, NK + 1], F32), ("bS", [NS, HG * G, NK + 1], F32), ("n8", [NS, 12], F32),
        ("smx", [NS, HG], F32), ("sls", [NS, HG], F32), ("srl", [NS, HG], F32),
        ("t8", [NS, AW], F32), ("nv8", [NS, 256], F32), ("pTs", [P, G, NS, HG], F32), ("mk", [HG, 2, 256], F32),
        ("w_grp", [P, 4, P], F32))
    assert e <= e2, (e, e2)
    v_s = k_s
    (t_tails,), e = region(e1 - 2 * AW * 4, ("t_tails", [23, 2, 512], F32))
    assert e <= e1
    (merged,), e = region(L0, ("merged", [P, KD, T], F32))
    (sg, mt), e = region(e, ("sg", [P, 3, T], F32), ("mt", [P, 2, T], F32))
    (bH, bL), eM = region(e, ("bH", [P, 10, T], F32R), ("bL", [P, 10, T], F32R))
    assert eM <= e3, (eM, e3)
    mixT = merged
    WM = (LIM - 4 * UNIT * 4) // 32 * 32
    more, e = region(WM, *[(f"{n}{i}", [P, UNIT], F32R) for n in ("whi", "wlo") for i in (2, 3)])
    assert max(eM, end0) <= WM and e <= LIM, (eM, end0, WM)
    whi, wlo = whi + more[:2], wlo + more[2:]
    (xR, sacc, rbn, sqc), eO = region(L0 + KD * T * 4, ("xR", [P, KD, T], F32), ("sacc", [P, T], F32), ("rbn", [P, T], F32), ("sqc", [P, 2, T], F32))
    (acc, fH, fL, us, cv, ft, sqf, rsf, fsum), eF = region(
        L0, ("acc", [P, KD, T], F32), ("fH", [P, FPR, T], F32R), ("fL", [P, FPR, T], F32R),
        ("us", [P, 2, T], F32), ("cv", [P, 2, T], F32), ("ft", [P, T], F32),
        ("sqf", [P, 2, T], F32), ("rsf", [P, 5], F32), ("fsum", [P, T], F32))
    assert max(eF, eO) <= WM, (eF, eO, WM)
    (fc, yN), e = region(H0, ("fc", [P, KD, T], F32), ("yN", [P, 4, NB, 512], F32))
    (yNs, trow, st_rows, st_f), e_ = region(
        max(eO, eF), ("yNs", [NS, D], F32), ("trow", [10, 2, 512], F32), ("st_rows", [16, 2, 512], F32),
        ("st_f", [P, 2, 4, NS, 2], F32))
    assert e_ <= WM
    assert e <= L0

    X = nc.alloc_psum_tensor("X", [P, 2, 512], F32).ap()
    Y = nc.alloc_psum_tensor("Y", [P, 2, 512], F32).ap()
    BA = nc.alloc_psum_tensor("BA", [P, 512], F32).ap()
    BT = nc.alloc_psum_tensor("BT", [P, 512], F32).ap()
    BS = nc.alloc_psum_tensor("BS", [P, 512], F32).ap()
    BO = nc.alloc_psum_tensor("BO", [P, 512], F32).ap()
    PAIR = (X, Y)
    half = lambda t, h: t[:, h * HALF:(h + 1) * HALF]

    d_x = nc.dram_tensor("d_x", (P, KD * T), F32, kind="Internal").ap()
    d_x1 = nc.dram_tensor("d_x1", (TP, D), F32, kind="Internal").ap()
    d_bias = nc.dram_tensor("d_bias", (HG, G, BW), F32, kind="Internal").ap()
    d_table = nc.dram_tensor("d_table", (HG, P, G, RW), F32, kind="Internal").ap()
    d_q = nc.dram_tensor("d_q", (NS, AW), F32, kind="Internal").ap()

    sem = nc.alloc_semaphore

    def named(*names):
        return (sem(n) for n in names)

    w_raw = [sem(f"w_raw{i}") for i in range(RAW)]
    w_hi, w_lo, w_used, w_attn, branch_turn = named("w_hi", "w_lo", "w_used", "w_attn", "branch_turn")
    x_free, y_free = free = tuple(named("x_free", "y_free"))
    dve_step, = named("dve_step")
    c_in, k_in, x_in, row_in, bias_in, set_up = named("c_in", "k_in", "x_in", "row_in", "bias_in", "set_up")
    silu, c_tr, c_split, par_tr, par_out, b_mm, b_out = named("silu", "c_tr", "c_split", "par_tr", "par_out", "b_mm", "b_out")
    x_tr, x_out, ssq_done, rt_done, diag_done, rb_mm, rb_done = named(
        "x_tr", "x_out", "ssq_done", "rt_done", "diag_done", "rb_mm", "rb_done")
    mod_row, mod_bias, mod_tr, mod_out = named("mod_row", "mod_bias", "mod_tr", "mod_out")
    h_pre, h_hi, h_lo, bias_st, table_st, xT_st = named("h_pre", "h_hi", "h_lo", "bias_st", "table_st", "xT_st")
    nat_tr, qk_out, nat_out, q_st, k_st, v_st, out_st = named("nat_tr", "qk_out", "nat_out", "q_st", "k_st", "v_st", "out_st")
    u_in, u_used, q2_in, s_mm, s_soft, s_exp, p_tr, p_out, o_mm, o_out, oT_tr, oT_out = named(
        "u_in", "u_used", "q2_in", "s_mm", "s_soft", "s_exp", "p_tr", "p_out", "o_mm", "o_out", "oT_tr", "oT_out")
    c_cp, ks_used = named("c_cp", "ks_used")
    qB_in, ks_in, vs_in = ([sem(f"{n}{i}") for i in range(2)] for n in ("qB_in", "ks_in", "vs_in"))
    bS_in, ss_tr, ss_max, ss_exp, ss_norm, pts_tr, pts_out, vs_mm, vs_out, nv_out, oTs_mm, oTs_out = named(
        "bS_in", "ss_tr", "ss_max", "ss_exp", "ss_norm", "pts_tr", "pts_out", "vs_mm", "vs_out", "nv_out", "oTs_mm", "oTs_out")
    ptail_tr, ptail_out, pool_done, grp_in, grp_mm, grp_out, b_hi, b_lo = named(
        "ptail_tr", "ptail_out", "pool_done", "grp_in", "grp_mm", "grp_out", "b_hi", "b_lo")
    br_mm, br_out, m_hi, m_lo, mix_out, sacc_done, rbn_mm, rt2 = named(
        "br_mm", "br_out", "m_hi", "m_lo", "mix_out", "sacc_done", "rbn_mm", "rt2")
    x_back, x1_done, sq_in, sq_mm, h2_pre, h2_hi, h2_lo = named("x_back", "x1_done", "sq_in", "sq_mm", "h2_pre", "h2_hi", "h2_lo")
    st_in, st_tr, st_seen, st_out, us_c, cv_done, gelu_done, f_done, f_hi, f_lo = named(
        "st_in", "st_tr", "st_seen", "st_out", "us_c", "cv_done", "gelu_done", "f_done", "f_hi", "f_lo")
    tail_tr, tail_out, tail_st, tail_free, down_mm, down_out = named(
        "tail_tr", "tail_out", "tail_st", "tail_free", "down_mm", "down_out")
    x1_tr, x1_nat, x1_st, x1_st_last, x1_back, sqf_in, sqf_used, sqf_mm, rt3 = named(
        "x1_tr", "x1_nat", "x1_st", "x1_st_last", "x1_back", "sqf_in", "sqf_used", "sqf_mm", "rt3")
    fc_done, fcs_done, y_tr, y_nat, y_st = named("fc_done", "fcs_done", "y_tr", "y_nat", "y_st")

    kview = lambda w: w.rearrange("(k p) n -> p k n", p=P)
    w_ada, w_in, w_o, w_up = (kview(a[n][0]) for n in ("w_ada", "w_in", "w_o", "w_up"))
    w_pool_br, w_conv_br, w_attn_br = (kview(a[n][0]) for n in ("w_pool_br", "w_conv_br", "w_attn_br"))

    def sync_program(sp):
        def load(u, dst, src, free=False):
            if not free:
                sp.wait_ge(w_lo, u.raw_free)
            sp.dma_start(dst, src).then_inc(w_raw[u.raw], 16)

        def slab(u, w, k0, col, k=8, width=P, off=0, free=False):
            dst = raw[:, u.raw, off * P:(off + k * width // P) * P].rearrange("p (k n) -> p k n", n=width)
            load(u, dst, w[:, k0:k0 + k, bass.ds(col, width)], free)

        def ada_unit(u, tile, j):
            slab(u, w_ada, 2 * j, tile * 512, k=2, width=512)

        sp.dma_start(ident, a["ident"]).then_inc(c_in, 16)
        sp.dma_start(cc[0:1, :], a["c_prompt"]).then_inc(c_in, 16)
        sp.dma_start(cc[1:9, :], a["c_sample"]).then_inc(c_in, 16)
        with sp.Fori(0, 8) as it:
            for l in range(8):
                ada_unit(Unit(U_ADA, 8, it, l), it, l)
        with sp.Fori(0, 9) as it:
            for l in range(4):
                slab(Unit(U_QKV, 4, it, l), w_in, 8 * (l % 2), it * 256 + l // 2 * P)
        with sp.Fori(0, 2) as it:
            for c, col in enumerate((COL_P, COL_P + P, COL_C, COL_H, COL_B, COL_C + P, COL_H + P, COL_B + P)):
                for l in range(2):
                    slab(Unit(U_PC, 16, it, 2 * c + l), w_in, 8 * l, it * 256 + col)
        with sp.Fori(0, KD) as it:
            for l in range(13):
                if l in M_GATE:
                    slab(Unit(U_M, 16, it, l), w_in, 8 * (M_GATE.index(l) % 2), it * P + (COL_G + M_GATE.index(l) // 2 * D))
                else:
                    ada_unit(Unit(U_M, 16, it, l), it + 8, M_ADA.index(l))
            u = Unit(U_M, 16, it, M_BR)
            sp.wait_ge(w_lo, u.raw_free)
            sp.sem_inc(branch_turn, 1)
            slab(u, w_pool_br, 0, it * P, k=4, free=True)
            sp.dma_start(raw[:, u.raw, 4 * P:6 * P].rearrange("p (k n) -> p k n", n=P),
                         w_attn_br[:, 0:2, bass.ds(it * P, P)]).then_inc(w_attn, 16)
            ada_unit(Unit(U_M, 16, it, 14), it + 8, 7)
            slab(Unit(U_M, 16, it, M_CONV), w_conv_br, 0, it * P, k=4)
        with sp.Fori(0, 8) as it:
            for l in range(4):
                slab(Unit(U_O, 4, it, l), w_o, 8 * (l % 2), it * 256 + l // 2 * P)

        def up(base, per, it, l0, rnd, pair):
            for l in range(4):
                slab(Unit(base, per, it, l0 + l), w_up, 8 * (l % 2), rnd * 512 + (pair * P + l // 2 * DFF))

        def down(base, per, it, l0, rnd):
            rows = a["w_down"][0].rearrange("(r k p) n -> r p k n", p=P, k=FPR)
            for l in range(8):
                u = Unit(base, per, it, l0 + l)
                load(u, raw[:, u.raw, :].rearrange("p (k n) -> p k n", n=256),
                     rows[bass.ds(rnd, 1), :, :, l * 256:(l + 1) * 256].rearrange("r p k n -> (r p) k n"))

        for pair in range(FPR):
            up(U_F0, 16, 0, 4 * pair, 0, pair)
        with sp.Fori(0, 10) as it:
            up(U_F, 24, it, 0, it + 1, 0)
            down(U_F, 24, it, 4, it)
            for pair in range(1, FPR):
                up(U_F, 24, it, 8 + 4 * pair, it + 1, pair)
        down(U_END, 8, 0, 0, ROUNDS - 1)
        for n, (q, b) in enumerate(Y_TILES):
            sp.wait_ge(y_nat, n + 1)
            if b < NB:
                sp.dma_start(out["y_p"][0, b * P:(b + 1) * P, q * 512:(q + 1) * 512],
                             yN[:, q, b, :]).then_inc(y_st, 16)
            elif q == 3:
                sp.dma_start(out["y_s"].rearrange("b t n -> (b t) n"), yNs).then_inc(y_st, 16)
        sp.wait_ge(y_st, 16 * (4 * NB + 1))

    def pool_program(gp):
        gp.dma_start(sel, a["sel"]).then_inc(k_in, 16)

        def mod_bias_row(tile):
            gp.dma_start(mod_rows[18:19, :], a["b_ada"][0:1, bass.ds(tile * 512, 512)]).then_inc(mod_bias, 16)

        def next_bias_rows(first, last):
            with gp.Fori(first, last) as it:
                gp.wait_ge(mod_tr, it + 2)
                mod_bias_row(it + 1)

        mod_bias_row(0)
        gp.dma_start(rows1[0:64, :], a["norm_g"][0].rearrange("n (k p) -> (n k) p", p=P)).then_inc(row_in, 16)
        gp.dma_start(rows1[64:76, :], a["conv_w"][0].rearrange("n (k p) -> (n k) p", p=P)).then_inc(row_in, 16)
        gp.dma_start(rows1[76:80, :], a["pool_scale"][0].rearrange("(k p) -> k p", p=P)).then_inc(row_in, 16)
        gp.dma_start(rowsF, a["ffn_conv_w"][0].rearrange("t (k p) -> k t p", p=P)).then_inc(row_in, 16)
        gp.dma_start(rowsC, a["state_conv"][0].rearrange("b r n -> (b r) n")).then_inc(row_in, 16)
        gp.dma_start(rowsP, a["state_pool"][0].rearrange("b r n -> (b r) n")).then_inc(row_in, 16)
        gp.wait_ge(set_up, 1)
        gp.dma_start(relb[0:32, :], a["rel_bias"]).then_inc(bias_in, 16)
        gp.dma_start(onehot, a["onehot"]).then_inc(bias_in, 16)
        next_bias_rows(0, 1)
        for b in range(NB):
            gp.dma_start(xN[:, b, :], a["x_prompt"][0, b * P:(b + 1) * P, :]).then_inc(x_in, 16)
        gp.dma_start(xs, a["x_sample"].rearrange("b t n -> (b t) n")).then_inc(x_in, 16)
        gp.dma_start(heads_mask, a["heads"]).then_inc(k_in, 16)
        gp.dma_start(counts, a["counts"]).then_inc(k_in, 16)
        next_bias_rows(1, 7)
        gp.wait_ge(mod_tr, 9)
        gp.wait_ge(b_out, 6)
        gp.dma_start(d_bias, brows).then_inc(bias_st, 16)
        gp.wait_ge(x_out, 17)
        gp.dma_start(d_x, xT.rearrange("p k t -> p (k t)")).then_inc(xT_st, 16)
        gp.wait_ge(bias_st, 16)
        for h in range(HG):
            gp.dma_start(d_table[h], d_bias[h, :, 0:RW].unsqueeze(0).to_broadcast([P, G, RW])).then_inc(table_st, 16)
        gp.dma_start(out["pool_s"][0, :, 0:14, :], a["state_pool"][0, :, 1:15, :]).then_inc(out_st, 16)
        gp.dma_start(out["conv_s"][0, :, 0, :], a["state_conv"][0, :, 1, :]).then_inc(out_st, 16)
        gp.dma_start(out["ffn_s"][0, :, 0, :], a["state_ffn_conv"][0, :, 1, :]).then_inc(out_st, 16)
        gp.wait_ge(nat_out, QCH + 2)
        gp.dma_start(d_q, ns[:, 0:AW]).then_inc(q_st, 16)
        caches = [a[n] for n in ("cache_kv_w128", "cache_kv_w512", "cache_kv_w2048")]

        def cache_rows(dst, b, kv, done):
            for g in range(G):
                rows = caches[g][0].rearrange("b (i d) v h e -> b i d v (h e)", d=DIL[g])[b, :, 0, kv, :]
                gp.dma_start(dst[:, g * 256:(g + 1) * 256], rows).then_inc(done, 16)

        def bias_tables(pair):
            for h in range(2):
                for g0, n, w, c in ((0, 1, 256, 0), (1, 2, 512, 256)):
                    rows = bass.AP(d_table.tensor, (2 * pair + h) * P * G * RW + g0 * RW + P - 1 + 512 - w,
                                   [[G * RW - 1, P], [RW, n], [1, w]])
                    gp.dma_start(u_bias[:, h, c:c + n * w].rearrange("p (g n) -> p g n", n=w), rows).then_inc(u_in, 16)

        def sample_keys(b):
            gp.dma_start(qB[:, b % 2, :], d_q[b:b + 1, :].to_broadcast([P, AW])).then_inc(qB_in[b % 2], 16)
            cache_rows(k_s[:, b % 2, :], b, 0, ks_in[b % 2])

        gp.wait_ge(table_st, 16 * HG)
        gp.wait_ge(xT_st, 16)
        bias_tables(0)
        gp.wait_ge(q_st, 16)
        sample_keys(0)
        sample_keys(1)
        gp.wait_ge(nat_out, 2 * QCH + 2)
        for g, name in enumerate(("kv128_p", "kv512_p", "kv2048_p")):
            store_kv(gp, kn, 0, g, name)
            gp.dma_start(out[name[:-1] + "s"][0, :, 0, 0, :, :].rearrange("b h d -> b (h d)"),
                         ns[:, AW + g * 256:AW + g * 256 + 256]).then_inc(k_st, 16)
        gp.wait_ge(nat_out, 3 * QCH + 2)
        for g, name in enumerate(("kv128_p", "kv512_p", "kv2048_p")):
            store_kv(gp, vn, 1, g, name)
            gp.dma_start(out[name[:-1] + "s"][0, :, 0, 1, :, :].rearrange("b h d -> b (h d)"),
                         ns[:, 2 * AW + g * 256:2 * AW + g * 256 + 256]).then_inc(v_st, 16)
        for b in range(2, NS):
            if b == 4:
                gp.wait_ge(u_used, 2)
                bias_tables(1)
            gp.wait_ge(ks_used, b + 1)
            sample_keys(b)
        gp.wait_ge(u_used, 3)
        gp.wait_ge(oT_out, 8)
        gp.dma_start(bS, d_bias[:, :, RW:BW].rearrange("h g n -> (h g) n").unsqueeze(0).to_broadcast([NS, HG * G, NK + 1])
                     ).then_inc(bS_in, 16)
        gp.dma_start(w_grp, a["w_pool_grp"][0].rearrange("g c e -> c g e")).then_inc(grp_in, 16)
        gp.wait_ge(ks_used, 10)
        for b in range(NS):
            if b >= 2:
                gp.wait_ge(vs_mm, b - 1)
            cache_rows(v_s[:, b % 2, :], b, 1, vs_in[b % 2])
        gp.wait_ge(ptail_out, 2)
        gp.dma_start(out["pool_p"][0, 0], t_tails[0:15, 0, :]).then_inc(out_st, 16)
        gp.dma_start(out["pool_s"][0, :, 14, :], t_tails[15:23, 0, :]).then_inc(out_st, 16)
        gp.dma_start(out["conv_p"][0, 0], t_tails[0:2, 1, :]).then_inc(out_st, 16)
        gp.dma_start(out["conv_s"][0, :, 1, :], t_tails[2:10, 1, :]).then_inc(out_st, 16)
        with gp.Fori(0, KD) as it:
            gp.wait_ge(mod_tr, it + 9)
            mod_bias_row(it + 8)
        gp.wait_ge(xT_st, 16)
        gp.wait_ge(w_used, Unit(U_M, 16, KD - 1, 15).used)
        gp.wait_ge(br_out, 3 * KD + 1)
        gp.dma_start(xR.rearrange("p k t -> p (k t)"), d_x).then_inc(x_back, 16)

        def state_rows(rnd):
            for v in range(2):
                gp.dma_start(st_rows[:, v, :], a["state_ffn_conv"][0, :, :, bass.ds(rnd * 512 + v * DFF, 512)]
                             .rearrange("b r n -> (b r) n")).then_inc(st_in, 16)

        state_rows(0)
        x1_rows = d_x1.rearrange("(b p) n -> p b n", p=P)
        for q in range(4):
            gp.wait_ge(x1_nat, (NB + 1) * (q + 1))
            gp.dma_start(x1_rows[:, :, q * 512:(q + 1) * 512], yN[:, q, :, :]).then_inc(x1_st_last if q == 3 else x1_st, 16)
        gp.wait_ge(x1_st, 48)
        gp.wait_ge(x1_st_last, 16)

        def store_tails(rnd):
            for v in range(2):
                col = bass.ds(rnd * 512 + v * DFF, 512)
                gp.dma_start(out["ffn_p"][0, 0, :, col], trow[0:2, v, :]).then_inc(tail_st, 16)
                gp.dma_start(out["ffn_s"][0, :, 1, col], trow[2:10, v, :]).then_inc(tail_st, 16)

        with gp.Fori(0, 10) as it:
            gp.wait_ge(st_tr, it + 1)
            state_rows(it + 1)
            gp.wait_ge(tail_out, it * 4 + 5)
            store_tails(it)
            gp.wait_ge(tail_st, it * 64 + 64)
            gp.sem_inc(tail_free, 4)
        gp.wait_ge(tail_out, 4 * ROUNDS + 1)
        store_tails(ROUNDS - 1)
        gp.wait_ge(w_used, Unit(U_F, 24, 9, 23).used)
        for q in range(4):
            gp.dma_start(yN[:, q, :, :], x1_rows[:, :, q * 512:(q + 1) * 512]).then_inc(x1_back, 16)
        gp.wait_ge(out_st, 16 * 7)
        gp.wait_ge(k_st, 16 * 6)
        gp.wait_ge(v_st, 16 * 6)
        gp.wait_ge(tail_st, 16 * 4 * ROUNDS)

    def store_kv(gp, nat, kv, g, name):
        dst = out[name][0, 0, :, kv, :, :].rearrange("t h d -> t (h d)")
        if g == 0:
            gp.dma_start(dst, nat[:, g, NB - 1, :]).then_inc((k_st, v_st)[kv], 16)
        else:
            gp.dma_start(dst.rearrange("(b p) n -> p b n", p=P), nat[:, g, :, :]).then_inc((k_st, v_st)[kv], 16)

    def scalar_program(act):
        def hi(u, first=False):
            act.wait_ge(w_raw[u.raw], u.arrived)
            if not first:
                act.wait_ge(w_used, u.spl_free)
            nc.scalar.copy(whi[u.spl], raw[:, u.raw, :]).then_inc(w_hi, 1)

        def lead(base, per, it, l):
            hi(Unit(base, per, it, l + 2))

        act.wait_ge(c_in, 48)
        nc.scalar.activation(csig, cc, ACT.Sigmoid).then_inc(silu, 1)
        for l in range(2):
            hi(Unit(0, 0, 0, l), first=True)

        def tiles(part):
            with act.Fori(ADA_PARTS[part], ADA_PARTS[part + 1]) as it:
                for l in range(8):
                    lead(U_ADA, 8, it, l)
                act.wait_ge(w_used, Unit(U_ADA, 8, it, 7).used)
                act.wait_ge(mod_tr, it + 1)
                nc.scalar.copy(mod_rows[0:18, :], BA[0:18, :]).then_inc(mod_row, 1)

        def squares(blocks):
            for b in blocks:
                nc.scalar.activation(sqj, xN[:, b, :], ACT.Square, accum_out=ssq[:, b:b + 1]).then_inc(ssq_done, 1)
                act.wait_ge(ssq_done, b + 1)

        tiles(0)
        tiles(1)
        for i, (g, n0, n1) in enumerate(BIAS_MM):
            act.wait_ge(b_mm, i + 1)
            nc.scalar.copy(brows[:, g, n0:n1], BIAS_BANK[i][0:HG, 0:n1 - n0]).then_inc(b_out, 1)
        act.wait_ge(x_in, 16 * 5)
        act.wait_ge(c_tr, 1)
        squares((0, 1))
        tiles(2)
        squares((2, 3))
        nc.scalar.activation(sqj[0:NS, :], xs, ACT.Square, accum_out=ssq[0:NS, 4:5]).then_inc(ssq_done, 1)
        act.wait_ge(ssq_done, 5)
        act.wait_ge(set_up, 1)
        nc.scalar.activation(rs[:, 0:4], ssq[:, 0:4], ACT.Sqrt, bias=eps, scale=1.0 / D).then_inc(rt_done, 1)
        nc.scalar.activation(rs[0:NS, 4:5], ssq[0:NS, 4:5], ACT.Sqrt, bias=eps[0:NS], scale=1.0 / D).then_inc(rt_done, 1)
        act.wait_ge(x_tr, 17)
        act.wait_ge(rb_mm, 1)
        nc.scalar.copy(rb[:, :TP], X[:, 0, :]).then_inc(rb_done, 1)
        nc.scalar.copy(rb[:, TP:], X[:, 1, 0:NS]).then_inc(rb_done, 1)
        tiles(3)
        for k in range(KD):
            act.wait_ge(h_pre, k + 1)
            nc.scalar.copy(hH[:, k, :], xr[:, k, :]).then_inc(h_hi, 1)
        for part in range(3):
            with act.Fori(0, 3) as it:
                for l in range(4):
                    lead(U_QKV + 12 * part, 4, it, l)
                    if l % 2:
                        c = it * 2 + (l // 2 + 6 * part)
                        act.wait_ge(w_used, Unit(U_QKV + 12 * part, 4, it, l).used)
                        act.wait_ge(nat_tr, c + 1)
                        act.wait_ge(qk_out, c + 1)
                        act.copy(half(stage[:, l // 2, :], 0), PAIR[l // 2][:, 0, 0:HALF])
                        act.copy(half(stage[:, l // 2, :], 1), PAIR[l // 2][:, 1, 0:HALF]).then_inc(free[l // 2], 1)
        with act.Fori(0, 2) as it:
            for c in range(8):
                h, qb = c % 2, c // 2
                w0, w = min(qb + 1, 2) * P, (qb + 1) * P
                wide = w0 + 2 * w
                m = it * 8 + c
                act.wait_ge(s_soft, m + 1)
                act.wait_ge(o_out, m + 1)
                nc.scalar.activation(sc_p[:, 0:wide], sc_p[:, 0:wide], ACT.Exp, bias=nm[:, h:h + 1],
                                     accum_out=ls[:, h:h + 1]).then_inc(s_exp, 1)
                lead(U_PC, 16, it, 2 * c)
                act.wait_ge(p_tr, m + 1)
                nt = wide // P
                act.wait_ge(o_mm, m + 1)
                for i, bank in enumerate((BT, BS, BA)):
                    n = min(4, nt - 4 * i)
                    if n > 0:
                        ins = act.copy(pT_t[:, 4 * i:4 * i + n, :], bank[:, 0:n * P].rearrange("p (n q) -> p n q", q=P))
                ins.then_inc(p_out, 1)
                lead(U_PC, 16, it, 2 * c + 1)
                pair = PAIR[c % 2]
                act_chunk = (c < 2) or c in (2, 5)
                if act_chunk:
                    act.wait_ge(w_used, Unit(U_PC, 16, it, 2 * c + 1).used)
                if c < 2:
                    for hf in range(2):
                        dst = pT[:, bass.ds(it * 2 + c, 1), hf * HALF:(hf + 1) * HALF].rearrange("p k t -> p (k t)")
                        ins = act.copy(dst, pair[:, hf, 0:HALF])
                    ins.then_inc(free[c % 2], 1)
                if c in (2, 5):
                    act.wait_ge(c_cp, it * 2 + (1 if c == 2 else 2))
                    act.copy(half(cS, 0), pair[:, 0, 0:HALF])
                    act.copy(half(cS, 1), pair[:, 1, 0:HALF]).then_inc(free[c % 2], 1)
        def sample_exp():
            act.wait_ge(ss_max, 1)
            for h in range(HG):
                nc.scalar.activation(ss[:, h, :, :], ss[:, h, :, :], ACT.Exp, bias=smx[:, h:h + 1],
                                     accum_out=sls[:, h:h + 1]).then_inc(ss_exp, 1)

        def branch_hi():
            act.wait_ge(grp_out, 4)
            act.wait_ge(oTs_out, 1)
            act.wait_ge(out_st, 16 * 7)
            for i in range(10):
                src = pT[:, i, :] if i < 4 else aT[:, i - 4, :] if i < 6 else bcv[:, i - 6, :]
                nc.scalar.copy(bH[:, i, :], src).then_inc(b_hi, 1)

        def gates(it, between):
            for l in range(16):
                if l + 2 == M_BR:
                    act.wait_ge(w_attn, it * 16 + 16)
                lead(U_M, 16, it, l)
                if l in between:
                    between[l]()
                if l in M_GATE[1::2]:
                    i = M_GATE.index(l) // 2
                    act.wait_ge(w_used, Unit(U_M, 16, it, l).used)
                    act.wait_ge(br_out, it * 3 + 1)
                    for hf in range(2):
                        ins = nc.scalar.activation(half(sg[:, i, :], hf), PAIR[i % 2][:, hf, 0:HALF], ACT.Sigmoid)
                    ins.then_inc(free[i % 2], 1)
                if l == M_ADA[-1]:
                    act.wait_ge(w_used, Unit(U_M, 16, it, l).used)
                    act.wait_ge(mod_tr, it + 9)
                    nc.scalar.copy(mod_rows[0:18, :], BA[0:18, :]).then_inc(mod_row, 1)

        gates(0, {0: sample_exp, 12: branch_hi})
        act.wait_ge(b_lo, 10)
        with act.Fori(1, KD) as it:
            gates(it, {})
        act.wait_ge(w_used, Unit(U_M, 16, KD - 1, M_GATE[-1]).used)
        act.wait_ge(br_out, 3 * KD + 1)
        for k in range(KD):
            nc.scalar.copy(hH[:, k, :], merged[:, k, :]).then_inc(m_hi, 1)
        act.wait_ge(m_lo, KD)
        with act.Fori(0, 8) as it:
            for l in range(4):
                lead(U_O, 4, it, l)
                if l % 2:
                    act.wait_ge(w_used, Unit(U_O, 4, it, l).used)
                    dst = mixT[:, bass.ds(it * 2 + l // 2, 1), :].rearrange("p k t -> p (k t)")
                    act.copy(half(dst, 0), PAIR[l // 2][:, 0, 0:HALF]).then_inc(mix_out, 1)
                    act.copy(half(dst, 1), PAIR[l // 2][:, 1, 0:HALF]).then_inc(free[l // 2], 1)
        norm_root(act, rbn_mm, 1, rbn, rt2)

        def x1_rows(q, blocks):
            for b in blocks:
                act.wait_ge(x1_tr, (NB + 1) * q + b + 1)
                if b < NB:
                    nc.scalar.copy(yN[:, q, b, :], (BA, BT, BS, BO)[b]).then_inc(x1_nat, 1)
                else:
                    nc.scalar.copy(yNs[:, q * 512:(q + 1) * 512], Y[0:NS, q % 2, :]).then_inc(x1_nat, 1)

        for k in range(KD):
            act.wait_ge(x1_done, k + 1)
            if k >= 2:
                act.wait_ge(sq_mm, k - 1)
            nc.scalar.activation(sqc[:, k % 2, :], xR[:, k, :], ACT.Square).then_inc(sq_in, 1)
            if k >= 5:
                x1_rows(*X1_TURNS[k - 5])
        act.wait_ge(h2_pre, 1)
        norm_root(act, sq_mm, KD, rbn, rt2)
        for q, blocks in X1_TURNS[KD - 5:]:
            x1_rows(q, blocks)
        act.wait_ge(h2_pre, 2)
        nc.scalar.copy(hH[:, :, SA], mixT[:, :, SA]).then_inc(h2_hi, 1)
        for k in range(KD):
            act.wait_ge(h2_pre, k + 3)
            nc.scalar.activation(hH[:, k, PR], mixT[:, k, PR], ACT.Identity, bias=mods[:, 3 * KD + k, 0:1]).then_inc(h2_hi, 1)

        act.wait_ge(h2_lo, KD + 2)

        def up_pair(base, per, it, l0, rnd4, p, late=False):
            for l in range(4):
                if base == U_F0 or l0 + l < 24:
                    lead(base, per, it, l0 + l)
                if l % 2:
                    v = l // 2
                    act.wait_ge(w_used, Unit(base, per, it, l0 + l).used)
                    act.wait_ge(tail_tr, rnd4 + 1)
                    act.wait_ge(cv_done, rnd4 * 2 + (v + 1))
                    act.copy(half(us[:, v, :], 0), PAIR[v][:, 0, 0:HALF])
                    act.copy(half(us[:, v, :], 1), PAIR[v][:, 1, 0:HALF]).then_inc(free[v], 1)
                    act.wait_ge(free[v], CF(rnd4) + 2)
                    act.wait_ge(f_done, rnd4 + 1)
                    nc.scalar.mul(cv[:, v, :], us[:, v, :], tap(2, v, rnd4)).then_inc(us_c, 1)
            act.wait_ge(cv_done, rnd4 * 2 + 3)
            nc.scalar.activation(cv[:, 0, :], cv[:, 0, :], ACT.Gelu_apprx_tanh).then_inc(gelu_done, 1)
            if not late:
                f_split(rnd4, p)

        def f_split(rnd4, p):
            act.wait_ge(f_done, rnd4 + 2)
            nc.scalar.copy(fH[:, p, :], ft).then_inc(f_hi, 1)

        for pair in range(FPR):
            up_pair(U_F0, 16, 0, 4 * pair, pair, pair)
        with act.Fori(0, 10) as it:
            r4 = it * 4 + 4
            up_pair(U_F, 24, it, 0, r4, 0, late=True)
            for l in range(4, 12):
                lead(U_F, 24, it, l)
            act.wait_ge(w_used, Unit(U_F, 24, it, 11).used)
            f_split(r4, 0)
            for pair in range(1, FPR):
                up_pair(U_F, 24, it, 8 + 4 * pair, r4 + pair, pair)
        for l in range(9):
            if l < 6:
                lead(U_END, 8, 0, l)
            for k in (2 * l - 2, 2 * l - 1) if l else ():
                act.wait_ge(down_out, 2 * (10 * KD + k) + 6)
                if k >= 2:
                    act.wait_ge(sqf_used, k - 1)
                nc.scalar.activation(sqf[:, k % 2, :], acc[:, k, :], ACT.Square).then_inc(sqf_in, 1)
                nc.scalar.mul(fc[:, k, PR], acc[:, k, PR], coef[:, k, 0:1]).then_inc(fc_done, 1)
        act.wait_ge(sqf_mm, 1)
        nc.scalar.activation(rsf[:, 0:NB], BO[:, 0:NB], ACT.Sqrt, bias=eps, scale=1.0 / D).then_inc(rt3, 1)
        nc.scalar.activation(rsf[0:NS, NB:NB + 1], BO[0:NS, NB:NB + 1], ACT.Sqrt, bias=eps[0:NS], scale=1.0 / D).then_inc(rt3, 1)

    Y_TILES = [(q, b) for q in range(4) for b in range(NB + 1)]
    X1_TURNS = [(j // NB, (j % NB,) if j % NB < NB - 1 else (NB - 1, NB)) for j in range(4 * NB)]
    Y_BANK = [X[:, 0, :], X[:, 1, :], Y[:, 0, :], Y[:, 1, :], BA, BT, BS]
    CF = lambda rnd4: rnd4 + C_F0

    def tap(i, v, rnd4):
        return ffn_w[:, i, bass.ds(rnd4 + v * FCH, 1)]

    def norm_root(act, s, n, dst, done):
        act.wait_ge(s, n)
        act.activation(dst[:, 0:HALF], X[:, 0, 0:HALF], ACT.Sqrt, bias=eps, scale=1.0 / D)
        act.activation(dst[:, HALF:T], X[:, 1, 0:HALF], ACT.Sqrt, bias=eps, scale=1.0 / D).then_inc(done, 1)

    BIAS_MM = [(g, n0, n1) for g in range(G) for n0, n1 in ((0, 385), (385, BW))]
    BIAS_BANK = [BS, BO, X[:, 0, :], X[:, 1, :], Y[:, 0, :], Y[:, 1, :]]
    X_BANK = [X[:, 0, :], BS, BO, X[:, 1, :]]

    def vector_program(dve):
        step = Step(dve, dve_step)

        def lo(u):
            dve.wait_ge(w_hi, u.hi_done)
            dve.tensor_tensor(wlo[u.spl], raw[:, u.raw, :], whi[u.spl], ALU.subtract).then_inc(w_lo, 1)

        def lead(base, per, it, l):
            lo(Unit(base, per, it, l + 2))

        for s, n in ((w_lo, 4), (w_used, 2), (x_free, 1), (y_free, 1), (mod_tr, 1), (mod_row, 1), (mod_out, 1),
                     (nat_tr, 2), (qk_out, 2), (nat_out, 2), (o_out, 1), (o_mm, 1), (oT_tr, 1), (c_cp, 1), (ks_used, 2),
                     (u_used, 1), (p_out, 1), (tail_tr, 1), (tail_out, 1), (cv_done, 2), (f_done, 1), (f_hi, 1),
                     (tail_free, 4), (down_out, 4)):
            dve.sem_inc(s, n)
        dve.memset(ones, 1.0)
        dve.memset(eps, EPS)
        dve.memset(relb, 1.0).then_inc(set_up, 1)
        dve.wait_ge(silu, 1)
        step(dve.tensor_tensor(cc, cc, csig, ALU.mult))
        step.settle()
        dve.sem_inc(c_split, 1)
        dve.wait_ge(c_tr, 1)
        cps = BA[:, 0:KD * 9].rearrange("p (k n) -> p k n", n=9)
        step(dve.tensor_copy(cT[:, :, 0:9], cps))
        step.settle()
        dve.tensor_tensor(cT[:, :, 9:18], cps, cT[:, :, 0:9], ALU.subtract).then_inc(c_split, 1)
        for l in range(2):
            lo(Unit(0, 0, 0, l))

        def tiles(part, scaling=False):
            with dve.Fori(ADA_PARTS[part], ADA_PARTS[part + 1]) as it:
                here = it - ADA_PARTS[part]
                step.enter(here, 8 if scaling else 0)
                for l in range(8):
                    lead(U_ADA, 8, it, l)
                    if scaling:
                        k = bass.ds(here * 8 + l, 1)
                        flat = lambda t: t[:, k, :].rearrange("p k t -> p (k t)")
                        step(dve.tensor_tensor(flat(xr), flat(xT), rb, ALU.mult))
                mod_columns(dve, it, it + 1)
                step.leave(2)

        def x_columns(n0, n1):
            for n in range(n0, n1):
                dve.wait_ge(x_tr, n + 1)
                if n < 16:
                    b, q = n // 4, n % 4
                    dve.tensor_copy(xT[:, 4 * q:4 * q + 4, b * P:(b + 1) * P], X_BANK[n % 4].rearrange("p (k t) -> p k t", t=P)).then_inc(x_out, 1)
                else:
                    dve.tensor_copy(xT[:, :, SA], Y[:, 1, 0:KD * NS].rearrange("p (k t) -> p k t", t=NS)).then_inc(x_out, 1)

        tiles(0)
        dve.wait_ge(par_tr, 1)
        dve.tensor_copy(cols, Y[:, 0, 0:80]).then_inc(par_out, 1)
        dve.tensor_copy(ffn_w, BS[:, 0:3 * 88].rearrange("p (t k) -> p t k", t=3)).then_inc(par_out, 1)
        dve.tensor_copy(st_conv, BO[:, 0:64].rearrange("p (k b r) -> p k b r", k=4, b=NS)).then_inc(par_out, 1)
        dve.tensor_copy(st_pool, X[:, 0, 0:480].rearrange("p (k b r) -> p k b r", k=4, b=NS)).then_inc(par_out, 1)
        tiles(1)
        x_columns(0, 8)
        tiles(2)
        x_columns(8, 17)
        dve.wait_ge(rt_done, 2)
        step(dve.reciprocal(rs[:, 0:4], rs[:, 0:4]))
        step(dve.reciprocal(rs[0:NS, 4:5], rs[0:NS, 4:5]))
        step.settle()
        for b in range(NB):
            step(dve.tensor_scalar(diag[:, b, :], ident, rs[:, b:b + 1], None, ALU.mult))
        dve.tensor_scalar(diag[0:NS, 4, 0:NS], ident[0:NS, 0:NS], rs[0:NS, 4:5], None, ALU.mult).then_inc(diag_done, 1)
        dve.wait_ge(rb_done, 2)
        dve.wait_ge(x_out, 17)
        tiles(3, scaling=True)
        step.settle()
        dve.wait_ge(mod_out, 9)
        modulate(dve, step, xr, 0, 1, 0, h_pre, h_hi, h_lo)
        for part in range(3):
            with dve.Fori(0, 3) as it:
                step.enter(it, 0)
                for l in range(4):
                    lead(U_QKV + 12 * part, 4, it, l)
                    i = l // 2
                    c = it * 2 + (i + 6 * part)
                    if l % 2:
                        dve.wait_ge(free[i], it + (3 * part + 2))
                        if part < 2:
                            dst = qk[:, bass.ds(c, 1), :].rearrange("p k t -> p (k t)")
                            dve.tensor_copy(dst, stage[:, i, 0:TP]).then_inc(qk_out, 1)
                        else:
                            dve.sem_inc(qk_out, 1)
                        dve.wait_ge(nat_tr, c + 3)
                        nat_rows = dve.tensor_copy(ns[:, bass.ds(c * P, P)], (BO, BA)[i][0:NS, 0:P])
                        if part == 0:
                            nat_rows.then_inc(nat_out, 1)
                        else:
                            nat = (kn, vn)[part - 1][:, bass.ds(it, 1), :, i * P:(i + 1) * P].rearrange("p g b n -> p (g b) n")
                            dve.tensor_copy(nat, (BT, BS)[i].rearrange("p (b n) -> p b n", n=P)).then_inc(nat_out, 1)
                step.leave(3)
        dve.wait_ge(k_st, 16 * 6)
        step(dve.memset(q2, 0.0))
        step.settle()
        with dve.Fori(0, 2) as it:
            step.enter(it, 58)
            def queries(c):
                h, qb = c % 2, c // 2
                src = qk[64 * h:64 * h + 64, 0:QCH, qb * P:(qb + 1) * P].rearrange("p (g j) q -> p j g q", j=2)
                dve.tensor_copy(q2[64 * h:64 * h + 64, h, :, :], src[:, bass.ds(it, 1)].rearrange("p j g q -> p (j g) q")).then_inc(q2_in, 1)

            queries(0)
            dve.wait_ge(u_in, it * 64 + 64)
            for c in range(8):
                h, qb = c % 2, c // 2
                m = it * 8 + c
                wg = [min(qb + 1, 2) * P, (qb + 1) * P, (qb + 1) * P]
                wide = sum(wg)
                dve.wait_ge(s_mm, m + 1)
                o = 0
                for g, bank in enumerate((BT, BS, BA)):
                    end = 256 if g == 0 else 256 + 512 * g
                    step(dve.scalar_tensor_tensor(out=sc_p[:, o:o + wg[g]], in0=bank[:, 0:wg[g]], scalar=SCALE,
                                                  in1=u_bias[:, h, end - wg[g]:end], op0=ALU.mult, op1=ALU.add))
                    o += wg[g]
                step.settle()
                step(dve.tensor_reduce(mx[:, h:h + 1], sc_p[:, 0:wide], AX.X, ALU.max))
                step.settle()
                dve.tensor_scalar(nm[:, h:h + 1], mx[:, h:h + 1], -1.0, None, ALU.mult).then_inc(s_soft, 1)
                if c < 7:
                    queries(c + 1)
                lead(U_PC, 16, it, 2 * c)
                if c % 2 == 0:
                    b = c // 2
                    s = b % 2
                    dve.wait_ge(qB_in[s], it * 32 + (b // 2 + 1) * 16)
                    dve.wait_ge(ks_in[s], it * 96 + (b // 2 + 1) * 48)
                    prod = k_s[:, s, :]
                    step(dve.tensor_tensor(prod, prod, qB[:, s, :], ALU.mult))
                    step.settle()
                    dst = sc_s[:, bass.ds(it * 4 + b, 1), :].rearrange("p b n -> p (b n)")
                    dve.tensor_reduce(dst, prod.rearrange("p (n e) -> p n e", e=DH), AX.X, ALU.add).then_inc(ks_used, 1)
                    dve.wait_ge(ks_used, it * 4 + b + 3)
                lead(U_PC, 16, it, 2 * c + 1)
                pair = PAIR[c % 2]
                kind, i = ("p", c) if c < 2 else ("chb"[(c - 2) % 3], (c - 2) // 3)
                if kind in "hb":
                    dve.wait_ge(w_used, Unit(U_PC, 16, it, 2 * c + 1).used)
                if kind == "h":
                    dve.wait_ge(free[(c - 1) % 2], it * 4 + (C_PC + (c - 1) // 2 + 2))
                    step(dve.tensor_tensor(half(uS, 0), half(cS, 0), pair[:, 0, 0:HALF], ALU.mult))
                    dve.tensor_tensor(half(uS, 1), half(cS, 1), pair[:, 1, 0:HALF], ALU.mult).then_inc(free[c % 2], 1)
                    step.settle()
                    dve.wait_ge(free[c % 2], it * 4 + (C_PC + c // 2 + 2))
                    dve.sem_inc(c_cp, 1)
                    ci = it * 2 + i
                    w = lambda t: cols[:, bass.ds(ci + (64 + 4 * t), 1)]
                    st = lambda r: st_conv[:, bass.ds(ci, 1), :, r].rearrange("p k b -> p (k b)")
                    step(dve.tensor_copy(utail[:, bass.ds(ci, 1), :].rearrange("p k t -> p (k t)"), uS[:, TP - 2:T]))
                    step(dve.tensor_scalar(yS, uS, w(2), None, ALU.mult))
                    step.settle()
                    stt = lambda o, x_, w_: dve.scalar_tensor_tensor(out=o, in0=x_, scalar=w_, in1=o, op0=ALU.mult, op1=ALU.add)
                    step(stt(yS[:, 1:TP], uS[:, 0:TP - 1], w(1)))
                    step(stt(yS[:, SA], st(1), w(1)))
                    step.settle()
                    step(stt(yS[:, 2:TP], uS[:, 0:TP - 2], w(0)))
                    step(stt(yS[:, SA], st(0), w(0)))
                    step.settle()
                if kind == "b":
                    for hf in range(2):
                        dst = bcv[:, bass.ds(it * 2 + i, 1), hf * HALF:(hf + 1) * HALF].rearrange("p k t -> p (k t)")
                        ins = dve.tensor_tensor(dst, half(yS, hf), pair[:, hf, 0:HALF], ALU.mult)
                    ins.then_inc(free[c % 2], 1)
                dve.wait_ge(s_exp, m + 1)
                step(dve.reciprocal(rl[:, h:h + 1], ls[:, h:h + 1]))
                step.settle()
                dve.wait_ge(o_mm, m + 2)
                if h == 0:
                    dve.wait_ge(oT_tr, it * 4 + (qb + 1))
                dve.tensor_scalar(osb[:, h, :], BO[:, 0:DH], rl[:, h:h + 1], None, ALU.mult).then_inc(o_out, 1)
                if h == 1:
                    dve.wait_ge(oT_tr, it * 4 + (qb + 2))
                    dst = aT[:, bass.ds(it, 1), qb * P:(qb + 1) * P].rearrange("p k t -> p (k t)")
                    dve.tensor_copy(dst, BO[:, P:2 * P]).then_inc(oT_out, 1)
            dve.sem_inc(u_used, 1)
            step.leave(2)
        bv = bS.rearrange("p (h g) n -> p h g n", g=G)

        def sample_scores():
            dve.wait_ge(oT_out, 8)
            dve.wait_ge(bS_in, 16)
            dve.wait_ge(ss_tr, 1)
            for n in range(12):
                h, g = n // G, n % G
                step(dve.scalar_tensor_tensor(out=ss[:, h, g, 0:NK], in0=(BT, BS, BO)[n // 4][0:NS, n % 4 * P:(n % 4 + 1) * P],
                                              scalar=SCALE, in1=bv[:, h, g, 0:NK], op0=ALU.mult, op1=ALU.add))
            step(dve.tensor_tensor(t8, ns[:, 0:AW], ns[:, AW:2 * AW], ALU.mult))
            step.settle()
            step(dve.tensor_reduce(n8, t8.rearrange("p (n e) -> p n e", e=DH), AX.X, ALU.add))
            step.settle()
            step(dve.scalar_tensor_tensor(out=ss[:, :, :, NK], in0=n8.rearrange("p (g h) -> p h g", g=G), scalar=SCALE,
                                          in1=bv[:, :, :, NK], op0=ALU.mult, op1=ALU.add))
            step.settle()
            step(dve.tensor_reduce(smx, ss.rearrange("p h g n -> p h (g n)"), AX.X, ALU.max))
            step.settle()
            dve.tensor_scalar(smx, smx, -1.0, None, ALU.mult).then_inc(ss_max, 1)

        def sample_probs():
            dve.wait_ge(ss_exp, HG)
            step(dve.reciprocal(srl, sls))
            step.settle()
            for h in range(HG):
                ins = dve.tensor_scalar(ss[:, h, :, :], ss[:, h, :, :], srl[:, h:h + 1], None, ALU.mult)
                if h < HG - 1:
                    step(ins)
            ins.then_inc(ss_norm, 1)
            dve.wait_ge(ss_norm, 1)
            step.settle()
            v4 = ns[:, 2 * AW:3 * AW].rearrange("p (g h e) -> p g h e", g=G, h=HG)
            t4 = t8.rearrange("p (g h e) -> p g h e", g=G, h=HG)
            for g in range(G):
                step(dve.tensor_tensor(t4[:, g], v4[:, g], ss[:, :, g, NK:NK + 1].to_broadcast([NS, HG, DH]), ALU.mult))
            step.settle()
            step(dve.tensor_tensor(nv8, t8[:, 0:256], t8[:, 256:512], ALU.add))
            step.settle()
            dve.tensor_tensor(nv8, nv8, t8[:, 512:768], ALU.add).then_inc(nv_out, 1)

        def probs_columns():
            dve.wait_ge(pts_tr, 1)
            pts = BT[:, 0:12 * NS].rearrange("p (h g b) -> p h g b", h=HG, g=G)
            for h in range(HG):
                ins = dve.tensor_copy(pTs[:, :, :, h], pts[:, h])
            ins.then_inc(pts_out, 1)
            dve.wait_ge(ptail_tr, 1)
            dve.tensor_copy(t_tails[:, 0, :], Y[0:23, 0, :]).then_inc(ptail_out, 1)
            dve.tensor_copy(t_tails[0:10, 1, :], Y[0:10, 1, :]).then_inc(ptail_out, 1)

        def sample_outputs(b0):
            for b in (b0, b0 + 1):
                dve.wait_ge(vs_mm, b + 1)
                bank = (BS, BT)[b % 2]
                dve.tensor_tensor(mk[:, b % 2, :], bank[0:HG, 0:256], heads_mask, ALU.mult).then_inc(vs_out, 1)

        def sample_columns():
            dve.wait_ge(oTs_mm, 1)
            dve.tensor_copy(aT[:, :, SA], BO[:, 0:2 * NS].rearrange("p (c b) -> p c b", c=2)).then_inc(oTs_out, 1)

        def pool(i):
            w = WIN[i]
            pc = pT[:, i, :]
            a_, b_ = stage[:, 0, :], stage[:, 1, :]
            src, width = pc, 1
            while width < w:
                dst = a_ if src is not a_ else b_
                step(dve.tensor_tensor(dst[:, width:TP], src[:, width:TP], src[:, 0:TP - width], ALU.add))
                step(dve.tensor_copy(dst[:, 0:width], src[:, 0:width]))
                step.settle()
                src, width = dst, 2 * width
            oth = a_ if src is not a_ else b_
            step(dve.tensor_tensor(oth[:, 0:16], src[:, 0:16], counts[:, i, :], ALU.mult))
            step(dve.tensor_reduce(oth[:, TP:T], st_pool[:, i, :, 16 - w:15], AX.X, ALU.add))
            step.settle()
            step(dve.tensor_tensor(oth[:, TP:T], oth[:, TP:T], pc[:, SA], ALU.add))
            step.settle()
            step(dve.scalar_tensor_tensor(out=pc[:, 16:TP], in0=src[:, 16:TP], scalar=1.0 / w, in1=pc[:, 16:TP],
                                          op0=ALU.mult, op1=ALU.subtract))
            step(dve.tensor_tensor(pc[:, 0:16], oth[:, 0:16], pc[:, 0:16], ALU.subtract))
            dve.scalar_tensor_tensor(out=pc[:, SA], in0=oth[:, TP:T], scalar=1.0 / w, in1=pc[:, SA],
                                     op0=ALU.mult, op1=ALU.subtract).then_inc(pool_done, 1)
            step.settle()
            dve.wait_ge(pool_done, i + 1)

        def group(i):
            dve.wait_ge(grp_mm, i + 1)
            for hf, bank in enumerate((BT, BS)):
                ins = dve.tensor_scalar(half(pT[:, i, :], hf), bank[:, 0:HALF], cols[:, 76 + i:77 + i], None, ALU.mult)
                if hf == 0:
                    step(ins)
            ins.then_inc(grp_out, 1)

        def branch_lo():
            for i in range(10):
                dve.wait_ge(b_hi, i + 1)
                src = pT[:, i, :] if i < 4 else aT[:, i - 4, :] if i < 6 else bcv[:, i - 6, :]
                dve.tensor_tensor(bL[:, i, :], src, bH[:, i, :], ALU.subtract).then_inc(b_lo, 1)
            dve.wait_ge(b_lo, 10)
            dve.wait_ge(k_st, 16 * 6)
            dve.wait_ge(v_st, 16 * 6)

        def gates(it, between):
            dst = merged[:, bass.ds(it, 1), :].rearrange("p k t -> p (k t)")
            for l in range(M_BR + 1):
                lead(U_M, 16, it, l)
                for stage_ in between.get(l, ()):
                    stage_()
            for n, (i, pr) in enumerate(((0, 1), (2, 0), (1, 1))):
                if n == 0:
                    dve.wait_ge(br_mm, it + 1)
                    dve.wait_ge(x_free, it * 3 + (C_M + 3))
                    dve.wait_ge(y_free, it * 3 + (C_M + 2))
                else:
                    if n == 2:
                        lead(U_M, 16, it, 14)
                        lead(U_M, 16, it, 15)
                    last = (M_BR, M_CONV)[n - 1]
                    dve.wait_ge(w_used, Unit(U_M, 16, it, last).used)
                for hf in range(2):
                    o = half(dst, hf) if n == 0 else half(mt[:, n - 1, :], hf)
                    ins = dve.tensor_tensor(o, half(sg[:, i, :], hf), PAIR[pr][:, hf, 0:HALF], ALU.mult)
                    if hf == 0:
                        step(ins)
                ins.then_inc(free[pr], 1)
                dve.wait_ge(free[pr], it * 3 + (C_M + (3 if n == 0 else 4)))
                if n == 0:
                    dve.sem_inc(br_out, 1)
                else:
                    dve.tensor_tensor(dst, dst, mt[:, n - 1, :], ALU.add).then_inc(br_out, 1)
                    dve.wait_ge(br_out, it * 3 + (n + 2))
            mod_columns(dve, it + 8, it + 9)

        dve.sem_inc(br_out, 1)
        sample_scores()
        gates(0, {1: [sample_probs], 2: [probs_columns, lambda: pool(0)], 3: [lambda: sample_outputs(0)],
                  4: [lambda: sample_outputs(2), lambda: pool(1)], 6: [lambda: sample_outputs(4)],
                  7: [lambda: sample_outputs(6), lambda: pool(2)], 8: [sample_columns], 9: [lambda: group(0)],
                  10: [lambda: group(1), lambda: pool(3)], 11: [lambda: group(2)], 12: [lambda: group(3), branch_lo]})
        with dve.Fori(1, KD) as it:
            step.enter(it - 1, 3)
            gates(it, {})
            step.leave(KD - 1)
        for k in range(KD):
            dve.wait_ge(m_hi, k + 1)
            dve.tensor_tensor(hL[:, k, :], merged[:, k, :], hH[:, k, :], ALU.subtract).then_inc(m_lo, 1)
        dve.wait_ge(w_used, Unit(U_M, 16, KD - 1, 15).used)
        step(dve.memset(sacc, 0.0))
        with dve.Fori(0, 8) as it:
            step.enter(it, 4)
            for l in range(4):
                lead(U_O, 4, it, l)
                if l % 2:
                    dve.wait_ge(free[l // 2], it + (C_O + 2))
                    src = mixT[:, bass.ds(it * 2 + l // 2, 1), :].rearrange("p k t -> p (k t)")
                    step(dve.tensor_tensor(sqc[:, 0, :], src, src, ALU.mult))
                    step.settle()
                    step(dve.tensor_tensor(sacc, sacc, sqc[:, 0, :], ALU.add))
                    step.settle()
            step.leave(8)
        dve.sem_inc(sacc_done, 1)
        coefficients(dve, step, 1, 2, False)
        dve.wait_ge(rt2, 1)
        step(dve.reciprocal(rbn, rbn))
        step.settle()
        dve.wait_ge(x_back, 16)
        residual(dve, step, mixT, rbn, xR, x1_done)
        dve.wait_ge(x1_done, KD)
        coefficients(dve, step, 2, 4, True)
        dve.sem_inc(h2_pre, 1)
        dve.wait_ge(rt2, 2)
        step(dve.reciprocal(rbn, rbn))
        step.settle()
        rS, shift = rbn[:, SA].unsqueeze(1).to_broadcast([P, KD, NS]), mods[:, 3 * KD:4 * KD, :]
        step(dve.tensor_tensor(mixT[:, :, SA], xR[:, :, SA], coef[:, :, 1:9], ALU.mult))
        step.settle()
        step(dve.tensor_tensor(mixT[:, :, SA], mixT[:, :, SA], rS, ALU.mult))
        step.settle()
        dve.tensor_tensor(mixT[:, :, SA], mixT[:, :, SA], shift[:, :, 1:9], ALU.add).then_inc(h2_pre, 1)
        for k in range(KD + 1):
            if k < KD:
                dve.scalar_tensor_tensor(out=mixT[:, k, PR], in0=xR[:, k, PR], scalar=coef[:, k, 0:1], in1=rbn[:, PR],
                                         op0=ALU.mult, op1=ALU.mult).then_inc(h2_pre, 1)
            dve.wait_ge(h2_hi, k + 1)
            if k == 0:
                dve.wait_ge(x1_st, 48)
            if k == 9:
                dve.wait_ge(x1_st_last, 16)
            if k in (0, 9):
                o = slice(0, 8) if k == 0 else slice(8, KD)
                dve.tensor_tensor(hL[:, o, SA], mixT[:, o, SA], hH[:, o, SA], ALU.subtract).then_inc(h2_lo, 1)
            if k:
                dve.scalar_tensor_tensor(out=hL[:, k - 1, PR], in0=mixT[:, k - 1, PR], scalar=shift[:, k - 1, 0:1],
                                         in1=hH[:, k - 1, PR], op0=ALU.add, op1=ALU.subtract).then_inc(h2_lo, 1)

        def states(rnd):
            dve.wait_ge(st_tr, rnd + 1)
            ins = dve.tensor_copy(st_f, BO[:, 0:128].rearrange("p (v k b r) -> p v k b r", v=2, k=4, b=NS))
            ins.then_inc(st_out, 1)
            dve.wait_ge(st_out, rnd + 1)

        def tails(rnd4, p):
            dve.wait_ge(tail_tr, rnd4 + 2)
            dve.wait_ge(tail_free, TAILS_FREE(rnd4, p))
            ins = dve.tensor_copy(trow[:, :, p * P:(p + 1) * P], BA[0:10, 0:256].rearrange("p (v n) -> p v n", v=2))
            ins.then_inc(tail_out, 1)

        def convolve(base, per, it, l0, rnd4, p, after={}):
            for l in range(4):
                lead(base, per, it, l0 + l)
                if l in after:
                    after[l]()
                if l % 2:
                    v = l // 2
                    st = lambda r: st_f[:, v, p, :, r]
                    stt = lambda o, x_, w_: dve.scalar_tensor_tensor(out=o, in0=x_, scalar=w_, in1=o, op0=ALU.mult, op1=ALU.add)
                    dve.wait_ge(us_c, rnd4 * 2 + (v + 1))
                    step(stt(cv[:, v, 1:TP], us[:, v, 0:TP - 1], tap(1, v, rnd4)))
                    step(stt(cv[:, v, SA], st(1), tap(1, v, rnd4)))
                    step.settle()
                    step(stt(cv[:, v, 2:TP], us[:, v, 0:TP - 2], tap(0, v, rnd4)))
                    stt(cv[:, v, SA], st(0), tap(0, v, rnd4)).then_inc(cv_done, 1)
            dve.wait_ge(gelu_done, rnd4 + 1)
            dve.wait_ge(cv_done, rnd4 * 2 + 4)
            step.settle()
            dve.wait_ge(f_hi, rnd4 + 1)
            dve.tensor_tensor(ft, cv[:, 0, :], cv[:, 1, :], ALU.mult).then_inc(f_done, 1)

        def f_lo_part(rnd4, p):
            dve.wait_ge(f_hi, rnd4 + 2)
            dve.tensor_tensor(fL[:, p, :], ft, fH[:, p, :], ALU.subtract).then_inc(f_lo, 1)

        def accumulate(rnd, l, done, between):
            for i in range(2):
                m = 2 * l + i
                if i == 0:
                    dve.wait_ge(down_mm, rnd * 8 + (l + 1))
                else:
                    dve.wait_ge(w_used, done)
                for hf, bank in enumerate(((BA, BT), (BS, BO))[i]):
                    o = half(acc[:, m, :], hf)
                    dve.tensor_tensor(o, o, bank[:, 0:HALF], ALU.add).then_inc(down_out, 1)
            if between:
                between()

        states(0)
        for p in range(FPR):
            convolve(U_F0, 16, 0, 4 * p, p, p, {0: lambda: tails(p - 1, p - 1)} if p else {})
            f_lo_part(p, p)
            step(dve.memset(acc[:, 4 * p:4 * p + 4, :], 0.0))
        step.settle()
        with dve.Fori(0, 10) as it:
            step.enter(it, 24)
            r4 = it * 4 + 4
            convolve(U_F, 24, it, 0, r4, 0, {0: lambda: tails(it * 4 + 3, 3), 1: lambda: states(it + 1)})
            for l in range(8):
                accumulate(it, l, Unit(U_F, 24, it, 4 + l).used, lambda: lead(U_F, 24, it, 4 + l))
            f_lo_part(r4, 0)
            for p in range(1, FPR):
                convolve(U_F, 24, it, 8 + 4 * p, r4 + p, p, {0: lambda: tails(r4 + (p - 1), p - 1)})
                f_lo_part(r4 + p, p)
            step.leave(10)
        tails(4 * ROUNDS - 1, 3)
        def add_square(m):
            dve.wait_ge(sqf_in, m + 1)
            dve.tensor_tensor(fsum, fsum, sqf[:, m % 2, :], ALU.add).then_inc(sqf_used, 1)
            dve.wait_ge(sqf_used, m + 1)

        coefficients(dve, step, 3, 5, False)
        step(dve.memset(fsum, 0.0))
        step.settle()
        for l in range(8):
            def behind():
                if l < 6:
                    lead(U_END, 8, 0, l)
                for m in (2 * l, 2 * l + 1):
                    dve.wait_ge(down_out, 2 * (10 * KD + m) + 6)
                    dve.tensor_tensor(fc[:, m, SA], acc[:, m, SA], coef[:, m, 1:9], ALU.mult).then_inc(fcs_done, 1)
                for m in (2 * l - 2, 2 * l - 1):
                    if m >= 0:
                        add_square(m)

            accumulate(ROUNDS - 1, l, Unit(U_END, 8, 0, l).used, behind)
        add_square(KD - 2)
        add_square(KD - 1)
        dve.wait_ge(rt3, 2)
        step(dve.reciprocal(rsf[:, 0:NB], rsf[:, 0:NB]))
        step(dve.reciprocal(rsf[0:NS, NB:NB + 1], rsf[0:NS, NB:NB + 1]))
        step.settle()
        dve.wait_ge(x1_back, 64)
        for n, (q, b) in enumerate(Y_TILES):
            dve.wait_ge(y_tr, n + 1)
            rows = P if b < NB else NS
            y = yN[:, q, b, :] if b < NB else yNs[:, q * 512:(q + 1) * 512]
            dve.scalar_tensor_tensor(out=y, in0=Y_BANK[n % 7][0:rows, :], scalar=rsf[0:rows, b:b + 1], in1=y,
                                     op0=ALU.mult, op1=ALU.add).then_inc(y_nat, 1)

    TAILS_FREE = lambda rnd4, p: (rnd4 - p) + 4

    def mod_columns(dve, tile, n):
        dve.wait_ge(mod_tr, n + 1)
        dst = mods[:, bass.ds(tile * 4, 4), :]
        dve.tensor_copy(dst, BT[:, 0:36].rearrange("p (k n) -> p k n", n=9)).then_inc(mod_out, 1)

    def coefficients(dve, step, norm, mod, plus_one):
        gcol = cols[:, norm * KD:(norm + 1) * KD].unsqueeze(2).to_broadcast([P, KD, 9])
        step(dve.scalar_tensor_tensor(out=coef, in0=mods[:, mod * KD:(mod + 1) * KD, :], scalar=1.0 if plus_one else 0.0,
                                      in1=gcol, op0=ALU.add, op1=ALU.mult))
        step.settle()

    def modulate(dve, step, x, norm, scale, shift, pre, hi_, lo_):
        coefficients(dve, step, norm, scale, True)
        sh = mods[:, shift * KD:(shift + 1) * KD, :]
        step(dve.tensor_tensor(x[:, :, SA], x[:, :, SA], coef[:, :, 1:9], ALU.mult))
        step.settle()
        step(dve.tensor_tensor(x[:, :, SA], x[:, :, SA], sh[:, :, 1:9], ALU.add))
        step.settle()
        for k in range(KD + 1):
            if k < KD:
                dve.tensor_scalar(x[:, k, PR], x[:, k, PR], coef[:, k, 0:1], sh[:, k, 0:1], ALU.mult, ALU.add).then_inc(pre, 1)
            if k:
                dve.wait_ge(hi_, k)
                dve.tensor_tensor(hL[:, k - 1, :], x[:, k - 1, :], hH[:, k - 1, :], ALU.subtract).then_inc(lo_, 1)

    def residual(dve, step, f, root, x, done):
        rS = root[:, SA].unsqueeze(1).to_broadcast([P, KD, NS])
        step(dve.tensor_tensor(f[:, :, SA], f[:, :, SA], coef[:, :, 1:9], ALU.mult))
        step.settle()
        step(dve.tensor_tensor(f[:, :, SA], f[:, :, SA], rS, ALU.mult))
        for k in range(KD + 1):
            if k < KD:
                step(dve.scalar_tensor_tensor(out=f[:, k, PR], in0=f[:, k, PR], scalar=coef[:, k, 0:1], in1=root[:, PR],
                                              op0=ALU.mult, op1=ALU.mult))
            if k:
                step.settle(1 if k < KD else 0)
                dve.tensor_tensor(x[:, k - 1, :], x[:, k - 1, :], f[:, k - 1, :], ALU.add).then_inc(done, 1)

    def tensor_program(pe):
        def three(ps, u, w0, xh, xl, first, last, wn=P):
            h, l = whi[u.spl][:, w0:w0 + wn], wlo[u.spl][:, w0:w0 + wn]
            pe.matmul(ps, h, xh, start=first, stop=False)
            pe.matmul(ps, h, xl, start=False, stop=False)
            return pe.matmul(ps, l, xh, start=False, stop=last)

        def ready(u):
            pe.wait_ge(w_lo, u.lo_done)

        def chunk(base, per, it, l0, pair, fr, before, between=None, split=None, apart=1, lag=1):
            pe.wait_ge(fr, before + 1)
            for l in range(2):
                u = Unit(base, per, it, l0 + l * apart)
                ready(u)
                for hf in range(2):
                    for k in range(8):
                        kk = 8 * l + k
                        if split is not None and hf == 0:
                            pe.wait_ge(split, kk + lag + (l if lag > 1 else 0))
                        m = three(pair[:, hf, 0:HALF], u, k * P, half(hH[:, kk, :], hf), half(hL[:, kk, :], hf),
                                  kk == 0, kk == 15)
                m.then_inc(w_used, 1)
                if l == 0 and between:
                    between()

        def ada_unit(u, n, j):
            if j == 0:
                pe.wait_ge(mod_row, n + 1)
            ready(u)
            for k in range(2):
                for part in (whi, wlo):
                    kk = 2 * j + k
                    m = pe.matmul(BA[0:18, :], cT[:, kk, :], part[u.spl][:, k * 512:(k + 1) * 512],
                                  start=(kk == 0 and part is whi), stop=(kk == 15 and part is wlo), skip_group_check=True)
            m.then_inc(w_used, 1)

        def turn_mods(n):
            pe.wait_ge(mod_row, n + 2)
            pe.wait_ge(mod_bias, n * 16 + 16)
            pe.wait_ge(mod_out, n + 1)
            for i in range(4):
                m = pe.matmul(BT[:, 9 * i:9 * i + 9], mod_rows[:, i * P:(i + 1) * P], sel, start=True, stop=True)
            m.then_inc(mod_tr, 1)

        pe.wait_ge(c_split, 1)
        for k in range(KD):
            m = pe.transpose(BA[:, 9 * k:9 * k + 9], cc[:, k * P:(k + 1) * P], ident[0:9, 0:9])
        m.then_inc(c_tr, 1)
        pe.wait_ge(c_split, 2)
        pe.wait_ge(k_in, 16)

        def tiles(part):
            with pe.Fori(ADA_PARTS[part], ADA_PARTS[part + 1]) as it:
                for l in range(8):
                    ada_unit(Unit(U_ADA, 8, it, l), it, l)
                turn_mods(it)

        def x_columns(n0, n1):
            for n in range(n0, n1):
                b, q = n // 4, n % 4
                if n >= 4:
                    pe.wait_ge(x_out, n - 3)
                for i in range(4):
                    k = 4 * q + i
                    m = pe.transpose(X_BANK[n % 4][:, i * P:(i + 1) * P], xN[:, b, k * P:(k + 1) * P], ident)
                m.then_inc(x_tr, 1)

        tiles(0)
        pe.wait_ge(row_in, 16 * 6)
        pe.transpose(Y[:, 0, 0:80], rows1, ident[0:80, 0:80])
        for t in range(3):
            pe.transpose(BS[:, 88 * t:88 * t + 88], rowsF[:, t, :], ident[0:88, 0:88])
        for k in range(4):
            pe.transpose(BO[:, 16 * k:16 * k + 16], rowsC[:, k * P:(k + 1) * P], ident[0:16, 0:16])
        for k in range(4):
            m = pe.transpose(X[:, 0, 120 * k:120 * k + 120], rowsP[:, k * P:(k + 1) * P], ident[0:120, 0:120])
        m.then_inc(par_tr, 1)
        pe.wait_ge(bias_in, 32)
        pe.wait_ge(par_out, 4)
        for i, (g, n0, n1) in enumerate(BIAS_MM):
            pe.matmul(BIAS_BANK[i][0:HG, 0:n1 - n0], relb[:, 4 * g:4 * g + 4], onehot[:, g, n0:n1],
                      start=True, stop=True).then_inc(b_mm, 1)
        tiles(1)
        pe.wait_ge(x_in, 16 * 5)
        pe.wait_ge(b_out, 6)
        x_columns(0, 8)
        tiles(2)
        x_columns(8, 16)
        for k in range(KD):
            m = pe.transpose(Y[:, 1, NS * k:NS * k + NS], xs[:, k * P:(k + 1) * P], ident[0:NS, 0:NS])
        m.then_inc(x_tr, 1)
        pe.wait_ge(diag_done, 1)
        pe.wait_ge(x_out, 17)
        for b in range(NB):
            pe.matmul(X[:, 0, b * P:(b + 1) * P], ones, diag[:, b, :], start=True, stop=True)
        pe.matmul(X[:, 1, 0:NS], ones[0:NS, :], diag[0:NS, 4, 0:NS], start=True, stop=True).then_inc(rb_mm, 1)
        tiles(3)
        pe.wait_ge(rb_done, 2)
        last_turn = None
        for part in range(3):
            def turn(it, i, part=part):
                c = it * 2 + (i + 6 * part)
                pe.wait_ge(free[i], it + (3 * part + 2))
                pe.wait_ge(nat_out, c + 1)
                if part:
                    for b in range(NB):
                        pe.transpose((BT, BS)[i][:, b * P:(b + 1) * P], stage[:, i, b * P:(b + 1) * P], ident)
                pe.transpose((BO, BA)[i][0:NS, 0:P], stage[:, i, SA], ident).then_inc(nat_tr, 1)

            def two_chunks(it, before):
                base = U_QKV + 12 * part
                chunk(base, 4, it, 0, X, x_free, it + (C_QKV + 3 * part), between=before, split=h_lo if part == 0 else None)
                chunk(base, 4, it, 2, Y, y_free, it + (C_QKV + 3 * part), between=lambda: turn(it, 0))

            two_chunks(0, last_turn)
            with pe.Fori(1, 3) as it:
                two_chunks(it, lambda: turn(it - 1, 1))
            last_turn = lambda turn=turn: turn(2, 1)
        last_turn()
        pe.wait_ge(nat_out, 3 * QCH + 2)
        with pe.Fori(0, 2) as it:
            def turn_outputs(qb):
                pe.wait_ge(o_out, it * 8 + (2 * qb + 3))
                pe.transpose(BO[:, P:2 * P], osb.rearrange("p h e -> p (h e)"), ident).then_inc(oT_tr, 1)

            for c in range(8):
                h, qb = c % 2, c // 2
                m = it * 8 + c
                lo_kb = (max(qb - 1, 0), 0, 0)
                pe.wait_ge(q2_in, m + 1)
                pe.wait_ge(p_out, m + 1)
                for g, bank in enumerate((BT, BS, BA)):
                    keys = qk[:, bass.ds(it + (QCH + 2 * g), 1), lo_kb[g] * P:(qb + 1) * P].rearrange("p k t -> p (k t)")
                    ins = pe.matmul(bank[:, 0:(qb + 1 - lo_kb[g]) * P], q2[:, h, g, :], keys, start=True, stop=True)
                ins.then_inc(s_mm, 1)
                if c and c % 2 == 0:
                    turn_outputs(qb - 1)

                blocks = [(g, kb) for g in range(G) for kb in range(lo_kb[g], qb + 1)]

                def turn_probs():
                    pe.wait_ge(s_exp, m + 1)
                    for n in range(len(blocks)):
                        t = pe.transpose((BT, BS, BA)[n // 4][:, n % 4 * P:(n % 4 + 1) * P], sc_p[:, n * P:(n + 1) * P], ident)
                    t.then_inc(p_tr, 1)

                chunk(U_PC, 16, it, 2 * c, PAIR[c % 2], free[c % 2], it * 4 + (C_PC + c // 2), between=turn_probs)
                pe.wait_ge(p_out, m + 2)
                pe.wait_ge(o_out, m + 1)
                if qb:
                    pe.wait_ge(oT_out, it * 4 + qb)
                for n, (g, kb) in enumerate(blocks):
                    v = vn[:, g, kb, :].rearrange("p (j n) -> p j n", j=2)[:, bass.ds(it, 1), h * DH:(h + 1) * DH]
                    t = pe.matmul(BO[:, 0:DH], pT_t[:, n, :], v.rearrange("p j n -> p (j n)"), start=(n == 0), stop=(n == len(blocks) - 1))
                t.then_inc(o_mm, 1)
            turn_outputs(NB - 1)
        def sample_scores():
            pe.wait_ge(ks_used, 10)
            pe.wait_ge(p_out, 17)
            pe.wait_ge(oT_out, 8)
            for n in range(12):
                h, g = n // G, n % G
                t = pe.transpose((BT, BS, BO)[n // 4][0:NS, n % 4 * P:(n % 4 + 1) * P], sc_s[:, :, g * HG + h], ident)
            t.then_inc(ss_tr, 1)
            pe.wait_ge(y_free, C_M + 1)
            for k in range(4):
                pe.transpose(Y[0:23, 0, k * P:(k + 1) * P], pT[:, k, TP - 15:T], ident)
            for k in range(4):
                t = pe.transpose(Y[0:10, 1, k * P:(k + 1) * P], utail[:, k, :], ident)
            t.then_inc(ptail_tr, 1)

        def probs_columns():
            pe.wait_ge(ss_norm, 1)
            for n in range(12):
                t = pe.transpose(BT[:, n * NS:(n + 1) * NS], ss[:, n // G, n % G, 0:NK], ident[0:NS, 0:NS])
            t.then_inc(pts_tr, 1)
            pe.wait_ge(nv_out, 1)
            for c in range(2):
                pe.matmul(BO[:, c * NS:(c + 1) * NS], nv8[:, c * P:(c + 1) * P], ident[0:NS, 0:NS],
                          start=(c == 0), stop=False, skip_group_check=True)

        def gather(b):
            pe.wait_ge(vs_out, b + 1)
            for c in range(2):
                t = pe.matmul(BO[:, c * NS + b:c * NS + b + 1], mk[:, b % 2, c * P:(c + 1) * P], ones[0:HG, 0:1],
                              start=False, stop=(b == NS - 1 and c == 1), skip_group_check=True)
            return t

        def sample_values(b0):
            pe.wait_ge(pts_out, 1)
            for b in (b0, b0 + 1):
                pe.wait_ge(vs_in[b % 2], 48 * (b // 2 + 1))
                if b >= 2:
                    gather(b - 2)
                for g in range(G):
                    t = pe.matmul((BS, BT)[b % 2][0:HG, 0:256], pTs[:, g, b, :], v_s[:, b % 2, g * 256:(g + 1) * 256],
                                  start=(g == 0), stop=(g == G - 1))
                t.then_inc(vs_mm, 1)

        def last_gathers():
            gather(NS - 2)
            gather(NS - 1).then_inc(oTs_mm, 1)

        def group(i):
            pe.wait_ge(grp_in, 16)
            pe.wait_ge(pool_done, i + 1)
            if i:
                pe.wait_ge(grp_out, i)
            for hf, bank in enumerate((BT, BS)):
                t = pe.matmul(bank[:, 0:HALF], w_grp[:, i, :], half(pT[:, i, :], hf), start=True, stop=True)
            t.then_inc(grp_mm, 1)

        def branch(u, pair, fr, before, w0, k0, n):
            pe.wait_ge(fr, before + 1)
            for hf in range(2):
                for k in range(n):
                    t = three(pair[:, hf, 0:HALF], u, (w0 + k) * P, half(bH[:, k0 + k, :], hf), half(bL[:, k0 + k, :], hf),
                              k == 0, k == n - 1)
            return t

        def gates(it, between):
            def behind(l):
                if l in between:
                    between[l]()

            def mods(j):
                ada_unit(Unit(U_M, 16, it, M_ADA[j]), it + 8, j)
                behind(M_ADA[j])

            chunk(U_M, 16, it, M_GATE[0], X, x_free, it * 3 + C_M, between=lambda: mods(0), apart=2)
            behind(M_GATE[1])
            mods(1)
            chunk(U_M, 16, it, M_GATE[2], Y, y_free, it * 3 + C_M, between=lambda: (behind(M_GATE[2]), mods(2), mods(3)), apart=3)
            behind(M_GATE[3])
            mods(4)
            chunk(U_M, 16, it, M_GATE[4], X, x_free, it * 3 + (C_M + 1), between=lambda: (behind(M_GATE[4]), mods(5)), apart=2)
            behind(M_GATE[5])
            mods(6)
            pe.wait_ge(b_lo, 10)
            u = Unit(U_M, 16, it, M_BR)
            ready(u)
            branch(u, Y, y_free, it * 3 + (C_M + 1), 0, 0, 4).then_inc(br_mm, 1)
            branch(u, X, x_free, it * 3 + (C_M + 2), 4, 4, 2).then_inc(w_used, 1)
            mods(7)
            u = Unit(U_M, 16, it, M_CONV)
            ready(u)
            branch(u, Y, y_free, it * 3 + (C_M + 2), 0, 6, 4).then_inc(w_used, 1)
            turn_mods(it + 8)

        sample_scores()
        gates(0, {2: probs_columns, 3: lambda: (pe.wait_ge(ptail_out, 2), sample_values(0)), 4: lambda: sample_values(2),
                  6: lambda: sample_values(4), 7: lambda: sample_values(6), 8: last_gathers, 9: lambda: group(0),
                  10: lambda: group(1), 11: lambda: group(2), 12: lambda: group(3)})
        with pe.Fori(1, KD) as it:
            gates(it, {})
        with pe.Fori(0, 8) as it:
            chunk(U_O, 4, it, 0, X, x_free, it + C_O, split=m_lo)
            chunk(U_O, 4, it, 2, Y, y_free, it + C_O)

        def column_sums(src, done, last=True, first=True):
            for hf in range(2):
                t = pe.matmul(X[:, hf, 0:HALF], ones, half(src, hf), start=first, stop=last, skip_group_check=True)
            t.then_inc(done, 1)

        pe.wait_ge(sacc_done, 1)
        pe.wait_ge(x_free, C_F0 + 1)
        column_sums(sacc, rbn_mm)
        pe.wait_ge(rt2, 1)
        pe.wait_ge(y_free, C_F0 + 1)

        def x1_turn(q, blocks):
            for b in blocks:
                if q and b < NB:
                    pe.wait_ge(x1_nat, (NB + 1) * (q - 1) + b + 1)
                if q >= 2 and b == NB:
                    pe.wait_ge(x1_nat, (NB + 1) * (q - 1))
                for i in range(4):
                    if b < NB:
                        t = pe.transpose((BA, BT, BS, BO)[b][:, i * P:(i + 1) * P], xR[:, 4 * q + i, b * P:(b + 1) * P], ident)
                    else:
                        t = pe.transpose(Y[0:NS, q % 2, i * P:(i + 1) * P], xR[:, 4 * q + i, SA], ident)
                t.then_inc(x1_tr, 1)

        for k in range(KD):
            pe.wait_ge(sq_in, k + 1)
            column_sums(sqc[:, k % 2, :], sq_mm, k == KD - 1, k == 0)
            if k >= 4:
                x1_turn(*X1_TURNS[k - 4])
        for q, blocks in X1_TURNS[KD - 4:]:
            x1_turn(q, blocks)
        pe.wait_ge(rt2, 2)
        pe.wait_ge(x1_nat, 4 * (NB + 1))

        def states(rnd):
            pe.wait_ge(st_in, rnd * 32 + 32)
            pe.sem_inc(st_seen, 1)
            for v in range(2):
                for k in range(4):
                    n = (v * 4 + k) * 16
                    t = pe.transpose(BO[:, n:n + 16], st_rows[:, v, k * P:(k + 1) * P], ident[0:16, 0:16])
            t.then_inc(st_tr, 1)

        def tails(rnd4):
            pe.wait_ge(us_c, rnd4 * 2 + 2)
            pe.wait_ge(tail_out, rnd4 + 1)
            for v in range(2):
                t = pe.transpose(BA[0:10, v * P:(v + 1) * P], us[:, v, TP - 2:T], ident)
            t.then_inc(tail_tr, 1)

        def up(base, per, it, l0, rnd4, split=None, lag=1, gate_between=None, val_between=None):
            chunk(base, per, it, l0, X, x_free, CF(rnd4), between=gate_between, split=split, lag=lag)
            chunk(base, per, it, l0 + 2, Y, y_free, CF(rnd4), between=val_between)

        def down(base, per, it, l0, rnd):
            pe.wait_ge(f_lo, rnd * 4 + 4)
            for l in range(8):
                u = Unit(base, per, it, l0 + l)
                ready(u)
                for i in range(2):
                    pe.wait_ge(down_out, (rnd * KD) * 2 + (2 * (2 * l + i) + 2))
                    for hf, bank in enumerate(((BA, BT), (BS, BO))[i]):
                        for k in range(FPR):
                            t = three(bank[:, 0:HALF], u, (2 * k + i) * P, half(fH[:, k, :], hf), half(fL[:, k, :], hf),
                                      k == 0, k == FPR - 1)
                    t.then_inc(w_used if i else down_mm, 1)

        states(0)
        for p in range(FPR):
            up(U_F0, 16, 0, 4 * p, p, split=None if p else h2_lo, lag=2, gate_between=(lambda: tails(p - 1)) if p else None)
        with pe.Fori(0, 10) as it:
            r4 = it * 4 + 4

            def next_states():
                pe.wait_ge(st_out, it + 1)
                states(it + 1)

            up(U_F, 24, it, 0, r4, gate_between=lambda: tails(it * 4 + 3), val_between=next_states)
            pe.wait_ge(tail_out, it * 4 + 5)
            pe.wait_ge(st_out, it + 2)
            down(U_F, 24, it, 4, it)
            for p in range(1, FPR):
                def before_pair():
                    if p == 1:
                        pe.wait_ge(down_out, it * (2 * KD) + (2 * KD + 4))
                    tails(r4 + (p - 1))

                up(U_F, 24, it, 8 + 4 * p, r4 + p, gate_between=before_pair)
        tails(4 * ROUNDS - 1)
        pe.wait_ge(tail_out, 4 * ROUNDS + 1)
        down(U_END, 8, 0, 0, ROUNDS - 1)
        pe.wait_ge(x_free, C_F + 40 + 1)
        pe.wait_ge(y_free, C_F + 40 + 1)

        def y_tile(n):
            q, b = Y_TILES[n]
            if n >= 7:
                pe.wait_ge(y_nat, n - 6)
            if b in (0, NB):
                pe.wait_ge((fc_done, fcs_done)[b == NB], 4 * q + 4)
            for i in range(4):
                tokens = slice(b * P, (b + 1) * P) if b < NB else SA
                t = pe.transpose(Y_BANK[n % 7][0:P if b < NB else NS, i * P:(i + 1) * P], fc[:, 4 * q + i, tokens], ident)
            t.then_inc(y_tr, 1)

        for n in range(4):
            y_tile(n)
        pe.wait_ge(down_out, 2 * ROUNDS * KD + 4)
        for n in range(4, 7):
            y_tile(n)
        pe.wait_ge(sqf_used, KD)
        for b in range(NB):
            pe.matmul(BO[:, b:b + 1], fsum[:, b * P:(b + 1) * P], ones[:, 0:1], start=True, stop=True)
        pe.matmul(BO[0:NS, NB:NB + 1], fsum[:, SA], ones[:, 0:1], start=True, stop=True).then_inc(sqf_mm, 1)
        for n in range(7, len(Y_TILES)):
            y_tile(n)

    with nc.Block() as block:
        block.sync(sync_program)
        block.gpsimd(pool_program)
        block.scalar(scalar_program)
        block.vector(vector_program)
        block.tensor(tensor_program)


INS = ["x_prompt", "x_sample", "c_prompt", "c_sample", "cache_kv_w128", "cache_kv_w512", "cache_kv_w2048",
       "state_pool", "state_conv", "state_ffn_conv", "rel_bias", "norm_g", "w_ada", "b_ada", "w_in", "w_attn_br",
       "w_pool_grp", "pool_scale", "w_pool_br", "conv_w", "w_conv_br", "w_o", "w_up", "ffn_conv_w", "w_down"]
OUTS = [("y_p", (1, TP, D)), ("y_s", (NS, 1, D)),
        ("kv128_p", (1, 1, 128, 2, HG, DH)), ("kv512_p", (1, 1, 512, 2, HG, DH)), ("kv2048_p", (1, 1, 512, 2, HG, DH)),
        ("pool_p", (1, 1, 15, PW)), ("conv_p", (1, 1, 2, CC)), ("ffn_p", (1, 1, 2, 2 * DFF)),
        ("kv128_s", (1, NS, 1, 2, HG, DH)), ("kv512_s", (1, NS, 1, 2, HG, DH)), ("kv2048_s", (1, NS, 1, 2, HG, DH)),
        ("pool_s", (1, NS, 15, PW)), ("conv_s", (1, NS, 2, CC)), ("ffn_s", (1, NS, 2, 2 * DFF))]


def kernel(**inputs):
    import concourse.bacc as bacc
    from concourse.bass_utils import run_bass_kernel_spmd

    nc = bacc.Bacc("TRN2", target_bir_lowering=False, num_devices=1, dynamic_dma_scratch_size=4096)
    arrays, ins, outs = {}, {}, {}
    for name, x in [(n, inputs[n]) for n in INS] + list(constants().items()):
        x = np.ascontiguousarray(x)
        arrays[f"in_{name}"] = x
        ins[name] = nc.dram_tensor(f"in_{name}", x.shape, mybir.dt.from_np(x.dtype), kind="ExternalInput").ap()
    for name, shape in OUTS:
        outs[name] = nc.dram_tensor(f"out_{name}", shape, F32, kind="ExternalOutput").ap()
    layer(nc, ins, outs)
    r = run_bass_kernel_spmd(nc, [arrays], core_ids=[0])
    return tuple(r.results[0][f"out_{name}"] for name, _ in OUTS)
```
